# Optimizing a Trainium2 kernel written in Bass

```python
import numpy as np
import jax
import jax.numpy as jnp
from jax import lax

D_MODEL = 1024
BATCH = 1
SEQ = 1024
DEPTH = 1

N_META = 16
LEAD = 128
N_PAD = LEAD - N_META
BLOCK = 128

HG_HEADS = 8
HG_DK = 128
HG_DV = 128
HG_WIDTH = HG_HEADS * HG_DK
HG_CHUNK = 16

MLA_HEADS = 16
MLA_NOPE = 128
MLA_ROPE = 64
MLA_V = 128
MLA_Q_RANK = 384
MLA_KV_RANK = 256
MLA_SCALE = (MLA_NOPE + MLA_ROPE) ** -0.5
ROPE_BASE = 10000.0

PEER_HEADS = 8
PEER_NKEYS = 128
PEER_N = PEER_NKEYS * PEER_NKEYS
PEER_HALF = 128
PEER_QDIM = 2 * PEER_HALF
PEER_TOPK = 16

ALPHA = (2 * DEPTH) ** 0.25
BETA = (8 * DEPTH) ** -0.25
EPS = 1e-5

IN_SIZES = (HG_WIDTH, HG_WIDTH, HG_WIDTH, HG_WIDTH, MLA_Q_RANK, MLA_KV_RANK, MLA_ROPE, D_MODEL, D_MODEL)
IN_WIDTH = 4 * HG_WIDTH + MLA_Q_RANK + MLA_KV_RANK + MLA_ROPE + 2 * D_MODEL

kernel_name = 'hybrid_hgrn2_mla_peer_block'

def layer_norm(t, gain, bias):
    tf = t.astype(jnp.float32)
    mu = jnp.mean(tf, axis=-1, keepdims=True)
    var = jnp.mean(jnp.square(tf - mu), axis=-1, keepdims=True)
    return ((tf - mu) * lax.rsqrt(var + EPS) * gain + bias).astype(t.dtype)

def rms_norm(t, gain):
    tf = t.astype(jnp.float32)
    ms = jnp.mean(jnp.square(tf), axis=-1, keepdims=True)
    return (tf * lax.rsqrt(ms + EPS) * gain).astype(t.dtype)

def rope_tables(pos):
    half = MLA_ROPE // 2
    inv_freq = ROPE_BASE ** (-jnp.arange(half, dtype=jnp.float32) / half)
    ang = pos.astype(jnp.float32)[:, None] * inv_freq[None, :]
    return jnp.cos(ang), jnp.sin(ang)

def apply_rope(t, cos, sin):
    half = MLA_ROPE // 2
    tf = t.astype(jnp.float32)
    t1, t2 = tf[..., :half], tf[..., half:]
    return jnp.concatenate([t1 * cos - t2 * sin, t2 * cos + t1 * sin], axis=-1).astype(t.dtype)

def hgrn2_branch(q, f_logit, inp, gate, lower_bound, valid, norm_gain):
    B, P, _ = q.shape
    n_chunks = P // HG_CHUNK
    f32 = jnp.float32
    f = lower_bound + (1.0 - lower_bound) * jax.nn.sigmoid(f_logit.astype(f32))
    vmask = valid[None, :, None]
    log_f = jnp.where(vmask, jnp.log(f), 0.0)
    k = jnp.where(vmask, 1.0 - f, 0.0)

    def chunks(t):
        return t.reshape(B, n_chunks, HG_CHUNK, HG_HEADS, -1).transpose(0, 3, 1, 2, 4)

    qc = chunks(q.astype(f32))
    kc = chunks(k)
    ic = chunks(inp.astype(f32))
    bc = jnp.cumsum(chunks(log_f), axis=3)
    b_last = bc[:, :, :, -1:, :]
    q_dec = qc * jnp.exp(bc)
    k_intra = kc * jnp.exp(-bc)
    k_state = kc * jnp.exp(b_last - bc)

    causal = jnp.tril(jnp.ones((HG_CHUNK, HG_CHUNK), dtype=bool))
    scores = jnp.where(causal, jnp.einsum('bhnck,bhnsk->bhncs', q_dec, k_intra), 0.0)
    o_intra = jnp.einsum('bhncs,bhnsv->bhncv', scores, ic)

    def step(state, xs):
        qd, ks, iv, dec = xs
        o = jnp.einsum('bhck,bhkv->bhcv', qd, state)
        state = dec[..., None] * state + jnp.einsum('bhck,bhcv->bhkv', ks, iv)
        return state, o

    s0 = jnp.zeros((B, HG_HEADS, HG_DK, HG_DV), f32)
    xs = (jnp.moveaxis(q_dec, 2, 0), jnp.moveaxis(k_state, 2, 0), jnp.moveaxis(ic, 2, 0),
          jnp.moveaxis(jnp.exp(b_last[:, :, :, 0, :]), 2, 0))
    _, o_inter = lax.scan(step, s0, xs)
    o = o_intra + jnp.moveaxis(o_inter, 0, 2)
    o = o.transpose(0, 2, 3, 1, 4).reshape(B, P, HG_HEADS, HG_DV)
    o = rms_norm(o, norm_gain.reshape(HG_HEADS, HG_DV)).reshape(B, P, HG_WIDTH)
    return (o * jax.nn.silu(gate.astype(f32))).astype(q.dtype)

def mla_branch(c_q, c_kv, k_rope, q_norm_gain, kv_norm_gain, w_uq, w_ukv, cos, sin):
    B, P, _ = c_q.shape
    q = (rms_norm(c_q, q_norm_gain) @ w_uq).reshape(B, P, MLA_HEADS, MLA_NOPE + MLA_ROPE)
    q_nope = q[..., :MLA_NOPE]
    q_rope = apply_rope(q[..., MLA_NOPE:], cos[:, None, :], sin[:, None, :])
    kv = (rms_norm(c_kv, kv_norm_gain) @ w_ukv).reshape(B, P, MLA_HEADS, MLA_NOPE + MLA_V)
    k_nope, v = kv[..., :MLA_NOPE], kv[..., MLA_NOPE:]
    k_r = apply_rope(k_rope, cos, sin)

    n_blocks = P // BLOCK
    qn_b = q_nope.reshape(B, n_blocks, BLOCK, MLA_HEADS, MLA_NOPE).transpose(1, 0, 3, 2, 4)
    qr_b = q_rope.reshape(B, n_blocks, BLOCK, MLA_HEADS, MLA_ROPE).transpose(1, 0, 3, 2, 4)
    qpos_b = jnp.arange(P).reshape(n_blocks, BLOCK)
    kpos = jnp.arange(P)
    key_real = kpos >= N_PAD

    def attend(args):
        qn, qr, qpos = args
        s = (jnp.einsum('bhqd,bkhd->bhqk', qn, k_nope, preferred_element_type=jnp.float32)
             + jnp.einsum('bhqr,bkr->bhqk', qr, k_r, preferred_element_type=jnp.float32)) * MLA_SCALE
        allowed = (kpos[None, :] <= qpos[:, None]) & (key_real[None, :] | (kpos[None, :] == qpos[:, None]))
        s = jnp.where(allowed, s, -jnp.inf)
        p = jax.nn.softmax(s, axis=-1).astype(v.dtype)
        return jnp.einsum('bhqk,bkhd->bqhd', p, v)

    out = lax.map(attend, (qn_b, qr_b, qpos_b))
    return out.transpose(1, 0, 2, 3, 4).reshape(B, P, MLA_HEADS * MLA_V)

def peer_ffn(h, w_query, sub_keys, u_table, v_table):
    B, P, D = h.shape
    T = B * P
    ht = h.reshape(T, D)
    q = (ht @ w_query).reshape(T, PEER_HEADS, 2, PEER_HALF)
    s = jnp.einsum('thpd,hpnd->thpn', q, sub_keys, preferred_element_type=jnp.float32)
    s_top, i_top = lax.top_k(s, PEER_TOPK)
    cand = s_top[:, :, 0, :, None] + s_top[:, :, 1, None, :]
    cand_idx = i_top[:, :, 0, :, None] * PEER_NKEYS + i_top[:, :, 1, None, :]
    best, sel = lax.top_k(cand.reshape(T, PEER_HEADS, PEER_TOPK * PEER_TOPK), PEER_TOPK)
    experts = jnp.take_along_axis(cand_idx.reshape(T, PEER_HEADS, PEER_TOPK * PEER_TOPK), sel, axis=-1)
    gates = jax.nn.softmax(best, axis=-1)
    n_blk = T // BLOCK
    n_sel = PEER_HEADS * PEER_TOPK

    def apply(args):
        xb, eb, gb = args
        u = jnp.take(u_table, eb, axis=0)
        a = jnp.einsum('tkd,td->tk', u, xb, preferred_element_type=jnp.float32)
        act = (jax.nn.gelu(a) * gb).astype(xb.dtype)
        vv = jnp.take(v_table, eb, axis=0)
        return jnp.einsum('tk,tkd->td', act, vv)

    out = lax.map(apply, (ht.reshape(n_blk, BLOCK, D), experts.reshape(n_blk, BLOCK, n_sel),
                          gates.reshape(n_blk, BLOCK, n_sel)))
    return out.reshape(B, P, D)

def setup_inputs(seed: int = 0) -> dict:
    key = jax.random.key(seed)
    ks = jax.random.split(key, 20)
    nrm = jax.random.normal
    f32 = jnp.float32
    L = DEPTH
    return {
        'x': nrm(ks[0], (BATCH, SEQ, D_MODEL), f32),
        'meta_tokens': nrm(ks[1], (N_META, D_MODEL), f32),
        'hgrn_lb_logits': 0.1 * nrm(ks[2], (DEPTH + 1, HG_WIDTH), f32),
        'w_in': nrm(ks[3], (L, D_MODEL, IN_WIDTH), f32) * D_MODEL ** -0.5,
        'q_norm_gain': 1.0 + 0.01 * nrm(ks[4], (L, MLA_Q_RANK), f32),
        'kv_norm_gain': 1.0 + 0.01 * nrm(ks[5], (L, MLA_KV_RANK), f32),
        'w_uq': nrm(ks[6], (L, MLA_Q_RANK, MLA_HEADS * (MLA_NOPE + MLA_ROPE)), f32) * MLA_Q_RANK ** -0.5,
        'w_ukv': nrm(ks[7], (L, MLA_KV_RANK, MLA_HEADS * (MLA_NOPE + MLA_V)), f32) * MLA_KV_RANK ** -0.5,
        'hgrn_norm_gain': 1.0 + 0.01 * nrm(ks[8], (L, HG_WIDTH), f32),
        'w_proj_hgrn': nrm(ks[9], (L, HG_WIDTH, D_MODEL), f32) * HG_WIDTH ** -0.5,
        'w_proj_mla': nrm(ks[10], (L, MLA_HEADS * MLA_V, D_MODEL), f32) * (MLA_HEADS * MLA_V) ** -0.5,
        'w_out': nrm(ks[11], (L, D_MODEL, D_MODEL), f32) * (BETA * D_MODEL ** -0.5),
        'ln1_gain': 1.0 + 0.01 * nrm(ks[12], (L, D_MODEL), f32),
        'ln1_bias': 0.01 * nrm(ks[13], (L, D_MODEL), f32),
        'peer_query': nrm(ks[14], (L, D_MODEL, PEER_HEADS * PEER_QDIM), f32) * D_MODEL ** -0.5,
        'peer_sub_keys': nrm(ks[15], (L, PEER_HEADS, 2, PEER_NKEYS, PEER_HALF), f32) * PEER_HALF ** -0.5,
        'peer_u': nrm(ks[16], (L, PEER_N, D_MODEL), f32) * D_MODEL ** -0.5,
        'peer_v': nrm(ks[17], (L, PEER_N, D_MODEL), f32) * BETA,
        'ln2_gain': 1.0 + 0.01 * nrm(ks[18], (L, D_MODEL), f32),
        'ln2_bias': 0.01 * nrm(ks[19], (L, D_MODEL), f32),
    }

def reference(x, meta_tokens, hgrn_lb_logits, w_in, q_norm_gain, kv_norm_gain, w_uq, w_ukv,
              hgrn_norm_gain, w_proj_hgrn, w_proj_mla, w_out, ln1_gain, ln1_bias,
              peer_query, peer_sub_keys, peer_u, peer_v, ln2_gain, ln2_bias):
    B, S, D = x.shape
    P = LEAD + S
    pad = jnp.zeros((B, N_PAD, D), x.dtype)
    meta = jnp.broadcast_to(meta_tokens.astype(x.dtype)[None], (B, N_META, D))
    h = jnp.concatenate([pad, meta, x], axis=1)
    rows = jnp.arange(P)
    valid = rows >= N_PAD
    cos, sin = rope_tables(rows - N_PAD)
    lower_bounds = jnp.cumsum(jax.nn.softmax(hgrn_lb_logits.astype(jnp.float32), axis=0), axis=0)
    offsets = [int(o) for o in np.cumsum(IN_SIZES)[:-1]]

    for l in range(DEPTH):
        proj = h @ w_in[l]
        hq, hf, hi, hg, cq, ckv, kr, ga, gb = jnp.split(proj, offsets, axis=-1)
        ya = hgrn2_branch(hq, hf, hi, hg, lower_bounds[l], valid, hgrn_norm_gain[l]) @ w_proj_hgrn[l]
        yb = mla_branch(cq, ckv, kr, q_norm_gain[l], kv_norm_gain[l], w_uq[l], w_ukv[l], cos, sin) @ w_proj_mla[l]
        mixed = (jax.nn.sigmoid(ga) * ya + jax.nn.sigmoid(gb) * yb) @ w_out[l]
        h = layer_norm(ALPHA * h + mixed, ln1_gain[l], ln1_bias[l])
        ffn = peer_ffn(h, peer_query[l], peer_sub_keys[l], peer_u[l], peer_v[l])
        h = layer_norm(ALPHA * h + ffn, ln2_gain[l], ln2_bias[l])

    return h[:, LEAD:]


_drawn_inputs = setup_inputs


def setup_inputs(seed=0):
    import zlib

    import numpy as np

    out = dict(_drawn_inputs(seed))
    spreads = {}
    factors = {'q_norm_gain': 8.0,
     'kv_norm_gain': 8.0,
     'hgrn_norm_gain': 20.788,
     'ln2_gain': 33.629,
     'ln2_bias': 33.009}
    for name, (base, spread) in spreads.items():
        noise = np.random.default_rng([zlib.crc32(name.encode()), seed]).standard_normal(out[name].shape)
        drawn = base * np.exp(spread * noise) if base else spread * noise
        out[name] = jnp.asarray(drawn.astype(out[name].dtype))
    for name, factor in factors.items():
        out[name] = (out[name] * factor).astype(out[name].dtype)
    return out
```

```python
from contextlib import ExitStack

import numpy as np

import concourse.bass as bass
from concourse import mybir

F32 = mybir.dt.float32
U32 = mybir.dt.uint32
U8 = mybir.dt.uint8
ALU = mybir.AluOpType
ACT = mybir.ActivationFunctionType
AX = mybir.AxisListType.X

P = 128
D = 1024
KD = D // P
SEQ = 1024
META = 16
HALF = 512
NH = SEQ // HALF
NB = HALF // P
NBLK = SEQ // P
KEYS = META + SEQ
CHUNK = 16
PAIR = 2 * CHUNK
NPAIR = HALF // PAIR
HG = 8
MH = 16
QT, KVT = 3, 2
ROPE = 64
SCALE = float((128 + ROPE) ** -0.5)
PH = 8
TOP = 16
NSEL = PH * TOP
ALPHA = float(2 ** 0.25)
EPS = 1e-5
NEG = -1e30
GRP = 4
GSLOT = 2 * GRP
NGRP = NSEL // GRP

C_ID, C_ONE, C_MA, C_NS, C_END = 0, 128, 256, 768, 1280
C_CAUS, C_IOTA, C_COS, C_SIN = 1792, 1920, 1952, 1952 + KEYS
C_W = C_SIN + KEYS
ARENA_W = 41500


def constants():
    c = np.zeros((P, C_W), np.float32)
    t = np.arange(HALF)
    s = np.arange(P)
    c[:, C_ID:C_ID + P] = np.eye(P)
    c[:, C_ONE:C_ONE + P] = 1.0
    tl = t % P
    c[:, C_MA:C_MA + HALF] = (s[:, None] <= tl) & (s[:, None] // CHUNK == tl // CHUNK)
    c[:, C_NS:C_NS + HALF] = t % CHUNK != 0
    c[:, C_END:C_END + HALF] = t % CHUNK == CHUNK - 1
    c[:, C_CAUS:C_CAUS + P] = np.where(s[None, :] <= s[:, None], 0.0, NEG)
    c[:, C_IOTA:C_IOTA + 32] = np.arange(32) % 16
    inv = (np.float32(10000.0) ** (-np.arange(32, dtype=np.float32) / np.float32(32))).astype(np.float32)
    ang = np.arange(KEYS, dtype=np.float32)[None, :] * inv[:, None]
    c[:, C_COS:C_COS + KEYS] = np.tile(np.cos(ang), (4, 1))
    c[:, C_SIN:C_SIN + KEYS] = np.concatenate([-np.sin(ang), np.sin(ang)] * 2)
    cross = (s[:, None] // PAIR == tl // PAIR) & (s[:, None] // CHUNK % 2 == 0) & (tl // CHUNK % 2 == 1)
    return c, cross.astype(np.float32)


def build_program(nc, a):
    with ExitStack() as ctx:
        def sb(name, shape, dt=F32, where=ctx):
            return where.enter_context(nc.sbuf_tensor(name, shape, dt))

        names = """c_in lb_ready fcol xt_in wF_in wG_in wQ_in wI_in m_F m_I F G Q I sig sigG gcol ks32a qd32a t2nd
        f fm fs eb est ebi qd16 k ki ks16 qd32 ks32 D T ksT M1 M2 sA sc st St S0 Sb inter isb sq ms std
        rs y1 y t2 wc_in cj csq mq stdq rsq cn mkv stdkv rskv ckn krA krB kr wuq_in wukv_in j6 j7 e6 e7
        qrb Sm cau mx ngm exp rcp pn pt3 pt4 pe3 pe4 pv3 pv4 OE wa_in wb_in wga_in wgb_in pga pgb
        pya pyb sga sgb m1 m2 mix wo_in xk_in ln_in wo r n2 n3 n4 n8 hT hTe h_out wpq_in wsk_in pq pqe
        ps pse dv dvb gmx gex g_h g_ln gz g_dot gel gac gdg gmm gidx l1 l4 l5 l6 l9 out_done start apart m_pe
        m_act m_dve m_pool dvc nd ld""".split()
        sem = {n: ctx.enter_context(nc.semaphore("s_" + n)) for n in names}
        got = [ctx.enter_context(nc.semaphore(f"s_got{i}")) for i in range(GSLOT)]
        stage_done = ctx.enter_context(nc.semaphore("s_stage_done"))

        def end_stage(eng, n):
            eng.drain().then_inc(stage_done, 1)
            eng.wait_ge(stage_done, 5 * n + 5)

        def apart(eng):
            eng.sem_inc(sem["apart"], 1)

        PS = ctx.enter_context(nc.psum_tensor("PS", [P, 8 * 512], F32))

        def bank(i):
            return PS[:, 512 * i:512 * i + 512]

        C = sb("C", [P, C_W])
        MB = sb("MB", [P, HALF], U8)
        PV = sb("PV", [P, 29])
        small = sb("small", [P, 64])
        fcol = small[:, 56:59]
        LB, OML = small[:, 0:8], small[:, 8:16]
        EPSC = small[:, 16:17]
        S_all = sb("S_all", [P, HG, P])
        ckvn = sb("ckvn", [P, KVT, KEYS])
        krT = sb("krT", [P, KEYS])
        EIDX = sb("EIDX", [P, NBLK, NSEL], U32)
        GATE = sb("GATE", [P, NBLK, NSEL])
        XM = sb("XM", [P, KD, META])
        ident, ones = C[:, C_ID:C_ID + P], C[:, C_ONE:C_ONE + P]
        H1 = nc.dram_tensor("h1_scratch", [NBLK, P, D], F32, kind="Internal").ap()


        ARENA = sb("ARENA", [P, ARENA_W])
        top = [0]

        def at(off):
            top[0] = off

        def new(n, **dims):
            v = ARENA[:, top[0]:top[0] + n]
            top[0] += n
            assert top[0] <= ARENA_W
            return v

        def new3(x, y):
            return new(x * y).rearrange("p (x y) -> p x y", x=x)

        def new4(x, y, z):
            return new(x * y * z).rearrange("p (x y z) -> p x y z", x=x, y=y)

        at(0)
        XT = new3(KD, HALF)
        YH = new3(HG, HALF)
        YM = new3(MH, HALF)
        scratch = top[0]
        wF, wG, wQ, wI = (new3(KD, P) for _ in range(4))
        (sg, sg2, f, fs, k, eb, est, ebi, qd16, ki, ks16, qd32, ks32, isb, ksT, sc, t2, y1, sqh, std,
         rs) = (new(HALF) for _ in range(21))
        fm = new(HALF + 1)
        Dp = new(NPAIR)
        Spp = [new(P) for _ in range(2)]
        msg, mf, mk, mest, mks = (new(P) for _ in range(5))
        mfm = new(P + 1)
        miT, mksT = new(HG * P), new(HG * P)
        at(scratch)
        cqn = new3(QT, HALF)
        wuq = new4(QT, 4, P)
        wukv = new4(KVT, 4, P)
        attend = top[0]
        wc = new4(KD, 7, P)
        csq = new3(QT + KVT, HALF)
        cstd, crs, kta, ktb = (new(HALF) for _ in range(4))
        mcsq = new3(KVT, META)
        mstd, mrs, mka, mkb = (new(META) for _ in range(4))
        at(attend)
        qn = [new(HALF) for _ in range(2)]
        qr, qra, qrb = (new(HALF) for _ in range(3))
        kn = [new(KEYS) for _ in range(2)]
        V = new3(NBLK + 1, 2 * P)
        PR = [new(KEYS) for _ in range(2)]
        PTs = [new(512) for _ in range(2)]
        smx = new(64)
        at(scratch)
        MIX = new3(KD, HALF)
        wa, wga, wgb = (new3(KD, P) for _ in range(3))
        wb = new3(MH, P)
        sga, sgb, mm1, mm2 = (new(HALF) for _ in range(4))
        at(0)
        WO = new3(KD, D)
        XK = new3(NB, D)
        HT = new3(KD, HALF)
        assert top[0] == scratch
        at(scratch + KD * HALF)
        LN1 = new3(2, D)
        R1 = [new(D) for _ in range(2)]
        R2 = [new(D) for _ in range(2)]
        junk = new(D)
        st1 = new(64)
        at(0)
        wpq = new4(KD, 2, P)
        wsk = new3(2, P)
        qT = [new(HALF) for _ in range(2)]
        SS, SS2 = new4(2, NB, P), new4(2, NB, P)
        tv = new4(2, NB, TOP)
        ti = new(2 * NB * TOP).bitcast(U32).rearrange("p (x y z) -> p x y z", x=2, y=NB)
        tif = new4(NB, 2, TOP)
        CA, CA2 = new3(NB, TOP * TOP), new3(NB, TOP * TOP)
        at(scratch)
        bv = new3(NB, TOP)
        bs = new(NB * TOP).bitcast(U32).rearrange("p (x y) -> p x y", x=NB)
        bs2 = new(2 * NB * TOP).bitcast(U32).rearrange("p (x y z) -> p x y z", x=NB, y=TOP)
        bsf = new4(NB, TOP, 2)
        OH, OH2 = new(NB * TOP * 2 * TOP), new(NB * TOP * 2 * TOP)
        osum = new4(NB, TOP, 2)
        eif, ge, gd = (new3(NB, TOP) for _ in range(3))
        gs, gr = new(NB), new(NB)
        at(0)
        ROW = [new(2 * D) for _ in range(GSLOT)]
        HB = new(D)
        GJ = [new(D) for _ in range(2)]
        DG = [new(P) for _ in range(GSLOT)]
        LN2 = new3(2, D)
        O1, O2 = new(D), new(D)
        IDX = [new(GSLOT).bitcast(U32) for _ in range(2)]
        av, ag, aw = (new(GSLOT) for _ in range(3))
        zero = new(P)
        st2 = new(8)

        block = ctx.enter_context(nc.Block())

        def jobs_of(hf):
            nfull = 4 * (hf + 1)
            out = [("qrA", None), ("qn", 0), ("qrB", None), ("qn", 1)]
            out += [("kn", (e, c, min(512, META + HALF * (hf + 1) - c)))
                    for c in range(0, META + HALF * (hf + 1), 512) for e in range(2)]
            out += [("v", (j, 2)) for j in range(0, nfull, 2)] + [("v", (nfull, 1))]
            return [(what, arg, 7 - i % 2, i // 2) for i, (what, arg) in enumerate(out)]

        def bank_jobs(hf, b):
            return sum(j[2] == b for j in jobs_of(hf))

        def before(count, hf, u):
            return count(hf) * u + (8 * count(0) if hf else 0)

        def groups_of(hf):
            out, n = [], 0
            for i in range(8):
                tiles = list(range(4 * hf + i % 4 + 2))
                here = []
                for c in range(0, len(tiles), 4):
                    here.append((tiles[c:c + 4], 3 + n % 2, n // 2))
                    n += 1
                out.append(here)
            return out

        def bank_groups(hf, b):
            return sum(g[1] == b for here in groups_of(hf) for g in here)

        def keys_of(hf, b):
            return META + HALF * hf + P * (b + 1)

        def rows_of(hf, b, tile):
            return P if tile < 4 * hf + b + 1 else META

        def cols(b):
            return slice(P * b, P * b + P)

        @block.sync
        def _(sp):
            sp.dma_start(C[:], a["consts"]).then_inc(sem["c_in"], 16)
            sp.dma_start(y1, a["cross"]).then_inc(sem["c_in"], 16)
            sp.dma_start(PV[:], a["pvec"]).then_inc(sem["c_in"], 16)
            sp.dma_start(XM[:], a["xm"]).then_inc(sem["c_in"], 16)
            with sp.Fori(0, HG) as h:
                sp.wait_ge(sem["m_F"], h)
                sp.dma_start(wF, a["whg"][h, 0]).then_inc(sem["wF_in"], 16)
                sp.wait_ge(sem["m_I"], h)
                sp.dma_start(wI, a["whg"][h, 3]).then_inc(sem["wI_in"], 16)
            sp.wait_ge(sem["m_F"], HG)
            sp.wait_ge(sem["m_I"], HG)
            for hf in range(NH):
                sp.dma_start(XT, a["xt"][hf]).then_inc(sem["xt_in"], 16)
                with sp.Fori(0, HG) as h:
                    for n, (name, w) in enumerate((("F", wF), ("G", wG), ("Q", wQ), ("I", wI))):
                        sp.wait_ge(sem[name], h + HG * hf)
                        sp.dma_start(w, a["whg"][h, (0, 1, 2, 3)[n]]).then_inc(sem[f"w{name}_in"], 16)
                end_stage(sp, 6 * hf)
                sp.dma_start(wc, a["wc"]).then_inc(sem["wc_in"], 16)
                end_stage(sp, 6 * hf + 1)
                n7, n6 = bank_jobs(hf, 7), bank_jobs(hf, 6)
                with sp.Fori(0, 8) as u:
                    sp.wait_ge(sem["j7"], before(lambda x: bank_jobs(x, 7), hf, u))
                    apart(sp)
                    sp.wait_ge(sem["j6"], before(lambda x: bank_jobs(x, 6), hf, u))
                    sp.dma_start(wuq, a["wuq"][u]).then_inc(sem["wuq_in"], 16)
                    sp.dma_start(wukv, a["wukv"][u]).then_inc(sem["wukv_in"], 16)
                end_stage(sp, 6 * hf + 2)
                with sp.Fori(0, KD) as n:
                    for name, w, k0, k1 in (("ga", wga, 24, 32), ("gb", wgb, 32, 40), ("ya", wa, 0, 8),
                                            ("yb", wb, 8, 24)):
                        sp.wait_ge(sem["p" + name], n + KD * hf)
                        apart(sp)
                        sp.dma_start(w, a["wmix"][n, :, k0:k1, :]).then_inc(
                            sem[{"ga": "wga_in", "gb": "wgb_in", "ya": "wa_in", "yb": "wb_in"}[name]], 16)
                end_stage(sp, 6 * hf + 3)
                sp.dma_start(WO, a["wout"]).then_inc(sem["wo_in"], 16)
                sp.dma_start(XK, a["xk"][hf]).then_inc(sem["xk_in"], 16)
                sp.dma_start(LN1, a["ln1"]).then_inc(sem["ln_in"], 16)
                for b in range(NB):
                    sp.wait_ge(sem["n8"], NB * hf + b + 1)
                    sp.dma_start(H1[NB * hf + b], R2[b % 2]).then_inc(sem["h_out"], 16)
                    sp.wait_ge(sem["h_out"], 16 * (NB * hf + b + 1))
                end_stage(sp, 6 * hf + 4)
                with sp.Fori(0, PH) as h:
                    sp.wait_ge(sem["pq"], 2 * h + 2 * PH * hf)
                    sp.dma_start(wpq, a["wpq"][h]).then_inc(sem["wpq_in"], 16)
                    sp.wait_ge(sem["ps"], 2 * h + 2 * PH * hf)
                    sp.dma_start(wsk, a["wsk"][h]).then_inc(sem["wsk_in"], 16)
                end_stage(sp, 6 * hf + 5)
            sp.dma_start(LN2, a["ln2"]).then_inc(sem["g_ln"], 16)
            sp.wait_ge(sem["h_out"], 16 * NBLK)
            with sp.Fori(0, NBLK) as t:
                sp.wait_ge(sem["l1"], t)
                sp.dma_start(HB, H1[t]).then_inc(sem["g_h"], 16)
                sp.wait_ge(sem["l9"], t + 1)
                sp.dma_start(a["out"][t], O2).then_inc(sem["out_done"], 16)
            sp.wait_ge(sem["out_done"], 16 * NBLK)

        @block.tensor
        def _(pe):
            def mm(out, lhsT, rhs, start, stop):
                return pe.matmul(out, lhsT, rhs, start=start, stop=stop, skip_group_check=True)

            def product(out, w, x, n=KD):
                for kt in range(n):
                    last = mm(out, w(kt), x(kt), kt == 0, kt == n - 1)
                return last

            pe.wait_ge(sem["c_in"], 64)
            with pe.Fori(0, HG) as h:
                pe.wait_ge(sem["wF_in"], 16 * h + 16)
                product(PS[:, bass.ds(h * META, META)], lambda kt: wF[:, kt, :], lambda kt: XM[:, kt, :]
                        ).then_inc(sem["m_F"], 1)
                pe.wait_ge(sem["wI_in"], 16 * h + 16)
                product(PS[0:META, bass.ds(h * P + 512, P)], lambda kt: XM[:, kt, :], lambda kt: wI[:, kt, :]
                        ).then_inc(sem["m_I"], 1)
            pe.wait_ge(sem["m_pool"], 2)
            for h in range(HG):
                last = pe.transpose(PS[0:META, 1536 + P * h:1536 + P * h + P], mks[:, META * h:META * h + META],
                                    ident)
            last.then_inc(sem["m_pe"], 1)
            pe.wait_ge(sem["m_act"], 3)
            pe.wait_ge(sem["m_act"], 2)
            for h in range(HG):
                last = mm(PS[:, 2560 + P * h:2560 + P * h + P], mksT[0:META, cols(h)], miT[0:META, cols(h)],
                          True, True)
            last.then_inc(sem["m_pe"], 1)
            pe.wait_ge(sem["m_dve"], 5)

            for hf in range(NH):
                def project(g, name):
                    w = {"F": wF, "G": wG, "Q": wQ, "I": wI}[name]
                    b = {"F": 0, "G": 1, "Q": 2, "I": 3}[name]
                    used = {"F": "sig", "G": "t2", "Q": "qd16", "I": "isb"}[name]
                    extra = 16 * HG if name in "FI" else 0
                    pe.wait_ge(sem[f"w{name}_in"], g * 16 + (16 + extra))
                    pe.wait_ge(sem[used], g)
                    for i in range(NB if name == "I" else 1):
                        for kt in range(KD):
                            if name == "I":
                                last = mm(bank(b)[:, cols(i)], XT[:, kt, cols(i)], w[:, kt, :], kt == 0, kt == KD - 1)
                            else:
                                last = mm(bank(b), w[:, kt, :], XT[:, kt, :], kt == 0, kt == KD - 1)
                            if kt == KD - 1 and i == (NB if name == "I" else 1) - 1:
                                last.then_inc(sem[name], 1)
                            yield

                def all_of(steps):
                    for _ in steps:
                        pass

                def head(g, following):
                    pe.wait_ge(sem["ks32"], g + 1)
                    pe.wait_ge(sem["st"], g * NPAIR)
                    for b in range(NB):
                        last = pe.transpose(bank(5)[:, cols(b)], ks32[:, cols(b)], ident)
                    last.then_inc(sem["T"], 1)
                    pe.wait_ge(sem["ki"], g + 1)
                    pe.wait_ge(sem["qd16"], g + 1)
                    pe.wait_ge(sem["std"], g)
                    for b in range(NB):
                        last = mm(bank(4)[:, cols(b)], ki[:, cols(b)], qd16[:, cols(b)], True, True)
                    last.then_inc(sem["M1"], 1)
                    pe.wait_ge(sem["ksT"], g + 1)
                    for b in range(NB):
                        last = mm(bank(5)[:, cols(b)], ks16[:, cols(b)], qd16[:, cols(b)], True, True)
                    last.then_inc(sem["M2"], 1)
                    pe.wait_ge(sem["sc"], g + 1)
                    pe.wait_ge(sem["isb"], g + 1)
                    pe.wait_ge(sem["y1"], g)
                    for b in range(NB):
                        mm(bank(6)[:, cols(b)], isb[:, cols(b)], sc[:, cols(b)], b == 0, True)
                    more = iter(())
                    if following:
                        def both():
                            yield from project(g + 1, "F")
                            yield from project(g + 1, "G")
                        more = both()
                    pe.wait_ge(sem["qd32"], g + 1)
                    for p in range(NPAIR):
                        if p >= 2:
                            pe.wait_ge(sem["st"], g * NPAIR + (p - 1))
                        r = 32 * (p % 4)
                        c = P * (p // 4)
                        u = bank(7 if p % 2 == 0 else 5)[:, 0:P]
                        mm(u, ksT[r:r + 32, c:c + P], isb[r:r + 32, c:c + P], True, True).then_inc(sem["St"], 1)
                        next(more, None)
                        if p == 0:
                            pe.wait_ge(sem["S0"], g + 1)
                        else:
                            pe.wait_ge(sem["st"], g * NPAIR + p)
                        mm(bank(6)[:, 32 * p:32 * p + 32], Spp[p % 2], qd32[:, 32 * p:32 * p + 32], False,
                           True).then_inc(sem["inter"], 1)
                    all_of(more)
                    if following:
                        all_of(project(g + 1, "Q"))
                    pe.wait_ge(sem["sq"], g + 1)
                    mm(bank(4), ones, sqh, True, True).then_inc(sem["ms"], 1)
                    if following:
                        all_of(project(g + 1, "I"))

                pe.wait_ge(sem["xt_in"], 16 * hf + 16)
                for name in "FGQI":
                    all_of(project(HG * hf, name))
                with pe.Fori(0, HG - 1) as h:
                    head(h + HG * hf, True)
                head(HG * hf + HG - 1, False)
                end_stage(pe, 6 * hf)

                pe.wait_ge(sem["wc_in"], 16 * hf + 16)
                for j in range(7):
                    product(bank(j), lambda kt: wc[:, kt, j, :], lambda kt: XT[:, kt, :]).then_inc(sem["cj"], 1)
                pe.wait_ge(sem["csq"], 5 * hf + 3)
                product(bank(7), lambda i: ones, lambda i: csq[:, i, :], QT).then_inc(sem["mq"], 1)
                pe.wait_ge(sem["csq"], 5 * hf + 5)
                pe.wait_ge(sem["stdq"], hf + 1)
                product(bank(7), lambda i: ones, lambda i: csq[:, QT + i, :], KVT).then_inc(sem["mkv"], 1)
                if hf == 0:
                    pe.wait_ge(sem["stdkv"], 1)
                    for j in range(4):
                        last = product(bank(7)[:, META * j:META * j + META], lambda kt: wc[:, kt, QT + j, :],
                                       lambda kt: XM[:, kt, :])
                    last.then_inc(sem["m_pe"], 1)
                    pe.wait_ge(sem["m_act"], 4)
                    pe.wait_ge(sem["cn"], QT)
                    product(bank(0)[:, 0:META], lambda i: ones, lambda i: mcsq[:, i, :], KVT
                            ).then_inc(sem["m_pe"], 1)
                end_stage(pe, 6 * hf + 1)

                groups = groups_of(hf)

                def pair(u):
                    G = u + 8 * hf
                    pe.wait_ge(sem["wuq_in"], G * 16 + 16)
                    pe.wait_ge(sem["wukv_in"], G * 16 + 16)
                    for what, arg, b, n in jobs_of(hf):
                        pe.wait_ge(sem[f"e{b}"], before(lambda x: bank_jobs(x, b), hf, u) + n)
                        if what in ("qrA", "qrB", "qn"):
                            j = {"qrA": 2, "qrB": 3}.get(what, arg)
                            last = product(bank(b), lambda i: wuq[:, i, j, :], lambda i: cqn[:, i, :], QT)
                        elif what == "kn":
                            e, c, n_ = arg
                            last = product(bank(b)[:, 0:n_], lambda i: wukv[:, i, e, :],
                                           lambda i: ckvn[:, i, c:c + n_], KVT)
                        else:
                            j, many = arg
                            for t in range(many):
                                r = P if many == 2 else META
                                c = P * (j + t)
                                for i in range(KVT):
                                    last = mm(bank(b)[0:r, 256 * t:256 * t + 256], ckvn[:, i, c:c + r],
                                              wukv[:, i, 2:4, :], i == 0, i == KVT - 1)
                        last.then_inc(sem[f"j{b}"], 1)
                    for b in (6, 7):
                        pe.wait_ge(sem[f"e{b}"], before(lambda x: bank_jobs(x, b), hf, u) + bank_jobs(hf, b))

                    def scores(i):
                        e, b = divmod(i, 4)
                        nk = keys_of(hf, b)
                        pe.wait_ge(sem["exp"], G * 8 + i)
                        for c in range(0, nk, 512):
                            n = min(512, nk - c)
                            mm(PS[:, c:c + n], qn[e][:, cols(b)], kn[e][:, c:c + n], True, False)
                            last = mm(PS[:, c:c + n], qr[ROPE * e:ROPE * e + ROPE, cols(b)],
                                      krT[ROPE * e:ROPE * e + ROPE, c:c + n], False, True)
                        last.then_inc(sem["Sm"], 1)

                    def turn(i, group):
                        tiles, bk, n = group
                        pe.wait_ge(sem[f"pe{bk}"], before(lambda x: bank_groups(x, bk), hf, u) + n)
                        for s, t in enumerate(tiles):
                            r = rows_of(hf, i % 4, t)
                            last = pe.transpose(bank(bk)[0:r, cols(s)], PR[i % 2][:, P * t:P * t + r], ident)
                        last.then_inc(sem[f"pt{bk}"], 1)

                    def values(i, group):
                        e, b = divmod(i, 4)
                        tiles, bk, n = group
                        pe.wait_ge(sem[f"pe{bk}"], before(lambda x: bank_groups(x, bk), hf, u) + (n + 1))
                        for s, t in enumerate(tiles):
                            r = rows_of(hf, b, t)
                            last = mm(bank(5)[:, cols(b)], V[0:r, t, cols(e)], PTs[bk - 3][0:r, cols(s)],
                                      t == 0, r < P)
                        last.then_inc(sem[f"pv{bk}"], 1)

                    def output(i):
                        pe.wait_ge(sem["pn"], G * 8 + (i + 1))
                        if i % 4 == 0:
                            pe.wait_ge(sem["OE"], G * 2 + i // 4)
                        for n, group in enumerate(groups[i]):
                            turn(i, group)
                            if n:
                                values(i, groups[i][n - 1])
                        values(i, groups[i][-1])

                    scores(0)
                    for i in range(1, 8):
                        scores(i)
                        output(i - 1)
                    output(7)

                with pe.Fori(0, 8) as u:
                    pair(u)
                end_stage(pe, 6 * hf + 2)

                with pe.Fori(0, KD) as n:
                    N = n + KD * hf
                    for name, wname, w, x, kn_, b, used in (
                            ("pga", "wga_in", wga, XT, KD, 2, "sga"), ("pgb", "wgb_in", wgb, XT, KD, 3, "sgb"),
                            ("pya", "wa_in", wa, YH, HG, 0, "m1"), ("pyb", "wb_in", wb, YM, MH, 1, "m2")):
                        pe.wait_ge(sem[wname], N * 16 + 16)
                        pe.wait_ge(sem[used], N)
                        product(bank(b), lambda kt: w[:, kt, :], lambda kt: x[:, kt, :], kn_).then_inc(sem[name], 1)
                end_stage(pe, 6 * hf + 3)

                pe.wait_ge(sem["wo_in"], 16 * hf + 16)
                for b in range(NB):
                    for j in range(2):
                        product(bank(2 * b + j), lambda kt: MIX[:, kt, cols(b)],
                                lambda kt: WO[:, kt, 512 * j:512 * j + 512]).then_inc(sem["wo"], 1)
                for b in range(NB):
                    pe.wait_ge(sem["n8"], NB * hf + b + 1)
                    for kt in range(KD):
                        last = pe.transpose(PS[:, 1024 * b + P * kt:1024 * b + P * kt + P],
                                            R2[b % 2][:, P * kt:P * kt + P], ident)
                    last.then_inc(sem["hT"], 1)
                end_stage(pe, 6 * hf + 4)

                with pe.Fori(0, PH) as h:
                    H = h + PH * hf
                    pe.wait_ge(sem["wpq_in"], H * 16 + 16)
                    for j in range(2):
                        pe.wait_ge(sem["pqe"], H * 2 + j)
                        product(bank(j), lambda kt: wpq[:, kt, j, :], lambda kt: HT[:, kt, :]
                                ).then_inc(sem["pq"], 1)
                    pe.wait_ge(sem["wsk_in"], H * 16 + 16)
                    for j in range(2):
                        pe.wait_ge(sem["pqe"], H * 2 + (j + 1))
                        pe.wait_ge(sem["pse"], H * 2 + j)
                        for b in range(NB):
                            last = mm(bank(2 + j)[:, cols(b)], qT[j][:, cols(b)], wsk[:, j, :], True, True)
                        last.then_inc(sem["ps"], 1)
                end_stage(pe, 6 * hf + 5)

            pe.wait_ge(sem["gz"], 1)
            with pe.Fori(0, NBLK) as t:
                pe.wait_ge(sem["l1"], t)
                for j in range(2):
                    mm(bank(j), zero, C[:, 0:512], True, False)
                with pe.Fori(0, NGRP // 2) as q:
                    for s in range(GSLOT):
                        pe.wait_ge(sem["gdg"], (t * (NGRP // 2) + q) * GSLOT + (s + 1))
                        for j in range(2):
                            last = mm(bank(j), DG[s], ROW[s][:, D + 512 * j:D + 512 * j + 512], False, s == GSLOT - 1)
                        last.then_inc(sem["gmm"], 1)

        @block.scalar
        def _(act):
            def run(out, in_, func, done, **kw):
                return act.activation(out, in_, func, **kw).then_inc(sem[done], 1)

            act.wait_ge(sem["lb_ready"], 3)
            run(small[:, 24:40], small[:, 24:40], ACT.Exp, "lb_ready")
            act.wait_ge(sem["m_F"], HG)
            run(msg, PS[:, 0:P], ACT.Sigmoid, "m_act")
            act.wait_ge(sem["m_I"], HG)
            run(miT[0:META, :], PS[0:META, 512:512 + HG * P], ACT.Copy, "m_act")
            act.wait_ge(sem["m_pe"], 1)
            run(mksT[0:META, :], PS[0:META, 1536:1536 + HG * P], ACT.Copy, "m_act")

            for hf in range(NH):
                def gates(g):
                    act.wait_ge(sem["F"], g + 1)
                    act.wait_ge(sem["f"], g * 2)
                    run(sg, bank(0), ACT.Sigmoid, "sig")
                    act.wait_ge(sem["G"], g + 1)
                    act.wait_ge(sem["t2"], g)
                    run(sg2, bank(1), ACT.Sigmoid, "sigG")

                def inputs(g):
                    act.wait_ge(sem["I"], g + 1)
                    act.wait_ge(sem["inter"], g * NPAIR)
                    run(isb, bank(3), ACT.Copy, "isb")

                def head(g, following):
                    act.wait_ge(sem["T"], g + 1)
                    act.wait_ge(sem["inter"], g * NPAIR)
                    run(ksT, bank(5), ACT.Copy, "ksT")
                    if following:
                        gates(g + 1)
                    act.wait_ge(sem["inter"], g * NPAIR + NPAIR)
                    act.wait_ge(sem["ms"], g)
                    run(sqh, bank(6), ACT.Square, "sq")
                    act.wait_ge(sem["ms"], g + 1)
                    act.wait_ge(sem["rs"], g)
                    run(std, bank(4), ACT.Sqrt, "std", scale=1.0 / P, bias=EPSC)
                    if following:
                        inputs(g + 1)

                gates(HG * hf)
                inputs(HG * hf)
                with act.Fori(0, HG - 1) as h:
                    head(h + HG * hf, True)
                head(HG * hf + HG - 1, False)
                end_stage(act, 6 * hf)

                for i in range(QT + KVT):
                    act.wait_ge(sem["cj"], 7 * hf + i + 1)
                    run(csq[:, i, :], bank(i), ACT.Square, "csq")
                act.wait_ge(sem["mq"], hf + 1)
                run(cstd, bank(7), ACT.Sqrt, "stdq", scale=1.0 / (QT * P), bias=EPSC)
                act.wait_ge(sem["mkv"], hf + 1)
                act.wait_ge(sem["rsq"], hf + 1)
                run(cstd, bank(7), ACT.Sqrt, "stdkv", scale=1.0 / (KVT * P), bias=EPSC)
                if hf == 0:
                    act.wait_ge(sem["m_pe"], 3)
                    run(mcsq.rearrange("p a b -> p (a b)"), bank(7)[:, 0:KVT * META], ACT.Square, "m_act")
                    act.wait_ge(sem["m_pe"], 4)
                    run(mstd, bank(0)[:, 0:META], ACT.Sqrt, "m_act", scale=1.0 / (KVT * P), bias=EPSC)
                end_stage(act, 6 * hf + 1)

                groups = groups_of(hf)
                with act.Fori(0, 8) as u:
                    G = u + 8 * hf
                    for what, arg, b, n in jobs_of(hf):
                        if b == 7:
                            continue
                        act.wait_ge(sem["j6"], before(lambda x: bank_jobs(x, 6), hf, u) + (n + 1))
                        if what == "qn":
                            run(qn[arg], bank(6), ACT.Copy, "e6")
                        elif what == "kn":
                            e, c, n_ = arg
                            run(kn[e][:, c:c + n_], bank(6)[:, 0:n_], ACT.Copy, "e6")
                        else:
                            j, many = arg
                            r = P if many == 2 else META
                            run(V[0:r, j:j + many, :], bank(6)[0:r, 0:256 * many], ACT.Copy, "e6")

                    def copy_turned(i):
                        for tiles, bk, n in groups[i]:
                            if bk == 3:
                                act.wait_ge(sem["pt3"], before(lambda x: bank_groups(x, 3), hf, u) + (n + 1))
                                act.wait_ge(sem["pv3"], before(lambda x: bank_groups(x, 3), hf, u) + n)
                                full = [t for t in tiles if rows_of(hf, i % 4, t) == P]
                                if full:
                                    one = act.activation(PTs[0][:, 0:P * len(full)], bank(3)[:, 0:P * len(full)],
                                                         ACT.Copy)
                                if len(full) < len(tiles):
                                    s = len(full)
                                    one = act.activation(PTs[0][0:META, cols(s)], bank(3)[0:META, cols(s)], ACT.Copy)
                                one.then_inc(sem["pe3"], 1)
                        if i % 4 == 3:
                            act.wait_ge(sem[f"pv{bk}"], before(lambda x: bank_groups(x, bk), hf, u) + (n + 1))
                            run(YM[:, bass.ds(u * 2 + i // 4, 1), :], bank(5), ACT.Copy, "OE")

                    for i in range(8):
                        nk = keys_of(hf, i % 4)
                        act.wait_ge(sem["ngm"], G * 8 + (i + 1))
                        run(PR[i % 2][:, 0:nk], PS[:, 0:nk], ACT.Exp, "exp", scale=SCALE,
                            bias=smx[:, 2 + i % 2:3 + i % 2], accum_out=smx[:, 4 + i % 2:5 + i % 2])
                        if i:
                            copy_turned(i - 1)
                    copy_turned(7)
                end_stage(act, 6 * hf + 2)

                with act.Fori(0, KD) as n:
                    N = n + KD * hf
                    act.wait_ge(sem["pga"], N + 1)
                    act.wait_ge(sem["m1"], N)
                    run(sga, bank(2), ACT.Sigmoid, "sga")
                    act.wait_ge(sem["pgb"], N + 1)
                    act.wait_ge(sem["m2"], N)
                    run(sgb, bank(3), ACT.Sigmoid, "sgb")
                end_stage(act, 6 * hf + 3)

                for b in range(NB):
                    n = NB * hf + b
                    act.wait_ge(sem["n2"], n + 1)
                    act.wait_ge(sem["n3"], n)
                    run(junk, R1[b % 2], ACT.Square, "n3", bias=st1[:, 8 * b + 2:8 * b + 3],
                        accum_out=st1[:, 8 * b + 3:8 * b + 4])
                    act.wait_ge(sem["n3"], n + 1)
                    run(st1[:, 8 * b + 4:8 * b + 5], st1[:, 8 * b + 3:8 * b + 4], ACT.Sqrt, "n4", scale=1.0 / D,
                        bias=EPSC)
                    act.wait_ge(sem["hT"], n + 1)
                    for j in range(2):
                        run(HT[:, 4 * j:4 * j + 4, cols(b)],
                            bank(2 * b + j).rearrange("p (x y) -> p x y", x=4), ACT.Copy, "hTe")
                end_stage(act, 6 * hf + 4)

                with act.Fori(0, PH) as h:
                    H = h + PH * hf
                    for j in range(2):
                        act.wait_ge(sem["pq"], H * 2 + (j + 1))
                        act.wait_ge(sem["ps"], H * 2 + j)
                        run(qT[j], bank(j), ACT.Copy, "pqe")
                    for j in range(2):
                        act.wait_ge(sem["ps"], H * 2 + (j + 1))
                        act.wait_ge(sem["t2nd"], H * 2)
                        run(SS[:, j, :, :], bank(2 + j), ACT.Copy, "pse")
                    act.wait_ge(sem["gmx"], H + 1)
                    act.wait_ge(sem["dvc"], H * 14)
                    run(ge, gd, ACT.Exp, "gex")
                end_stage(act, 6 * hf + 5)

            with act.Fori(0, NBLK) as t:
                with act.Fori(0, NGRP // 2) as q:
                    for z in range(2):
                        T = (t * (NGRP // 2) + q) * 2 + z
                        mine = slice(GRP * z, GRP * z + GRP)
                        act.wait_ge(sem["g_dot"], T * GRP + GRP)
                        act.wait_ge(sem["gac"], T)
                        run(ag[:, mine], av[:, mine], ACT.Gelu_apprx_tanh, "gel")
                        act.wait_ge(sem["gac"], T + 1)
                        for s in range(GRP * z, GRP * z + GRP):
                            act.wait_ge(sem["gmm"], T * GRP + (s - GRP * z + 1))
                            run(DG[s], ident, ACT.Copy, "gdg", scale=aw[:, s:s + 1])
                act.wait_ge(sem["l4"], t + 1)
                run(O2, O1, ACT.Square, "l5", bias=st2[:, 2:3], accum_out=st2[:, 3:4])
                act.wait_ge(sem["l5"], t + 1)
                run(st2[:, 4:5], st2[:, 3:4], ACT.Sqrt, "l6", scale=1.0 / D, bias=EPSC)

        @block.vector
        def _(dve):
            tt, ts, stt = dve.tensor_tensor, dve.tensor_scalar, dve.scalar_tensor_tensor

            NOTSTART, END = C[:, C_NS:C_NS + HALF], C[:, C_END:C_END + HALF]
            dve.memset(EPSC, EPS).then_inc(sem["start"], 1)
            dve.memset(mfm[:, P:P + 1], 0.0).then_inc(sem["start"], 1)
            dve.memset(fm[:, HALF:HALF + 1], 0.0).then_inc(sem["start"], 1)
            dve.wait_ge(sem["start"], 3)
            dve.wait_ge(sem["c_in"], 64)
            dve.tensor_copy(MB[:], y1).then_inc(sem["start"], 1)
            dve.wait_ge(sem["start"], 4)
            tt(small[:, 40:48], PV[:, 0:8], PV[:, 8:16], ALU.max).then_inc(sem["lb_ready"], 1)
            dve.wait_ge(sem["lb_ready"], 1)
            for j in range(2):
                tt(small[:, 24 + 8 * j:32 + 8 * j], PV[:, 8 * j:8 * j + 8], small[:, 40:48], ALU.subtract
                   ).then_inc(sem["lb_ready"], 1)
            dve.wait_ge(sem["lb_ready"], 4)
            tt(small[:, 48:56], small[:, 24:32], small[:, 32:40], ALU.add).then_inc(sem["lb_ready"], 1)
            dve.wait_ge(sem["lb_ready"], 5)
            dve.reciprocal(small[:, 48:56], small[:, 48:56]).then_inc(sem["lb_ready"], 1)
            dve.wait_ge(sem["lb_ready"], 6)
            tt(LB, small[:, 24:32], small[:, 48:56], ALU.mult).then_inc(sem["lb_ready"], 1)
            dve.wait_ge(sem["lb_ready"], 7)
            ts(OML, LB, -1.0, 1.0, ALU.mult, ALU.add).then_inc(sem["lb_ready"], 1)
            dve.wait_ge(sem["lb_ready"], 8)
            dve.wait_ge(sem["m_act"], 1)
            by_head = lambda x: x.rearrange("p (h t) -> p h t", h=HG)
            tt(by_head(mf), by_head(msg), OML.unsqueeze(2).to_broadcast([P, HG, META]), ALU.mult
               ).then_inc(sem["m_dve"], 1)
            dve.wait_ge(sem["m_dve"], 1)
            tt(by_head(mf), by_head(mf), LB.unsqueeze(2).to_broadcast([P, HG, META]), ALU.add
               ).then_inc(sem["m_dve"], 1)
            dve.wait_ge(sem["m_dve"], 2)
            tt(mfm[:, 0:P], mf, NOTSTART[:, 0:P], ALU.mult).then_inc(sem["m_dve"], 1)
            dve.wait_ge(sem["m_dve"], 3)
            dve.tensor_tensor_scan(mest[:, ::-1], mfm[:, P:0:-1], END[:, P - 1::-1], 0.0, ALU.mult, ALU.add
                                   ).then_inc(sem["m_dve"], 1)
            dve.wait_ge(sem["m_pe"], 2)
            dve.tensor_copy(S_all[:], PS[:, 2560:2560 + HG * P]).then_inc(sem["m_dve"], 1)

            for hf in range(NH):
                def chain(g, h):
                    dve.wait_ge(sem["sig"], g + 1)
                    dve.wait_ge(sem["k"], g)
                    dve.wait_ge(sem["ebi"], g)
                    dve.wait_ge(sem["est"], g)
                    dve.wait_ge(sem["qd16"], g)
                    ts(f, sg, fcol[:, 1:2], fcol[:, 0:1], ALU.mult, ALU.add).then_inc(sem["f"], 2)
                    dve.wait_ge(sem["f"], g * 2 + 2)
                    tt(fm[:, 0:HALF], f, NOTSTART, ALU.mult).then_inc(sem["fm"], 1)
                    dve.wait_ge(sem["fm"], g + 1)
                    tt(fs, f, fm[:, 0:HALF], ALU.subtract).then_inc(sem["fs"], 1)
                    dve.wait_ge(sem["ks16"], g)
                    dve.tensor_tensor_scan(est[:, ::-1], fm[:, HALF:0:-1], END[:, ::-1], 0.0, ALU.mult, ALU.add
                                           ).then_inc(sem["est"], 1)
                    dve.wait_ge(sem["fs"], g + 1)
                    dve.wait_ge(sem["D"], g)
                    dve.tensor_tensor_scan(eb, fm[:, 0:HALF], fs, 0.0, ALU.mult, ALU.add).then_inc(sem["eb"], 1)
                    dve.wait_ge(sem["eb"], g + 1)
                    dve.wait_ge(sem["ki"], g)
                    dve.reciprocal(ebi, eb).then_inc(sem["ebi"], 1)

                def queries(g):
                    dve.wait_ge(sem["Q"], g + 1)
                    dve.wait_ge(sem["M2"], g)
                    dve.wait_ge(sem["qd32"], g)
                    tt(qd16, bank(2), eb, ALU.mult).then_inc(sem["qd16"], 1)

                def gate(g):
                    dve.wait_ge(sem["sigG"], g + 1)
                    dve.wait_ge(sem["y"], g)
                    tt(t2, bank(1), sg2, ALU.mult).then_inc(sem["t2"], 1)

                def columns(g, h):
                    dve.wait_ge(sem["f"], g * 2)
                    apart(dve)
                    dve.tensor_copy(fcol[:, 0:1], LB[:, bass.ds(h, 1)]).then_inc(sem["fcol"], 1)
                    dve.tensor_copy(fcol[:, 1:2], OML[:, bass.ds(h, 1)]).then_inc(sem["fcol"], 1)
                    dve.wait_ge(sem["fcol"], g * 2 + 2)

                def head(g, h, following):
                    dve.wait_ge(sem["M1"], g + 1)
                    dve.wait_ge(sem["inter"], g * NPAIR)
                    tt(sc, bank(4), C[:, C_MA:C_MA + HALF], ALU.mult).then_inc(sem["sA"], 1)
                    dve.wait_ge(sem["y1"], g)
                    apart(dve)
                    dve.tensor_copy(fcol[:, 2:3], PV[:, bass.ds(h + 16, 1)]).then_inc(sem["gcol"], 1)
                    dve.tensor_copy(Spp[0], S_all[:, bass.ds(h, 1), :]).then_inc(sem["S0"], 1)
                    dve.wait_ge(sem["M2"], g + 1)
                    dve.wait_ge(sem["sA"], g + 1)
                    apart(dve)
                    dve.copy_predicated(sc, MB[:], bank(5)).then_inc(sem["sc"], 1)
                    dve.wait_ge(sem["D"], g + 1)
                    dve.wait_ge(sem["S0"], g + 1)
                    for p in range(NPAIR):
                        dve.wait_ge(sem["St"], g * NPAIR + (p + 1))
                        dve.wait_ge(sem["inter"], g * NPAIR + p)
                        if p:
                            dve.wait_ge(sem["st"], g * NPAIR + p)
                        stt(Spp[(p + 1) % 2], Spp[p % 2], Dp[:, p:p + 1], bank(7 if p % 2 == 0 else 5)[:, 0:P],
                            ALU.mult, ALU.add).then_inc(sem["st"], 1)
                    dve.wait_ge(sem["st"], g * NPAIR + NPAIR)
                    apart(dve)
                    dve.tensor_copy(S_all[:, bass.ds(h, 1), :], Spp[0]).then_inc(sem["Sb"], 1)
                    if following:
                        columns(g + 1, h + 1)
                        chain(g + 1, h + 1)
                    dve.wait_ge(sem["std"], g + 1)
                    dve.wait_ge(sem["y"], g)
                    dve.reciprocal(rs, std).then_inc(sem["rs"], 1)
                    dve.wait_ge(sem["rs"], g + 1)
                    stt(y1, bank(6), fcol[:, 2:3], rs, ALU.mult, ALU.mult).then_inc(sem["y1"], 1)
                    dve.wait_ge(sem["y1"], g + 1)
                    tt(YH[:, bass.ds(h, 1), :], y1.unsqueeze(1), t2.unsqueeze(1), ALU.mult).then_inc(sem["y"], 1)
                    if following:
                        gate(g + 1)
                        queries(g + 1)
                    dve.wait_ge(sem["Sb"], g + 1)
                    apart(dve)

                columns(HG * hf, 0)
                chain(HG * hf, 0)
                gate(HG * hf)
                queries(HG * hf)
                with dve.Fori(0, HG - 1) as h:
                    head(h + HG * hf, h, True)
                head(HG * hf + HG - 1, HG - 1, False)
                end_stage(dve, 6 * hf)

                t0 = META + HALF * hf
                dve.wait_ge(sem["stdq"], hf + 1)
                dve.reciprocal(crs, cstd).then_inc(sem["rsq"], 1)
                dve.wait_ge(sem["rsq"], hf + 1)
                for i in range(QT):
                    stt(cqn[:, i, :], bank(i), PV[:, 24 + i:25 + i], crs, ALU.mult, ALU.mult).then_inc(sem["cn"], 1)
                dve.wait_ge(sem["stdkv"], hf + 1)
                dve.wait_ge(sem["cn"], QT * hf + QT)
                dve.reciprocal(crs, cstd).then_inc(sem["rskv"], 1)
                dve.wait_ge(sem["rskv"], hf + 1)
                for i in range(KVT):
                    stt(ckvn[:, i, t0:t0 + HALF], bank(QT + i), PV[:, 27 + i:28 + i], crs, ALU.mult, ALU.mult
                        ).then_inc(sem["ckn"], 1)
                dve.wait_ge(sem["cj"], 7 * hf + 7)
                tt(kta, bank(5), C[:, C_COS + t0:C_COS + t0 + HALF], ALU.mult).then_inc(sem["krA"], 1)
                tt(ktb, bank(6), C[:, C_SIN + t0:C_SIN + t0 + HALF], ALU.mult).then_inc(sem["krB"], 1)
                dve.wait_ge(sem["krA"], hf + 1)
                dve.wait_ge(sem["krB"], hf + 1)
                tt(krT[:, t0:t0 + HALF], kta, ktb, ALU.add).then_inc(sem["kr"], 1)
                if hf == 0:
                    dve.wait_ge(sem["m_act"], 5)
                    dve.reciprocal(mrs, mstd).then_inc(sem["m_dve"], 1)
                    dve.wait_ge(sem["m_dve"], 6)
                    for i in range(KVT):
                        stt(ckvn[:, i, 0:META], bank(7)[:, META * i:META * i + META], PV[:, 27 + i:28 + i], mrs,
                            ALU.mult, ALU.mult).then_inc(sem["m_dve"], 1)
                    tt(mka, bank(7)[:, 2 * META:3 * META], C[:, C_COS:C_COS + META], ALU.mult
                       ).then_inc(sem["m_dve"], 1)
                    tt(mkb, bank(7)[:, 3 * META:4 * META], C[:, C_SIN:C_SIN + META], ALU.mult
                       ).then_inc(sem["m_dve"], 1)
                    dve.wait_ge(sem["m_dve"], 10)
                    tt(krT[:, 0:META], mka, mkb, ALU.add).then_inc(sem["m_dve"], 1)
                end_stage(dve, 6 * hf + 1)

                groups = groups_of(hf)
                with dve.Fori(0, 8) as u:
                    G = u + 8 * hf
                    for what, arg, b, n in jobs_of(hf):
                        if b == 6:
                            continue
                        dve.wait_ge(sem["j7"], before(lambda x: bank_jobs(x, 7), hf, u) + (n + 1))
                        if what == "qrA":
                            dve.wait_ge(sem["e7"], before(lambda x: bank_jobs(x, 7), hf, u))
                            tt(qra, bank(7), C[:, C_COS + t0:C_COS + t0 + HALF], ALU.mult).then_inc(sem["e7"], 1)
                        elif what == "qrB":
                            tt(qrb, bank(7), C[:, C_SIN + t0:C_SIN + t0 + HALF], ALU.mult).then_inc(sem["qrb"], 1)
                            dve.wait_ge(sem["qrb"], G + 1)
                            tt(qr, qra, qrb, ALU.add).then_inc(sem["e7"], 1)
                        elif what == "kn":
                            e, c, n_ = arg
                            dve.tensor_copy(kn[e][:, c:c + n_], bank(7)[:, 0:n_]).then_inc(sem["e7"], 1)
                        else:
                            j, many = arg
                            r = P if many == 2 else META
                            dve.tensor_copy(V[0:r, j:j + many, :], bank(7)[0:r, 0:256 * many]).then_inc(sem["e7"], 1)

                    def copy_turned(i):
                        for tiles, bk, n in groups[i]:
                            if bk == 4:
                                dve.wait_ge(sem["pt4"], before(lambda x: bank_groups(x, 4), hf, u) + (n + 1))
                                dve.wait_ge(sem["pv4"], before(lambda x: bank_groups(x, 4), hf, u) + n)
                                full = [t for t in tiles if rows_of(hf, i % 4, t) == P]
                                if full:
                                    one = dve.tensor_copy(PTs[1][:, 0:P * len(full)], bank(4)[:, 0:P * len(full)])
                                if len(full) < len(tiles):
                                    s = len(full)
                                    one = dve.tensor_copy(PTs[1][0:META, cols(s)], bank(4)[0:META, cols(s)])
                                one.then_inc(sem["pe4"], 1)

                    for i in range(8):
                        nk = keys_of(hf, i % 4)
                        dve.wait_ge(sem["Sm"], G * 8 + (i + 1))
                        tt(PS[:, nk - P:nk], PS[:, nk - P:nk], C[:, C_CAUS:C_CAUS + P], ALU.add
                           ).then_inc(sem["cau"], 1)
                        dve.wait_ge(sem["cau"], G * 8 + (i + 1))
                        dve.wait_ge(sem["ngm"], G * 8 + i)
                        dve.reduce_max(smx[:, i % 2:i % 2 + 1], PS[:, 0:nk], AX).then_inc(sem["mx"], 1)
                        dve.wait_ge(sem["mx"], G * 8 + (i + 1))
                        ts(smx[:, 2 + i % 2:3 + i % 2], smx[:, i % 2:i % 2 + 1], -SCALE, None, ALU.mult
                           ).then_inc(sem["ngm"], 1)
                        if i:
                            copy_turned(i - 1)
                        dve.wait_ge(sem["exp"], G * 8 + (i + 1))
                        dve.wait_ge(sem["pn"], G * 8 + max(i - 1, 0))
                        dve.reciprocal(smx[:, 6 + i % 2:7 + i % 2], smx[:, 4 + i % 2:5 + i % 2]
                                       ).then_inc(sem["rcp"], 1)
                    copy_turned(7)
                end_stage(dve, 6 * hf + 2)

                with dve.Fori(0, KD) as n:
                    N = n + KD * hf
                    dve.wait_ge(sem["pya"], N + 1)
                    dve.wait_ge(sem["sga"], N + 1)
                    dve.wait_ge(sem["mix"], N)
                    tt(mm1, bank(0), sga, ALU.mult).then_inc(sem["m1"], 1)
                    dve.wait_ge(sem["pyb"], N + 1)
                    dve.wait_ge(sem["sgb"], N + 1)
                    tt(mm2, bank(1), sgb, ALU.mult).then_inc(sem["m2"], 1)
                    dve.wait_ge(sem["m2"], N + 1)
                    tt(MIX[:, bass.ds(n, 1), :], mm1.unsqueeze(1), mm2.unsqueeze(1), ALU.add).then_inc(sem["mix"], 1)
                end_stage(dve, 6 * hf + 3)

                dve.wait_ge(sem["xk_in"], 16 * hf + 16)
                dve.wait_ge(sem["ln_in"], 16 * hf + 16)
                for b in range(NB):
                    n = NB * hf + b
                    c0 = 8 * b
                    dve.wait_ge(sem["wo"], 2 * n + 2)
                    if n >= 2:
                        dve.wait_ge(sem["n8"], n - 1)
                    for j in range(2):
                        stt(R1[b % 2][:, 512 * j:512 * j + 512], XK[:, b, 512 * j:512 * j + 512], ALPHA,
                            bank(2 * b + j), ALU.mult, ALU.add, accum_out=st1[:, c0 + j:c0 + j + 1]
                            ).then_inc(sem["r"], 1)
                    dve.wait_ge(sem["r"], 2 * n + 2)
                    tt(st1[:, c0 + 2:c0 + 3], st1[:, c0:c0 + 1], st1[:, c0 + 1:c0 + 2], ALU.add
                       ).then_inc(sem["nd"], 1)
                    dve.wait_ge(sem["nd"], 4 * n + 1)
                    ts(st1[:, c0 + 2:c0 + 3], st1[:, c0 + 2:c0 + 3], -1.0 / D, None, ALU.mult
                       ).then_inc(sem["n2"], 1)
                    dve.wait_ge(sem["n4"], n + 1)
                    dve.reciprocal(st1[:, c0 + 5:c0 + 6], st1[:, c0 + 4:c0 + 5]).then_inc(sem["nd"], 1)
                    dve.wait_ge(sem["nd"], 4 * n + 2)
                    ts(R1[b % 2], R1[b % 2], st1[:, c0 + 2:c0 + 3], st1[:, c0 + 5:c0 + 6], ALU.add, ALU.mult
                       ).then_inc(sem["nd"], 1)
                    dve.wait_ge(sem["nd"], 4 * n + 3)
                    tt(R1[b % 2], R1[b % 2], LN1[:, 0, :], ALU.mult).then_inc(sem["nd"], 1)
                    dve.wait_ge(sem["nd"], 4 * n + 4)
                    if b >= 2:
                        dve.wait_ge(sem["hT"], n - 1)
                        dve.wait_ge(sem["h_out"], 16 * (n - 1))
                    tt(R2[b % 2], R1[b % 2], LN1[:, 1, :], ALU.add).then_inc(sem["n8"], 1)
                end_stage(dve, 6 * hf + 4)

                big = -3e38

                with dve.Fori(0, PH) as h:
                    H = h + PH * hf
                    sets = [(j, b) for j in range(2) for b in range(NB)]

                    def wave(op, n, k, name, base):
                        for s in range(n):
                            op(s).then_inc(sem[name], 1)
                        dve.wait_ge(sem[name], base + n * k)
                        apart(dve)

                    B1 = H * 40
                    dve.wait_ge(sem["pse"], H * 2 + 2)
                    dve.wait_ge(sem["dvc"], H * 14)
                    dve.wait_ge(sem["gmx"], H)
                    apart(dve)
                    S = lambda s: SS[:, s // NB, s % NB, :]
                    S2 = lambda s: SS2[:, s // NB, s % NB, :]
                    tV = lambda s: tv[:, s // NB, s % NB, :]
                    tI = lambda s: ti[:, s // NB, s % NB, :]
                    wave(lambda s: dve.max(tV(s)[:, 0:8], S(s)), 8, 1, "dv", B1)
                    wave(lambda s: dve.max_index(tI(s)[:, 0:8], tV(s)[:, 0:8], S(s)), 8, 2, "dv", B1)
                    wave(lambda s: dve.match_replace(S2(s), tV(s)[:, 0:8], S(s), big), 8, 3, "dv", B1)
                    wave(lambda s: dve.max(tV(s)[:, 8:16], S2(s)), 8, 4, "dv", B1)
                    wave(lambda s: dve.max_index(tI(s)[:, 8:16], tV(s)[:, 8:16], S2(s)), 8, 5, "dv", B1)
                    dve.tensor_copy(tif[:, :, 0, :], ti[:, 0, :, :]).then_inc(sem["t2nd"], 1)
                    dve.tensor_copy(tif[:, :, 1, :], ti[:, 1, :, :]).then_inc(sem["t2nd"], 1)
                    B2 = H * 24
                    wave(lambda b: tt(CA[:, b, :].rearrange("p (x y) -> p x y", x=TOP),
                                      tv[:, 0, b, :].unsqueeze(2).to_broadcast([P, TOP, TOP]),
                                      tv[:, 1, b, :].unsqueeze(1).to_broadcast([P, TOP, TOP]), ALU.add),
                         4, 1, "dvb", B2)
                    wave(lambda b: dve.max(bv[:, b, 0:8], CA[:, b, :]), 4, 2, "dvb", B2)
                    wave(lambda b: dve.max_index(bs[:, b, 0:8], bv[:, b, 0:8], CA[:, b, :]), 4, 3, "dvb", B2)
                    wave(lambda b: dve.match_replace(CA2[:, b, :], bv[:, b, 0:8], CA[:, b, :], big),
                         4, 4, "dvb", B2)
                    wave(lambda b: dve.max(bv[:, b, 8:16], CA2[:, b, :]), 4, 5, "dvb", B2)
                    wave(lambda b: dve.max_index(bs[:, b, 8:16], bv[:, b, 8:16], CA2[:, b, :]), 4, 6, "dvb", B2)
                    dve.wait_ge(sem["gex"], H)
                    tt(gd, bv, bv[:, :, 0:1].to_broadcast([P, NB, TOP]), ALU.subtract).then_inc(sem["gmx"], 1)
                    ts(bs2[:, :, :, 0], bs, 4, None, ALU.logical_shift_right).then_inc(sem["dvc"], 1)
                    ts(bs2[:, :, :, 1], bs, 15, None, ALU.bitwise_and).then_inc(sem["dvc"], 1)
                    dve.wait_ge(sem["dvc"], H * 14 + 2)
                    dve.tensor_copy(bsf, bs2).then_inc(sem["dvc"], 1)
                    dve.wait_ge(sem["dvc"], H * 14 + 3)
                    oh = OH.rearrange("p (b j z r) -> p b j z r", b=NB, j=TOP, z=2)
                    oh2 = OH2.rearrange("p (b j z r) -> p b j z r", b=NB, j=TOP, z=2)
                    tt(OH.rearrange("p (n r) -> p n r", r=TOP),
                       bsf.rearrange("p b j z -> p (b j z)").unsqueeze(2).to_broadcast([P, NB * TOP * 2, TOP]),
                       C[:, C_IOTA:C_IOTA + TOP].unsqueeze(1).to_broadcast([P, NB * TOP * 2, TOP]), ALU.is_equal
                       ).then_inc(sem["dvc"], 1)
                    dve.wait_ge(sem["dvc"], H * 14 + 4)
                    dve.wait_ge(sem["t2nd"], H * 2 + 2)
                    for b in range(NB):
                        tt(oh2[:, b], oh[:, b], tif[:, b].unsqueeze(1).to_broadcast([P, TOP, 2, TOP]), ALU.mult
                           ).then_inc(sem["dvc"], 1)
                    dve.wait_ge(sem["dvc"], H * 14 + 8)
                    dve.tensor_reduce(osum.rearrange("p b j z -> p (b j z)"),
                                      OH2.rearrange("p (n r) -> p n r", r=TOP), AX, ALU.add).then_inc(sem["dvc"], 1)
                    dve.wait_ge(sem["dvc"], H * 14 + 9)
                    stt(eif, osum[:, :, :, 0], 128.0, osum[:, :, :, 1], ALU.mult, ALU.add).then_inc(sem["dvc"], 1)
                    dve.wait_ge(sem["dvc"], H * 14 + 10)
                    apart(dve)
                    dve.tensor_copy(EIDX[:, NB * hf:NB * hf + NB, bass.ds(h * TOP, TOP)], eif
                                    ).then_inc(sem["dvc"], 1)
                    dve.wait_ge(sem["gex"], H + 1)
                    dve.tensor_reduce(gs, ge, AX, ALU.add).then_inc(sem["dvc"], 1)
                    dve.wait_ge(sem["dvc"], H * 14 + 12)
                    dve.reciprocal(gr, gs).then_inc(sem["dvc"], 1)
                    dve.wait_ge(sem["dvc"], H * 14 + 13)
                    tt(GATE[:, NB * hf:NB * hf + NB, bass.ds(h * TOP, TOP)], ge,
                       gr.unsqueeze(2).to_broadcast([P, NB, TOP]), ALU.mult).then_inc(sem["dvc"], 1)
                end_stage(dve, 6 * hf + 5)

            dve.memset(zero, 0.0).then_inc(sem["gz"], 1)
            dve.memset(st2, 0.0).then_inc(sem["gmm"], GSLOT)
            dve.wait_ge(sem["gmm"], GSLOT)
            with dve.Fori(0, NBLK) as t:
                dve.wait_ge(sem["g_h"], t * 16 + 16)
                apart(dve)
                with dve.Fori(0, NGRP // 2) as q:
                    for z in range(2):
                        T = (t * (NGRP // 2) + q) * 2 + z
                        mine = slice(GRP * z, GRP * z + GRP)
                        dve.wait_ge(sem["gel"], T)
                        for s in range(GRP * z, GRP * z + GRP):
                            dve.wait_ge(got[s], (t * (NGRP // 2) + q) * 16 + 16)
                            if s > GRP * z:
                                dve.wait_ge(sem["g_dot"], T * GRP + (s - GRP * z - 1))
                            dve.tensor_tensor_reduce(GJ[s % 2], ROW[s][:, 0:D], HB, 1.0, 0.0, ALU.mult, ALU.add,
                                                     av[:, s:s + 1]).then_inc(sem["g_dot"], 1)
                        dve.wait_ge(sem["gel"], T + 1)
                        dve.wait_ge(sem["gdg"], T * GRP)
                        tt(aw[:, mine], ag[:, mine], GATE[:, bass.ds(t, 1), bass.ds(q * GSLOT + GRP * z, GRP)
                                                          ].rearrange("p a b -> p (a b)"),
                           ALU.mult).then_inc(sem["gac"], 1)
                dve.wait_ge(sem["gmm"], (t + 1) * NSEL + GSLOT)
                dve.wait_ge(sem["l9"], t)
                dve.wait_ge(sem["ld"], t * 5)
                for j in range(2):
                    one = stt(O1[:, 512 * j:512 * j + 512], HB[:, 512 * j:512 * j + 512], ALPHA, bank(j),
                              ALU.mult, ALU.add, accum_out=st2[:, j:j + 1])
                    one.then_inc(sem["ld"], 1)
                dve.wait_ge(sem["ld"], t * 5 + 2)
                tt(st2[:, 2:3], st2[:, 0:1], st2[:, 1:2], ALU.add).then_inc(sem["l1"], 1)
                dve.wait_ge(sem["l1"], t + 1)
                dve.wait_ge(sem["out_done"], t * 16)
                ts(st2[:, 2:3], st2[:, 2:3], -1.0 / D, None, ALU.mult).then_inc(sem["l4"], 1)
                dve.wait_ge(sem["l6"], t + 1)
                dve.reciprocal(st2[:, 5:6], st2[:, 4:5]).then_inc(sem["ld"], 1)
                dve.wait_ge(sem["ld"], t * 5 + 3)
                ts(O2, O1, st2[:, 2:3], st2[:, 5:6], ALU.add, ALU.mult).then_inc(sem["ld"], 1)
                dve.wait_ge(sem["ld"], t * 5 + 4)
                dve.wait_ge(sem["g_ln"], 16)
                tt(O1, O2, LN2[:, 0, :], ALU.mult).then_inc(sem["ld"], 1)
                dve.wait_ge(sem["ld"], t * 5 + 5)
                tt(O2, O1, LN2[:, 1, :], ALU.add).then_inc(sem["l9"], 1)

        @block.gpsimd
        def _(pool):
            tt, ts = pool.tensor_tensor, pool.tensor_scalar
            halves = lambda x: x.rearrange("p (n z t) -> p n z t", z=2, t=CHUNK)
            pool.wait_ge(sem["m_dve"], 2)
            ts(mk, mf, -1.0, 1.0, ALU.mult, ALU.add).then_inc(sem["m_pool"], 1)
            pool.wait_ge(sem["m_pool"], 1)
            pool.wait_ge(sem["m_dve"], 4)
            tt(mks, mk, mest, ALU.mult).then_inc(sem["m_pool"], 1)
            for hf in range(NH):
                with pool.Fori(0, HG) as h:
                    g = h + HG * hf
                    pool.wait_ge(sem["f"], g * 2 + 2)
                    pool.wait_ge(sem["ks16"], g)
                    pool.wait_ge(sem["ki"], g)
                    apart(pool)
                    ts(k, f, -1.0, 1.0, ALU.mult, ALU.add).then_inc(sem["k"], 1)
                    pool.wait_ge(sem["k"], g + 1)
                    pool.wait_ge(sem["est"], g + 1)
                    pool.wait_ge(sem["M2"], g)
                    tt(ks16, k, est, ALU.mult).then_inc(sem["ks16"], 1)
                    pool.wait_ge(sem["eb"], g + 1)
                    ends = halves(eb)[:, :, :, CHUNK - 1:CHUNK]
                    pool.wait_ge(sem["ks16"], g + 1)
                    pool.wait_ge(sem["T"], g)
                    tt(halves(ks32)[:, :, 0, :], halves(ks16)[:, :, 0, :],
                       ends[:, :, 1, :].to_broadcast([P, NPAIR, CHUNK]), ALU.mult).then_inc(sem["ks32a"], 1)
                    pool.tensor_copy(halves(ks32)[:, :, 1, :], halves(ks16)[:, :, 1, :]).then_inc(sem["ks32"], 1)
                    pool.wait_ge(sem["ebi"], g + 1)
                    pool.wait_ge(sem["M1"], g)
                    tt(ki, k, ebi, ALU.mult).then_inc(sem["ki"], 1)
                    pool.wait_ge(sem["st"], g * NPAIR)
                    tt(Dp.unsqueeze(2), ends[:, :, 0, :], ends[:, :, 1, :], ALU.mult).then_inc(sem["D"], 1)
                    pool.wait_ge(sem["qd16"], g + 1)
                    pool.wait_ge(sem["inter"], g * NPAIR)
                    tt(halves(qd32)[:, :, 1, :], halves(qd16)[:, :, 1, :],
                       ends[:, :, 0, :].to_broadcast([P, NPAIR, CHUNK]), ALU.mult).then_inc(sem["qd32a"], 1)
                    pool.tensor_copy(halves(qd32)[:, :, 0, :], halves(qd16)[:, :, 0, :]).then_inc(sem["qd32"], 1)
                end_stage(pool, 6 * hf)
                end_stage(pool, 6 * hf + 1)
                with pool.Fori(0, 8) as u:
                    for i in range(8):
                        nk = keys_of(hf, i % 4)
                        pool.wait_ge(sem["rcp"], (u + 8 * hf) * 8 + (i + 1))
                        apart(pool)
                        ts(PR[i % 2][:, 0:nk], PR[i % 2][:, 0:nk], smx[:, 6 + i % 2:7 + i % 2], 1.0, ALU.mult,
                           ALU.mult).then_inc(sem["pn"], 1)
                for s in range(2, 6):
                    end_stage(pool, 6 * hf + s)
            with pool.Fori(0, NBLK) as t:
                with pool.Fori(0, NGRP // 4) as q:
                    for z in range(2):
                        T = (t * (NGRP // 4) + q) * 2 + z
                        pool.wait_ge(sem["gmm"], T * GSLOT)
                        apart(pool)
                        pool.tensor_copy(IDX[z], EIDX[:, bass.ds(t, 1), bass.ds((q * 2 + z) * GSLOT, GSLOT)
                                                      ].rearrange("p a b -> p (a b)")).then_inc(sem["gidx"], 1)
                        pool.wait_ge(sem["gidx"], T + 1)
                        for s in range(GSLOT):
                            pool.wait_ge(sem["gmm"], T * GSLOT + (s + 1))
                            pool.wait_ge(got[s], T * 16)
                            apart(pool)
                            pool.indirect_dma_start(ROW[s], None, a["uv"], bass.IndirectOffsetOnAxis(
                                ap=IDX[z][:, s:s + 1], axis=0)).then_inc(got[s], 16)


def program(nc, a, out):
    build_program(nc, {**a, "out": out})


def kernel(**inputs):
    import concourse.bacc as bacc
    from concourse.bass_utils import run_bass_kernel_spmd

    x, w_in = inputs["x"][0], inputs["w_in"][0]
    w = {k: inputs[k][0] for k in ("w_uq", "w_ukv", "w_proj_hgrn", "w_proj_mla", "w_out", "peer_query",
                                   "peer_sub_keys", "peer_u", "peer_v")}

    def tiles(m):
        return m.reshape(-1, P, m.shape[1]).transpose(1, 0, 2)

    consts, cross = constants()
    q, f, i, g = (w_in[:, D * n:D * n + D] for n in range(4))
    whg = np.stack([tiles(m).reshape(P, KD, HG, P) for m in (f, g, q, i)])
    o = 4 * D
    cq, ckv, kr = w_in[:, o:o + 384], w_in[:, o + 384:o + 640], w_in[:, o + 640:o + 704]
    ga, gb = w_in[:, o + 704:o + 704 + D], w_in[:, o + 704 + D:]
    swap = np.concatenate([kr[:, 32:], kr[:, :32]], 1)
    wc = np.concatenate([cq, ckv, kr, kr, swap, swap], 1)
    uq = w["w_uq"].reshape(384, 8, 2, 192)
    ra, rb = uq[..., 128:], np.concatenate([uq[..., 160:], uq[..., 128:160]], -1)
    wuq = np.stack([uq[:, :, 0, :128], uq[:, :, 1, :128], ra.reshape(384, 8, 128), rb.reshape(384, 8, 128)], 2)
    ukv = w["w_ukv"].reshape(256, 8, 2, 2, 128).transpose(0, 1, 3, 2, 4).reshape(256, 8, 4, 128)
    mix = np.concatenate([tiles(m) for m in (w["w_proj_hgrn"], w["w_proj_mla"], ga, gb)], 1)
    feat = lambda v: v.reshape(-1, P).T
    pvec = np.concatenate([feat(inputs["hgrn_lb_logits"][0]), feat(inputs["hgrn_lb_logits"][1]),
                           feat(inputs["hgrn_norm_gain"][0]), feat(inputs["q_norm_gain"][0]),
                           feat(inputs["kv_norm_gain"][0])], 1)
    rows = lambda *v: np.stack([np.broadcast_to(z[0], (P, D)) for z in v], 1)
    arrays = {
        "consts": consts, "cross": cross, "pvec": pvec,
        "xm": tiles(inputs["meta_tokens"].T),
        "xt": x.T.reshape(KD, P, NH, HALF).transpose(2, 1, 0, 3),
        "xk": x.reshape(NH, NB, P, D).transpose(0, 2, 1, 3),
        "whg": whg.transpose(3, 0, 1, 2, 4),
        "wc": tiles(wc).reshape(P, KD, 7, P),
        "wuq": wuq.reshape(QT, P, 8, 4, 128).transpose(2, 1, 0, 3, 4),
        "wukv": ukv.reshape(KVT, P, 8, 4, 128).transpose(2, 1, 0, 3, 4),
        "wmix": mix.reshape(P, 40, KD, P).transpose(2, 0, 1, 3),
        "wout": tiles(w["w_out"]),
        "ln1": rows(inputs["ln1_gain"], inputs["ln1_bias"]),
        "ln2": rows(inputs["ln2_gain"], inputs["ln2_bias"]),
        "wpq": tiles(w["peer_query"]).reshape(P, KD, PH, 2, P).transpose(2, 0, 1, 3, 4),
        "wsk": w["peer_sub_keys"].transpose(0, 3, 1, 2),
        "uv": np.concatenate([w["peer_u"], w["peer_v"]], 1),
    }
    nc = bacc.Bacc("TRN2", target_bir_lowering=False, num_devices=1)
    arrays = {"in_" + k: np.ascontiguousarray(v) for k, v in arrays.items()}
    a = {k[3:]: nc.dram_tensor(k, v.shape, mybir.dt.from_np(v.dtype), kind="ExternalInput").ap()
         for k, v in arrays.items()}
    out = nc.dram_tensor("out_0", (NBLK, P, D), F32, kind="ExternalOutput").ap()
    program(nc, a, out)
    r = run_bass_kernel_spmd(nc, [arrays], core_ids=[0])
    return r.results[0]["out_0"].reshape(1, SEQ, D)
```

```python
from contextlib import ExitStack

import numpy as np

import concourse.bass as bass
from concourse import mybir

F32 = mybir.dt.float32
U32 = mybir.dt.uint32
U8 = mybir.dt.uint8
ALU = mybir.AluOpType
ACT = mybir.ActivationFunctionType
AX = mybir.AxisListType.X

P = 128
D = 1024
KD = D // P
SEQ = 1024
META = 16
HALF = 256
NH = SEQ // HALF
NB = HALF // P
NBLK = SEQ // P
KEYS = META + SEQ
CHUNK = 16
PAIR = 2 * CHUNK
NPAIR = HALF // PAIR
HG = 8
MH = 16
QT, KVT = 3, 2
ROPE = 64
SCALE = float((128 + ROPE) ** -0.5)
PH = 8
TOP = 16
NSEL = PH * TOP
ALPHA = float(2 ** 0.25)
EPS = 1e-5
NEG = -1e30
DVC = 10
STEPS = 4
ROUNDS = NSEL // STEPS
GSLOT = STEPS * NB
R_LATENT = HG
R_ATTEND = R_LATENT + 2
R_MIX = R_ATTEND + 16
MIX_ROUNDS = 4
R_NORM = R_MIX + MIX_ROUNDS
GELU_A, GELU_B = 0.044715, 0.7978845608028654

C_ID, C_ONE, C_MA, C_NS, C_END = 0, P, 2 * P, 2 * P + HALF, 2 * P + 2 * HALF
C_CAUS = C_END + HALF
C_IOTA = C_CAUS + P
C_COS = C_IOTA + 32
C_SIN = C_COS + KEYS
C_W = C_SIN + KEYS
ARENA_W = 42400


def constants():
    c = np.zeros((P, C_W), np.float32)
    t = np.arange(HALF)
    s = np.arange(P)
    c[:, C_ID:C_ID + P] = np.eye(P)
    c[:, C_ONE:C_ONE + P] = 1.0
    tl = t % P
    c[:, C_MA:C_MA + HALF] = (s[:, None] <= tl) & (s[:, None] // CHUNK == tl // CHUNK)
    c[:, C_NS:C_NS + HALF] = t % CHUNK != 0
    c[:, C_END:C_END + HALF] = t % CHUNK == CHUNK - 1
    c[:, C_CAUS:C_CAUS + P] = np.where(s[None, :] <= s[:, None], 0.0, NEG)
    c[:, C_IOTA:C_IOTA + 32] = np.arange(32) % 16
    inv = (np.float32(10000.0) ** (-np.arange(32, dtype=np.float32) / np.float32(32))).astype(np.float32)
    ang = np.arange(KEYS, dtype=np.float32)[None, :] * inv[:, None]
    c[:, C_COS:C_COS + KEYS] = np.tile(np.cos(ang), (4, 1))
    c[:, C_SIN:C_SIN + KEYS] = np.concatenate([-np.sin(ang), np.sin(ang)] * 2)
    cross = (s[:, None] // PAIR == tl // PAIR) & (s[:, None] // CHUNK % 2 == 0) & (tl // CHUNK % 2 == 1)
    return c, cross.astype(np.float32)


def build_program(nc, a):
    with ExitStack() as ctx:
        def sb(name, shape, dt=F32, where=ctx):
            return where.enter_context(nc.sbuf_tensor(name, shape, dt))

        names = """c_in lb_ready fcol xt_in wF_in wG_in wQ_in wI_in m_F m_I F G Q I sig sigG gcol ks32a qd32a t2nd
        f fm fs eb est ebi qd16 k ki ks16 qd32 ks32 D T ksT M1 M2 sA sc st St S0 Sb inter isb sq ms std
        rs y1 y t2 wc_in cj csq mq stdq rsq cn mkv stdkv rskv ckn krA krB kr wuq_in wukv_in j6 j7 e6 e7
        qrb Sm cau mx ngm exp rcp pn pt3 pt4 pe3 pe4 pv3 pv4 OE wa_in wb_in wga_in wgb_in pga pgb
        pya pyb sga sgb m1 m2 mix wo0_in wo1_in xk_in ln_in wo r n2 n3 n4 n8 hT hTe  wpq0_in wpq1_in wsk_in pq0 pq1 pqe
        ps pse dv dvb gmx gex onehot g_dot g_z g_th g_w g_v accv accp gidx acc0 q_in q1 q2   qd
        out_done start apart m_pe
        m_act m_dve m_pool dvc nd""".split()
        sem = {n: ctx.enter_context(nc.semaphore("s_" + n)) for n in names}
        got = [ctx.enter_context(nc.semaphore(f"s_got{i}")) for i in range(GSLOT)]
        stage_done = ctx.enter_context(nc.semaphore("s_stage_done"))

        def end_stage(eng, n):
            eng.drain().then_inc(stage_done, 1)
            eng.wait_ge(stage_done, 4 * n + 4)

        def apart(eng):
            eng.sem_inc(sem["apart"], 1)

        PS = ctx.enter_context(nc.psum_tensor("PS", [P, 8 * 512], F32))

        def bank(i):
            return PS[:, 512 * i:512 * i + HALF]

        def wide(i):
            return PS[:, 512 * i:512 * i + 512]

        C = sb("C", [P, C_W])
        MB = sb("MB", [P, HALF], U8)
        PV = sb("PV", [P, 29])
        small = sb("small", [P, 64])
        fcol = small[:, 56:59]
        LB, OML = small[:, 0:8], small[:, 8:16]
        EPSC = small[:, 16:17]
        S_all = sb("S_all", [P, HG, P])
        ckvn = sb("ckvn", [P, KVT, KEYS])
        krT = sb("krT", [P, KEYS])
        EIDX = sb("EIDX", [P, NB, NSEL], U32)
        GATE = sb("GATE", [P, NB, NSEL])
        XM = sb("XM", [P, KD, META])
        ident, ones = C[:, C_ID:C_ID + P], C[:, C_ONE:C_ONE + P]

        ARENA = sb("ARENA", [P, ARENA_W])
        top = [0]

        def at(off):
            top[0] = off

        def new(n):
            v = ARENA[:, top[0]:top[0] + n]
            top[0] += n
            assert top[0] <= ARENA_W
            return v

        def new3(x, y):
            return new(x * y).rearrange("p (x y) -> p x y", x=x)

        def new4(x, y, z):
            return new(x * y * z).rearrange("p (x y z) -> p x y z", x=x, y=y)

        at(0)
        ROW = [new(2 * D) for _ in range(GSLOT)]
        HB, ACC = new3(NB, D), new3(NB, D)
        IDX = [new(NB).bitcast(U32) for _ in range(STEPS)]
        ga_, gx_, gz_, gt_, gu_, gw_ = (new(GSLOT) for _ in range(6))
        st2 = new(16)
        BASE = top[0]
        XT = new3(KD, HALF)
        YH = new3(HG, HALF)
        YM = new3(MH, HALF)
        scratch = top[0]
        at(scratch - MH * HALF)
        wF, wG, wQ, wI = (new3(KD, P) for _ in range(4))
        (sg, sg2, f, fs, k, eb, est, ebi, qd16, ki, ks16, qd32, ks32, isb, ksT, sc, t2, y1, sqh, std,
         rs) = (new(HALF) for _ in range(21))
        fm = new(HALF + 1)
        Dp = new(NPAIR)
        Spp = [new(P) for _ in range(2)]
        msg, mf, mk, mest, mks = (new(P) for _ in range(5))
        mfm = new(P + 1)
        miT, mksT = new(HG * P), new(HG * P)
        at(scratch)
        cqn = new3(QT, HALF)
        wuq = new4(QT, 4, P)
        wukv = new4(KVT, 4, P)
        attend = top[0]
        csq = new3(QT + KVT, HALF)
        cstd, crs, kta, ktb = (new(HALF) for _ in range(4))
        mcsq = new3(KVT, META)
        mstd, mrs, mka, mkb = (new(META) for _ in range(4))
        assert top[0] <= ARENA_W - 7 * KD * P
        at(ARENA_W - 7 * KD * P)
        wc = new4(KD, 7, P)
        at(attend)
        qn = [new(HALF) for _ in range(2)]
        qr, qra, qrb = (new(HALF) for _ in range(3))
        kn = [new(KEYS) for _ in range(2)]
        V = new3(NBLK + 1, 2 * P)
        PR = [new(KEYS) for _ in range(2)]
        PTs = [new(512) for _ in range(2)]
        smx = new(64)
        at(scratch)
        MIX = new3(KD, HALF)
        wa, wga, wgb = (new3(KD, P) for _ in range(3))
        wb = new3(MH, P)
        sga, sgb, mm1, mm2 = (new(HALF) for _ in range(4))
        at(BASE)
        XK = new3(NB, D)
        HT = new3(KD, HALF)
        WO = [new3(KD, D // 2)]
        assert top[0] == scratch
        at(scratch + KD * HALF)
        WO.append(new3(KD, D // 2))
        R1 = [new(D) for _ in range(2)]
        junk = new(D)
        st1 = new(64)
        assert top[0] <= ARENA_W - 4 * D
        at(ARENA_W - 4 * D)
        LN1, LN2 = new3(2, D), new3(2, D)
        at(scratch)
        wpq = [new3(KD, P) for _ in range(2)]
        wsk = new3(2, P)
        qT = [new(HALF) for _ in range(2)]
        SS, SS2 = new4(2, NB, P), new4(2, NB, P)
        tv = new4(2, NB, TOP)
        ti = new(2 * NB * TOP).bitcast(U32).rearrange("p (x y z) -> p x y z", x=2, y=NB)
        tif = new4(NB, 2, TOP)
        CA, CA2 = new3(NB, TOP * TOP), new3(NB, TOP * TOP)
        bv = new3(NB, TOP)
        bs = new(NB * TOP).bitcast(U32).rearrange("p (x y) -> p x y", x=NB)
        bs2 = new(2 * NB * TOP).bitcast(U32).rearrange("p (x y z) -> p x y z", x=NB, y=TOP)
        bsf = new4(NB, TOP, 2)
        OH, OH2 = new(NB * TOP * 2 * TOP), new(NB * TOP * 2 * TOP)
        osum = new4(NB, TOP, 2)
        eif, ge, gd = (new3(NB, TOP) for _ in range(3))
        gs, gr = new(NB), new(NB)
        block = ctx.enter_context(nc.Block())

        def jobs_of(hf):
            nfull = NB * (hf + 1)
            out = [("qrA", None), ("qn", 0), ("qrB", None), ("qn", 1)]
            out += [("kn", (e, c, min(512, META + HALF * (hf + 1) - c)))
                    for c in range(0, META + HALF * (hf + 1), 512) for e in range(2)]
            out += [("v", (j, 2)) for j in range(0, nfull, 2)] + [("v", (nfull, 1))]
            return [(what, arg, 7 - i % 2, i // 2) for i, (what, arg) in enumerate(out)]

        def bank_jobs(hf, b):
            return sum(j[2] == b for j in jobs_of(hf))

        def before(count, hf, u):
            return count(hf) * u + 8 * sum(count(x) for x in range(hf))

        def groups_of(hf):
            out, n = [], 0
            for i in range(2 * NB):
                tiles = list(range(NB * hf + i % NB + 2))
                here = []
                for c in range(0, len(tiles), 4):
                    here.append((tiles[c:c + 4], 3 + n % 2, n // 2))
                    n += 1
                out.append(here)
            return out

        def bank_groups(hf, b):
            return sum(g[1] == b for here in groups_of(hf) for g in here)

        def keys_of(hf, b):
            return META + HALF * hf + P * (b + 1)

        def rows_of(hf, b, tile):
            return P if tile < NB * hf + b + 1 else META

        def cols(b):
            return slice(P * b, P * b + P)

        @block.sync
        def _(sp):
            sp.dma_start(C[:], a["consts"]).then_inc(sem["c_in"], 16)
            sp.dma_start(y1, a["cross"]).then_inc(sem["c_in"], 16)
            sp.dma_start(PV[:], a["pvec"]).then_inc(sem["c_in"], 16)
            sp.dma_start(XM[:], a["xm"]).then_inc(sem["c_in"], 16)
            with sp.Fori(0, HG) as h:
                sp.wait_ge(sem["m_F"], h)
                sp.dma_start(wF, a["whg"][h, 0]).then_inc(sem["wF_in"], 16)
                sp.wait_ge(sem["m_I"], h)
                sp.dma_start(wI, a["whg"][h, 3]).then_inc(sem["wI_in"], 16)
            sp.wait_ge(sem["m_F"], HG)
            sp.wait_ge(sem["m_I"], HG)

            def first_head(hf):
                sp.dma_start(XT, a["xt"][hf]).then_inc(sem["xt_in"], 16)
                for n, (name, w) in enumerate((("F", wF), ("G", wG), ("Q", wQ), ("I", wI))):
                    sp.dma_start(w, a["whg"][0, n]).then_inc(sem[f"w{name}_in"], 16)

            for hf in range(NH):
                if hf == 0:
                    first_head(0)
                with sp.Fori(1, HG) as h:
                    for n, (name, w) in enumerate((("F", wF), ("G", wG), ("Q", wQ), ("I", wI))):
                        sp.wait_ge(sem[name], h + HG * hf)
                        sp.dma_start(w, a["whg"][h, (0, 1, 2, 3)[n]]).then_inc(sem[f"w{name}_in"], 16)
                if hf == 0:
                    sp.wait_ge(sem["m_dve"], 5)
                sp.dma_start(wc, a["wc"]).then_inc(sem["wc_in"], 16)
                end_stage(sp, 6 * hf)
                sp.dma_start(wuq, a["wuq"][0]).then_inc(sem["wuq_in"], 16)
                sp.dma_start(wukv, a["wukv"][0]).then_inc(sem["wukv_in"], 16)
                end_stage(sp, 6 * hf + 1)
                n7, n6 = bank_jobs(hf, 7), bank_jobs(hf, 6)
                with sp.Fori(1, 8) as u:
                    sp.wait_ge(sem["j7"], before(lambda x: bank_jobs(x, 7), hf, u))
                    apart(sp)
                    sp.wait_ge(sem["j6"], before(lambda x: bank_jobs(x, 6), hf, u))
                    sp.dma_start(wuq, a["wuq"][u]).then_inc(sem["wuq_in"], 16)
                    sp.dma_start(wukv, a["wukv"][u]).then_inc(sem["wukv_in"], 16)
                end_stage(sp, 6 * hf + 2)
                with sp.Fori(0, KD) as n:
                    for name, w, k0, k1 in (("ga", wga, 24, 32), ("gb", wgb, 32, 40), ("ya", wa, 0, 8),
                                            ("yb", wb, 8, 24)):
                        sp.wait_ge(sem["p" + name], n + KD * hf)
                        apart(sp)
                        sp.dma_start(w, a["wmix"][n, :, k0:k1, :]).then_inc(
                            sem[{"ga": "wga_in", "gb": "wgb_in", "ya": "wa_in", "yb": "wb_in"}[name]], 16)
                sp.dma_start(LN1, a["ln1"]).then_inc(sem["ln_in"], 16)
                if hf:
                    sp.dma_start(LN2, a["ln2"]).then_inc(sem["q_in"], 16)
                end_stage(sp, 6 * hf + 3)
                for j in range(2):
                    sp.dma_start(WO[j], a["wout"][j]).then_inc(sem[f"wo{j}_in"], 16)
                sp.dma_start(XK, a["xk"][hf]).then_inc(sem["xk_in"], 16)
                if hf:
                    sp.wait_ge(sem["qd"], 4 * NB * hf)
                    sp.dma_start(a["out"][hf - 1], ACC).then_inc(sem["out_done"], 16)
                end_stage(sp, 6 * hf + 4)
                for j in range(2):
                    sp.dma_start(wpq[j], a["wpq"][0, j]).then_inc(sem[f"wpq{j}_in"], 16)
                sp.dma_start(wsk, a["wsk"][0]).then_inc(sem["wsk_in"], 16)
                if hf < NH - 1:
                    first_head(hf + 1)
                with sp.Fori(1, PH) as h:
                    for j in range(2):
                        sp.wait_ge(sem[f"pq{j}"], h + PH * hf)
                        sp.dma_start(wpq[j], a["wpq"][h, j]).then_inc(sem[f"wpq{j}_in"], 16)
                    sp.wait_ge(sem["ps"], 2 * h + 2 * PH * hf)
                    sp.dma_start(wsk, a["wsk"][h]).then_inc(sem["wsk_in"], 16)
                end_stage(sp, 6 * hf + 5)
            sp.dma_start(LN2, a["ln2"]).then_inc(sem["q_in"], 16)
            end_stage(sp, 6 * NH)
            sp.wait_ge(sem["qd"], 4 * NB * NH)
            sp.dma_start(a["out"][NH - 1], ACC).then_inc(sem["out_done"], 16)
            sp.wait_ge(sem["out_done"], 16 * NH)

        @block.tensor
        def _(pe):
            def mm(out, lhsT, rhs, start, stop):
                return pe.matmul(out, lhsT, rhs, start=start, stop=stop, skip_group_check=True)

            def product(out, w, x, n=KD):
                for kt in range(n):
                    last = mm(out, w(kt), x(kt), kt == 0, kt == n - 1)
                return last

            pe.wait_ge(sem["c_in"], 64)
            with pe.Fori(0, HG) as h:
                pe.wait_ge(sem["wF_in"], 16 * h + 16)
                product(PS[:, bass.ds(h * META, META)], lambda kt: wF[:, kt, :], lambda kt: XM[:, kt, :]
                        ).then_inc(sem["m_F"], 1)
                pe.wait_ge(sem["wI_in"], 16 * h + 16)
                product(PS[0:META, bass.ds(h * P + 512, P)], lambda kt: XM[:, kt, :], lambda kt: wI[:, kt, :]
                        ).then_inc(sem["m_I"], 1)
            pe.wait_ge(sem["m_pool"], 2)
            for h in range(HG):
                last = pe.transpose(PS[0:META, 1536 + P * h:1536 + P * h + P], mks[:, META * h:META * h + META],
                                    ident)
            last.then_inc(sem["m_pe"], 1)
            pe.wait_ge(sem["m_act"], 3)
            pe.wait_ge(sem["m_act"], 2)
            for h in range(HG):
                last = mm(PS[:, 2560 + P * h:2560 + P * h + P], mksT[0:META, cols(h)], miT[0:META, cols(h)],
                          True, True)
            last.then_inc(sem["m_pe"], 1)
            pe.wait_ge(sem["m_dve"], 5)

            for hf in range(NH):
                def project(g, name):
                    w = {"F": wF, "G": wG, "Q": wQ, "I": wI}[name]
                    b = {"F": 0, "G": 1, "Q": 2, "I": 3}[name]
                    used = {"F": "sig", "G": "t2", "Q": "qd16", "I": "isb"}[name]
                    extra = 16 * HG if name in "FI" else 0
                    pe.wait_ge(sem[f"w{name}_in"], g * 16 + (16 + extra))
                    pe.wait_ge(sem[used], g)
                    for i in range(NB if name == "I" else 1):
                        for kt in range(KD):
                            if name == "I":
                                last = mm(bank(b)[:, cols(i)], XT[:, kt, cols(i)], w[:, kt, :], kt == 0, kt == KD - 1)
                            else:
                                last = mm(bank(b), w[:, kt, :], XT[:, kt, :], kt == 0, kt == KD - 1)
                            if kt == KD - 1 and i == (NB if name == "I" else 1) - 1:
                                last.then_inc(sem[name], 1)
                            yield

                def all_of(steps):
                    for _ in steps:
                        pass

                def head(g, following):
                    pe.wait_ge(sem["ks32"], g + 1)
                    pe.wait_ge(sem["st"], g * NPAIR)
                    for b in range(NB):
                        last = pe.transpose(bank(5)[:, cols(b)], ks32[:, cols(b)], ident)
                    last.then_inc(sem["T"], 1)
                    pe.wait_ge(sem["ki"], g + 1)
                    pe.wait_ge(sem["qd16"], g + 1)
                    pe.wait_ge(sem["std"], g)
                    for b in range(NB):
                        last = mm(bank(4)[:, cols(b)], ki[:, cols(b)], qd16[:, cols(b)], True, True)
                    last.then_inc(sem["M1"], 1)
                    pe.wait_ge(sem["ksT"], g + 1)
                    for b in range(NB):
                        last = mm(bank(5)[:, cols(b)], ks16[:, cols(b)], qd16[:, cols(b)], True, True)
                    last.then_inc(sem["M2"], 1)
                    pe.wait_ge(sem["sc"], g + 1)
                    pe.wait_ge(sem["isb"], g + 1)
                    pe.wait_ge(sem["y1"], g)
                    for b in range(NB):
                        mm(bank(6)[:, cols(b)], isb[:, cols(b)], sc[:, cols(b)], b == 0, True)
                    more = iter(())
                    if following:
                        def both():
                            yield from project(g + 1, "F")
                            yield from project(g + 1, "G")
                        more = both()
                    pe.wait_ge(sem["qd32"], g + 1)
                    for p in range(NPAIR):
                        if p >= 2:
                            pe.wait_ge(sem["st"], g * NPAIR + (p - 1))
                        r = 32 * (p % 4)
                        c = P * (p // 4)
                        u = bank(7 if p % 2 == 0 else 5)[:, 0:P]
                        mm(u, ksT[r:r + 32, c:c + P], isb[r:r + 32, c:c + P], True, True).then_inc(sem["St"], 1)
                        next(more, None)
                        next(more, None)
                        if p == 0:
                            pe.wait_ge(sem["S0"], g + 1)
                        else:
                            pe.wait_ge(sem["st"], g * NPAIR + p)
                        mm(bank(6)[:, 32 * p:32 * p + 32], Spp[p % 2], qd32[:, 32 * p:32 * p + 32], False,
                           True).then_inc(sem["inter"], 1)
                    all_of(more)
                    if following:
                        all_of(project(g + 1, "Q"))
                    pe.wait_ge(sem["sq"], g + 1)
                    mm(bank(4), ones, sqh, True, True).then_inc(sem["ms"], 1)
                    if following:
                        all_of(project(g + 1, "I"))

                pe.wait_ge(sem["xt_in"], 16 * hf + 16)
                for name in "FGQI":
                    all_of(project(HG * hf, name))
                with pe.Fori(0, HG - 1) as h:
                    head(h + HG * hf, True)
                head(HG * hf + HG - 1, False)
                end_stage(pe, 6 * hf)

                pe.wait_ge(sem["wc_in"], 16 * hf + 16)
                for j in range(7):
                    product(bank(j), lambda kt: wc[:, kt, j, :], lambda kt: XT[:, kt, :]).then_inc(sem["cj"], 1)
                pe.wait_ge(sem["csq"], 5 * hf + 3)
                product(bank(7), lambda i: ones, lambda i: csq[:, i, :], QT).then_inc(sem["mq"], 1)
                pe.wait_ge(sem["csq"], 5 * hf + 5)
                pe.wait_ge(sem["stdq"], hf + 1)
                product(bank(7), lambda i: ones, lambda i: csq[:, QT + i, :], KVT).then_inc(sem["mkv"], 1)
                if hf == 0:
                    pe.wait_ge(sem["stdkv"], 1)
                    for j in range(4):
                        last = product(bank(7)[:, META * j:META * j + META], lambda kt: wc[:, kt, QT + j, :],
                                       lambda kt: XM[:, kt, :])
                    last.then_inc(sem["m_pe"], 1)
                    pe.wait_ge(sem["m_act"], 4)
                    pe.wait_ge(sem["cn"], QT)
                    product(bank(0)[:, 0:META], lambda i: ones, lambda i: mcsq[:, i, :], KVT
                            ).then_inc(sem["m_pe"], 1)
                end_stage(pe, 6 * hf + 1)

                groups = groups_of(hf)

                def pair(u):
                    G = u + 8 * hf
                    pe.wait_ge(sem["wuq_in"], G * 16 + 16)
                    pe.wait_ge(sem["wukv_in"], G * 16 + 16)
                    for what, arg, b, n in jobs_of(hf):
                        pe.wait_ge(sem[f"e{b}"], before(lambda x: bank_jobs(x, b), hf, u) + n)
                        if what in ("qrA", "qrB", "qn"):
                            j = {"qrA": 2, "qrB": 3}.get(what, arg)
                            last = product(bank(b), lambda i: wuq[:, i, j, :], lambda i: cqn[:, i, :], QT)
                        elif what == "kn":
                            e, c, n_ = arg
                            last = product(wide(b)[:, 0:n_], lambda i: wukv[:, i, e, :],
                                           lambda i: ckvn[:, i, c:c + n_], KVT)
                        else:
                            j, many = arg
                            for t in range(many):
                                r = P if many == 2 else META
                                c = P * (j + t)
                                for i in range(KVT):
                                    last = mm(wide(b)[0:r, 256 * t:256 * t + 256], ckvn[:, i, c:c + r],
                                              wukv[:, i, 2:4, :], i == 0, i == KVT - 1)
                        last.then_inc(sem[f"j{b}"], 1)
                    for b in (6, 7):
                        pe.wait_ge(sem[f"e{b}"], before(lambda x: bank_jobs(x, b), hf, u) + bank_jobs(hf, b))

                    def scores(i):
                        e, b = divmod(i, NB)
                        nk = keys_of(hf, b)
                        pe.wait_ge(sem["exp"], G * 2 * NB + i)
                        for c in range(0, nk, 512):
                            n = min(512, nk - c)
                            mm(PS[:, c:c + n], qn[e][:, cols(b)], kn[e][:, c:c + n], True, False)
                            last = mm(PS[:, c:c + n], qr[ROPE * e:ROPE * e + ROPE, cols(b)],
                                      krT[ROPE * e:ROPE * e + ROPE, c:c + n], False, True)
                        last.then_inc(sem["Sm"], 1)

                    def turn(i, group):
                        tiles, bk, n = group
                        pe.wait_ge(sem[f"pe{bk}"], before(lambda x: bank_groups(x, bk), hf, u) + n)
                        for s, t in enumerate(tiles):
                            r = rows_of(hf, i % NB, t)
                            last = pe.transpose(wide(bk)[0:r, cols(s)], PR[i % 2][:, P * t:P * t + r], ident)
                        last.then_inc(sem[f"pt{bk}"], 1)

                    def values(i, group):
                        e, b = divmod(i, NB)
                        tiles, bk, n = group
                        pe.wait_ge(sem[f"pe{bk}"], before(lambda x: bank_groups(x, bk), hf, u) + (n + 1))
                        for s, t in enumerate(tiles):
                            r = rows_of(hf, b, t)
                            last = mm(bank(5)[:, cols(b)], V[0:r, t, cols(e)], PTs[bk - 3][0:r, cols(s)],
                                      t == 0, r < P)
                        last.then_inc(sem[f"pv{bk}"], 1)

                    def output(i):
                        pe.wait_ge(sem["pn"], G * 2 * NB + (i + 1))
                        if i % NB == 0:
                            pe.wait_ge(sem["OE"], G * 2 + i // NB)
                        for n, group in enumerate(groups[i]):
                            turn(i, group)
                            if n:
                                values(i, groups[i][n - 1])
                        values(i, groups[i][-1])

                    scores(0)
                    for i in range(1, 2 * NB):
                        scores(i)
                        output(i - 1)
                    output(2 * NB - 1)

                with pe.Fori(0, 8) as u:
                    pair(u)
                end_stage(pe, 6 * hf + 2)

                with pe.Fori(0, KD) as n:
                    N = n + KD * hf
                    for name, wname, w, x, kn_, b, used in (
                            ("pga", "wga_in", wga, XT, KD, 2, "sga"), ("pgb", "wgb_in", wgb, XT, KD, 3, "sgb"),
                            ("pya", "wa_in", wa, YH, HG, 0, "m1"), ("pyb", "wb_in", wb, YM, MH, 1, "m2")):
                        pe.wait_ge(sem[wname], N * 16 + 16)
                        pe.wait_ge(sem[used], N)
                        product(bank(b), lambda kt: w[:, kt, :], lambda kt: x[:, kt, :], kn_).then_inc(sem[name], 1)
                end_stage(pe, 6 * hf + 3)

                for j in range(2):
                    pe.wait_ge(sem[f"wo{j}_in"], 16 * hf + 16)
                    for b in range(NB):
                        product(wide(2 * b + j), lambda kt: MIX[:, kt, cols(b)],
                                lambda kt: WO[j][:, kt, :]).then_inc(sem["wo"], 1)
                for b in range(NB):
                    pe.wait_ge(sem["n8"], NB * hf + b + 1)
                    for kt in range(KD):
                        last = pe.transpose(PS[:, 1024 * b + P * kt:1024 * b + P * kt + P],
                                            HB[:, b, P * kt:P * kt + P], ident)
                    last.then_inc(sem["hT"], 1)
                end_stage(pe, 6 * hf + 4)

                with pe.Fori(0, PH) as h:
                    H = h + PH * hf
                    for j in range(2):
                        pe.wait_ge(sem[f"wpq{j}_in"], H * 16 + 16)
                        pe.wait_ge(sem["pqe"], H * 2 + j)
                        product(bank(j), lambda kt: wpq[j][:, kt, :], lambda kt: HT[:, kt, :]
                                ).then_inc(sem[f"pq{j}"], 1)
                    pe.wait_ge(sem["wsk_in"], H * 16 + 16)
                    for j in range(2):
                        pe.wait_ge(sem["pqe"], H * 2 + (j + 1))
                        pe.wait_ge(sem["pse"], H * 2 + j)
                        for b in range(NB):
                            last = mm(bank(2 + j)[:, cols(b)], qT[j][:, cols(b)], wsk[:, j, :], True, True)
                        last.then_inc(sem["ps"], 1)
                end_stage(pe, 6 * hf + 5)
            end_stage(pe, 6 * NH)

        @block.scalar
        def _(act):
            def run(out, in_, func, done, **kw):
                return act.activation(out, in_, func, **kw).then_inc(sem[done], 1)

            def tanh(R, p):
                act.wait_ge(sem["g_z"], R * 2 * STEPS + (2 * p + 2))
                run(gt_[:, NB * p:NB * p + NB], gz_[:, NB * p:NB * p + NB], ACT.Tanh, "g_th", scale=GELU_B)

            def weigh(R, p):
                act.wait_ge(sem["g_w"], R * 2 * STEPS + (2 * p + 2))
                v = ROW[NB * p + 1][:, D:2 * D]
                run(v, v, ACT.Copy, "g_v", scale=gw_[:, NB * p + 1:NB * p + 2])

            def norm2(c):
                for b in range(NB):
                    n = NB * c + b
                    act.wait_ge(sem["q1"], 3 * n)
                    act.wait_ge(sem["accv"], (c + 1) * NSEL)
                    act.wait_ge(sem["accp"], (c + 1) * NSEL)
                    run(junk, ACC[:, b, :], ACT.Copy, "q1", accum_out=st2[:, 8 * b:8 * b + 1])
                    act.wait_ge(sem["q2"], n + 1)
                    act.wait_ge(sem["q1"], 3 * n + 1)
                    run(junk, ACC[:, b, :], ACT.Square, "q1", bias=st2[:, 8 * b + 1:8 * b + 2],
                        accum_out=st2[:, 8 * b + 2:8 * b + 3])
                    act.wait_ge(sem["q1"], 3 * n + 2)
                    run(st2[:, 8 * b + 3:8 * b + 4], st2[:, 8 * b + 2:8 * b + 3], ACT.Sqrt, "q1", scale=1.0 / D,
                        bias=EPSC)

            act.wait_ge(sem["lb_ready"], 3)
            run(small[:, 24:40], small[:, 24:40], ACT.Exp, "lb_ready")
            act.wait_ge(sem["m_F"], HG)
            run(msg, PS[:, 0:P], ACT.Sigmoid, "m_act")
            act.wait_ge(sem["m_I"], HG)
            run(miT[0:META, :], PS[0:META, 512:512 + HG * P], ACT.Copy, "m_act")
            act.wait_ge(sem["m_pe"], 1)
            run(mksT[0:META, :], PS[0:META, 1536:1536 + HG * P], ACT.Copy, "m_act")

            for hf in range(NH):
                def forget(g):
                    act.wait_ge(sem["F"], g + 1)
                    act.wait_ge(sem["f"], g * 2)
                    run(sg, bank(0), ACT.Sigmoid, "sig")

                def gate(g):
                    act.wait_ge(sem["G"], g + 1)
                    act.wait_ge(sem["t2"], g)
                    run(sg2, bank(1), ACT.Sigmoid, "sigG")

                def inputs(g):
                    act.wait_ge(sem["I"], g + 1)
                    act.wait_ge(sem["inter"], g * NPAIR)
                    run(isb, bank(3), ACT.Copy, "isb")

                def head(g, h, following):
                    R = h + ROUNDS * (hf - 1)
                    if hf:
                        tanh(R, 0)
                    if following:
                        forget(g + 1)
                    if hf:
                        tanh(R, 1)
                        weigh(R, 0)
                        tanh(R, 2)
                        weigh(R, 1)
                    if following:
                        gate(g + 1)
                    act.wait_ge(sem["inter"], g * NPAIR + NPAIR)
                    act.wait_ge(sem["ms"], g)
                    run(sqh, bank(6), ACT.Square, "sq")
                    act.wait_ge(sem["ms"], g + 1)
                    act.wait_ge(sem["rs"], g)
                    run(std, bank(4), ACT.Sqrt, "std", scale=1.0 / P, bias=EPSC)
                    if hf:
                        tanh(R, 3)
                        weigh(R, 2)
                    if following:
                        inputs(g + 1)
                    if hf:
                        weigh(R, 3)

                forget(HG * hf)
                gate(HG * hf)
                inputs(HG * hf)
                with act.Fori(0, HG - 1) as h:
                    head(h + HG * hf, h, True)
                head(HG * hf + HG - 1, HG - 1, False)
                end_stage(act, 6 * hf)

                for i in range(QT + KVT):
                    act.wait_ge(sem["cj"], 7 * hf + i + 1)
                    run(csq[:, i, :], bank(i), ACT.Square, "csq")
                    if hf:
                        if i < STEPS:
                            tanh(ROUNDS * (hf - 1) + R_LATENT, i)
                        if i:
                            weigh(ROUNDS * (hf - 1) + R_LATENT, i - 1)
                act.wait_ge(sem["mq"], hf + 1)
                run(cstd, bank(7), ACT.Sqrt, "stdq", scale=1.0 / (QT * P), bias=EPSC)
                act.wait_ge(sem["mkv"], hf + 1)
                act.wait_ge(sem["rsq"], hf + 1)
                run(cstd, bank(7), ACT.Sqrt, "stdkv", scale=1.0 / (KVT * P), bias=EPSC)
                if hf == 0:
                    act.wait_ge(sem["m_pe"], 3)
                    run(mcsq.rearrange("p a b -> p (a b)"), bank(7)[:, 0:KVT * META], ACT.Square, "m_act")
                    act.wait_ge(sem["m_pe"], 4)
                    run(mstd, bank(0)[:, 0:META], ACT.Sqrt, "m_act", scale=1.0 / (KVT * P), bias=EPSC)
                else:
                    for p in range(STEPS):
                        tanh(ROUNDS * (hf - 1) + R_LATENT + 1, p)
                        if p:
                            weigh(ROUNDS * (hf - 1) + R_LATENT + 1, p - 1)
                    weigh(ROUNDS * (hf - 1) + R_LATENT + 1, STEPS - 1)
                end_stage(act, 6 * hf + 1)

                groups = groups_of(hf)
                with act.Fori(0, 8) as u:
                    G = u + 8 * hf
                    for what, arg, b, n in jobs_of(hf):
                        if b == 7:
                            continue
                        act.wait_ge(sem["j6"], before(lambda x: bank_jobs(x, 6), hf, u) + (n + 1))
                        if what == "qn":
                            run(qn[arg], bank(6), ACT.Copy, "e6")
                        elif what == "kn":
                            e, c, n_ = arg
                            run(kn[e][:, c:c + n_], wide(6)[:, 0:n_], ACT.Copy, "e6")
                        else:
                            j, many = arg
                            r = P if many == 2 else META
                            run(V[0:r, j:j + many, :], wide(6)[0:r, 0:256 * many], ACT.Copy, "e6")
                        if hf and n < STEPS:
                            tanh(u * 2 + (ROUNDS * (hf - 1) + R_ATTEND), n)
                            if n:
                                weigh(u * 2 + (ROUNDS * (hf - 1) + R_ATTEND), n - 1)
                    if hf:
                        weigh(u * 2 + (ROUNDS * (hf - 1) + R_ATTEND), STEPS - 1)

                    def copy_turned(i, some):
                        for tiles, bk, n in groups[i][some]:
                            if bk == 3:
                                act.wait_ge(sem["pt3"], before(lambda x: bank_groups(x, 3), hf, u) + (n + 1))
                                act.wait_ge(sem["pv3"], before(lambda x: bank_groups(x, 3), hf, u) + n)
                                full = [t for t in tiles if rows_of(hf, i % NB, t) == P]
                                if full:
                                    one = act.activation(PTs[0][:, 0:P * len(full)], wide(3)[:, 0:P * len(full)],
                                                         ACT.Copy)
                                if len(full) < len(tiles):
                                    s = len(full)
                                    one = act.activation(PTs[0][0:META, cols(s)], wide(3)[0:META, cols(s)], ACT.Copy)
                                one.then_inc(sem["pe3"], 1)
                        if i % NB == NB - 1 and some.stop is None:
                            bk, n = groups[i][-1][1:]
                            act.wait_ge(sem[f"pv{bk}"], before(lambda x: bank_groups(x, bk), hf, u) + (n + 1))
                            run(YM[:, bass.ds(u * 2 + i // NB, 1), :], bank(5), ACT.Copy, "OE")

                    for i in range(2 * NB):
                        nk = keys_of(hf, i % NB)
                        if i:
                            copy_turned(i - 1, slice(0, 1))
                        act.wait_ge(sem["ngm"], G * 2 * NB + (i + 1))
                        run(PR[i % 2][:, 0:nk], PS[:, 0:nk], ACT.Exp, "exp", scale=SCALE,
                            bias=smx[:, 2 + i % 2:3 + i % 2], accum_out=smx[:, 4 + i % 2:5 + i % 2])
                        if i:
                            copy_turned(i - 1, slice(1, None))
                        if hf:
                            if i:
                                weigh(u * 2 + (ROUNDS * (hf - 1) + R_ATTEND + 1), i - 1)
                            tanh(u * 2 + (ROUNDS * (hf - 1) + R_ATTEND + 1), i)
                    copy_turned(2 * NB - 1, slice(0, None))
                    if hf:
                        weigh(u * 2 + (ROUNDS * (hf - 1) + R_ATTEND + 1), STEPS - 1)
                end_stage(act, 6 * hf + 2)

                with act.Fori(0, 2) as m:
                    for n in range(KD // 2):
                        N = m * (KD // 2) + (n + KD * hf)
                        act.wait_ge(sem["pga"], N + 1)
                        act.wait_ge(sem["m1"], N)
                        run(sga, bank(2), ACT.Sigmoid, "sga")
                        act.wait_ge(sem["pgb"], N + 1)
                        act.wait_ge(sem["m2"], N)
                        run(sgb, bank(3), ACT.Sigmoid, "sgb")
                        for j in range(2 * n, 2 * n + 2) if hf else ():
                            R, p = m * (MIX_ROUNDS // 2) + (ROUNDS * (hf - 1) + R_MIX + j // STEPS), j % STEPS
                            tanh(R, p)
                            if p:
                                weigh(R, p - 1)
                            if p == STEPS - 1:
                                weigh(R, p)
                end_stage(act, 6 * hf + 3)

                if hf:
                    for j in range(ROUNDS * (hf - 1) + R_NORM, ROUNDS * hf):
                        for p in range(STEPS):
                            tanh(j, p)
                            if p:
                                weigh(j, p - 1)
                        weigh(j, STEPS - 1)
                for b in range(NB):
                    n = NB * hf + b
                    act.wait_ge(sem["n2"], n + 1)
                    act.wait_ge(sem["n3"], n)
                    run(junk, R1[b % 2], ACT.Square, "n3", bias=st1[:, 8 * b + 2:8 * b + 3],
                        accum_out=st1[:, 8 * b + 3:8 * b + 4])
                    act.wait_ge(sem["n3"], n + 1)
                    run(st1[:, 8 * b + 4:8 * b + 5], st1[:, 8 * b + 3:8 * b + 4], ACT.Sqrt, "n4", scale=1.0 / D,
                        bias=EPSC)
                    act.wait_ge(sem["hT"], n + 1)
                    for j in range(2):
                        run(HT[:, 4 * j:4 * j + 4, cols(b)],
                            wide(2 * b + j).rearrange("p (x y) -> p x y", x=4), ACT.Copy, "hTe")
                if hf:
                    norm2(hf - 1)
                end_stage(act, 6 * hf + 4)

                def queries_and_scores(H):
                    for j in range(2):
                        act.wait_ge(sem[f"pq{j}"], H + 1)
                        act.wait_ge(sem["ps"], H * 2 + j)
                        run(qT[j], bank(j), ACT.Copy, "pqe")
                    for j in range(2):
                        act.wait_ge(sem["ps"], H * 2 + (j + 1))
                        act.wait_ge(sem["t2nd"], H * 2)
                        run(SS[:, j, :, :], bank(2 + j), ACT.Copy, "pse")

                def softmax(H):
                    act.wait_ge(sem["gmx"], H + 1)
                    act.wait_ge(sem["dvc"], H * DVC)
                    run(ge, gd, ACT.Exp, "gex")

                queries_and_scores(PH * hf)
                with act.Fori(0, PH - 1) as h:
                    queries_and_scores(h + (PH * hf + 1))
                    softmax(h + PH * hf)
                if hf:
                    act.wait_ge(sem["out_done"], 16 * hf)
                for b in range(NB):
                    run(ACC[:, b, :], HB[:, b, :], ACT.Copy, "acc0", scale=ALPHA)
                softmax(PH * hf + PH - 1)
                end_stage(act, 6 * hf + 5)

            with act.Fori(0, ROUNDS) as q:
                for p in range(STEPS):
                    tanh(q + ROUNDS * (NH - 1), p)
                    if p:
                        weigh(q + ROUNDS * (NH - 1), p - 1)
                weigh(q + ROUNDS * (NH - 1), STEPS - 1)
            end_stage(act, 6 * NH)
            norm2(NH - 1)

        @block.vector
        def _(dve):
            tt, ts, stt = dve.tensor_tensor, dve.tensor_scalar, dve.scalar_tensor_tensor

            def experts(R, first):
                def weight(p):
                    K = R * STEPS + p
                    mine = slice(NB * p, NB * p + NB)
                    dve.wait_ge(sem["g_th"], K + 1)
                    stt(gu_[:, mine], gt_[:, mine], 1.0, ga_[:, mine], ALU.add, ALU.mult).then_inc(sem["g_w"], 1)
                    yield
                    dve.wait_ge(sem["g_w"], K * 2 + 1)
                    k = first + p
                    stt(gw_[:, mine].unsqueeze(2), gu_[:, mine].unsqueeze(2), 0.5, GATE[:, :, bass.ds(k, 1)],
                        ALU.mult, ALU.mult).then_inc(sem["g_w"], 1)
                    yield
                    dve.wait_ge(sem["g_w"], K * 2 + 2)
                    dve.wait_ge(sem["accv"], K)
                    stt(ACC[:, 0, :], ROW[NB * p][:, D:2 * D], gw_[:, NB * p:NB * p + 1], ACC[:, 0, :],
                        ALU.mult, ALU.add).then_inc(sem["accv"], 1)
                for p in range(STEPS):
                    K = R * STEPS + p
                    mine = slice(NB * p, NB * p + NB)
                    before_ = weight(p - 1) if p else iter(())
                    for b in range(NB):
                        s = NB * p + b
                        dve.wait_ge(got[s], R * 16 + 16)
                        dve.tensor_tensor_reduce(ROW[s][:, 0:D], ROW[s][:, 0:D], HB[:, b, :], 1.0, 0.0, ALU.mult,
                                                 ALU.add, ga_[:, s:s + 1]).then_inc(sem["g_dot"], 1)
                        next(before_, None)
                        yield
                    dve.wait_ge(sem["g_dot"], K * NB + NB)
                    stt(gx_[:, mine], ga_[:, mine], GELU_A, ga_[:, mine], ALU.mult, ALU.mult
                        ).then_inc(sem["g_z"], 1)
                    next(before_, None)
                    dve.wait_ge(sem["g_z"], K * 2 + 1)
                    stt(gz_[:, mine], gx_[:, mine], 1.0, ga_[:, mine], ALU.add, ALU.mult).then_inc(sem["g_z"], 1)
                    yield
                for _ in weight(STEPS - 1):
                    pass

            def norm2(c):
                dve.wait_ge(sem["q_in"], 16 * (c + 1))
                for b in range(NB):
                    n = NB * c + b
                    dve.wait_ge(sem["q1"], 3 * n + 1)
                    ts(st2[:, 8 * b + 1:8 * b + 2], st2[:, 8 * b:8 * b + 1], -1.0 / D, None, ALU.mult
                       ).then_inc(sem["q2"], 1)
                    dve.wait_ge(sem["q1"], 3 * n + 3)
                    dve.reciprocal(st2[:, 8 * b + 4:8 * b + 5], st2[:, 8 * b + 3:8 * b + 4]).then_inc(sem["qd"], 1)
                    dve.wait_ge(sem["qd"], 4 * n + 1)
                    ts(ACC[:, b, :], ACC[:, b, :], st2[:, 8 * b + 1:8 * b + 2], st2[:, 8 * b + 4:8 * b + 5], ALU.add,
                       ALU.mult).then_inc(sem["qd"], 1)
                    dve.wait_ge(sem["qd"], 4 * n + 2)
                    tt(ACC[:, b, :], ACC[:, b, :], LN2[:, 0, :], ALU.mult).then_inc(sem["qd"], 1)
                    dve.wait_ge(sem["qd"], 4 * n + 3)
                    tt(ACC[:, b, :], ACC[:, b, :], LN2[:, 1, :], ALU.add).then_inc(sem["qd"], 1)

            def all_of(steps):
                for _ in steps:
                    pass

            NOTSTART, END = C[:, C_NS:C_NS + HALF], C[:, C_END:C_END + HALF]
            dve.memset(EPSC, EPS).then_inc(sem["start"], 1)
            dve.memset(mfm[:, P:P + 1], 0.0).then_inc(sem["start"], 1)
            dve.memset(fm[:, HALF:HALF + 1], 0.0).then_inc(sem["start"], 1)
            dve.wait_ge(sem["start"], 3)
            dve.wait_ge(sem["c_in"], 64)
            dve.tensor_copy(MB[:], y1).then_inc(sem["start"], 1)
            dve.wait_ge(sem["start"], 4)
            tt(small[:, 40:48], PV[:, 0:8], PV[:, 8:16], ALU.max).then_inc(sem["lb_ready"], 1)
            dve.wait_ge(sem["lb_ready"], 1)
            for j in range(2):
                tt(small[:, 24 + 8 * j:32 + 8 * j], PV[:, 8 * j:8 * j + 8], small[:, 40:48], ALU.subtract
                   ).then_inc(sem["lb_ready"], 1)
            dve.wait_ge(sem["lb_ready"], 4)
            tt(small[:, 48:56], small[:, 24:32], small[:, 32:40], ALU.add).then_inc(sem["lb_ready"], 1)
            dve.wait_ge(sem["lb_ready"], 5)
            dve.reciprocal(small[:, 48:56], small[:, 48:56]).then_inc(sem["lb_ready"], 1)
            dve.wait_ge(sem["lb_ready"], 6)
            tt(LB, small[:, 24:32], small[:, 48:56], ALU.mult).then_inc(sem["lb_ready"], 1)
            dve.wait_ge(sem["lb_ready"], 7)
            ts(OML, LB, -1.0, 1.0, ALU.mult, ALU.add).then_inc(sem["lb_ready"], 1)
            dve.wait_ge(sem["lb_ready"], 8)
            dve.wait_ge(sem["m_act"], 1)
            by_head = lambda x: x.rearrange("p (h t) -> p h t", h=HG)
            tt(by_head(mf), by_head(msg), OML.unsqueeze(2).to_broadcast([P, HG, META]), ALU.mult
               ).then_inc(sem["m_dve"], 1)
            dve.wait_ge(sem["m_dve"], 1)
            tt(by_head(mf), by_head(mf), LB.unsqueeze(2).to_broadcast([P, HG, META]), ALU.add
               ).then_inc(sem["m_dve"], 1)
            dve.wait_ge(sem["m_dve"], 2)
            tt(mfm[:, 0:P], mf, NOTSTART[:, 0:P], ALU.mult).then_inc(sem["m_dve"], 1)
            dve.wait_ge(sem["m_dve"], 3)
            dve.tensor_tensor_scan(mest[:, ::-1], mfm[:, P:0:-1], END[:, P - 1::-1], 0.0, ALU.mult, ALU.add
                                   ).then_inc(sem["m_dve"], 1)
            dve.wait_ge(sem["m_pe"], 2)
            dve.tensor_copy(S_all[:], PS[:, 2560:2560 + HG * P]).then_inc(sem["m_dve"], 1)

            for hf in range(NH):
                def chain(g):
                    dve.wait_ge(sem["sig"], g + 1)
                    dve.wait_ge(sem["k"], g)
                    dve.wait_ge(sem["ebi"], g)
                    dve.wait_ge(sem["est"], g)
                    dve.wait_ge(sem["qd16"], g)
                    ts(f, sg, fcol[:, 1:2], fcol[:, 0:1], ALU.mult, ALU.add).then_inc(sem["f"], 2)
                    yield
                    dve.wait_ge(sem["f"], g * 2 + 2)
                    tt(fm[:, 0:HALF], f, NOTSTART, ALU.mult).then_inc(sem["fm"], 1)
                    yield
                    dve.wait_ge(sem["fm"], g + 1)
                    dve.wait_ge(sem["ks16"], g)
                    dve.tensor_tensor_scan(est[:, ::-1], fm[:, HALF:0:-1], END[:, ::-1], 0.0, ALU.mult, ALU.add
                                           ).then_inc(sem["est"], 1)
                    tt(fs, f, fm[:, 0:HALF], ALU.subtract).then_inc(sem["fs"], 1)
                    yield
                    dve.wait_ge(sem["fs"], g + 1)
                    dve.wait_ge(sem["D"], g)
                    dve.wait_ge(sem["qd32"], g)
                    dve.tensor_tensor_scan(eb, fm[:, 0:HALF], fs, 0.0, ALU.mult, ALU.add).then_inc(sem["eb"], 1)
                    yield
                    dve.wait_ge(sem["eb"], g + 1)
                    dve.wait_ge(sem["ki"], g)
                    dve.reciprocal(ebi, eb).then_inc(sem["ebi"], 1)

                def queries(g):
                    dve.wait_ge(sem["Q"], g + 1)
                    dve.wait_ge(sem["M2"], g)
                    dve.wait_ge(sem["qd32"], g)
                    tt(qd16, bank(2), eb, ALU.mult).then_inc(sem["qd16"], 1)

                def gate(g):
                    dve.wait_ge(sem["sigG"], g + 1)
                    dve.wait_ge(sem["y"], g)
                    tt(t2, bank(1), sg2, ALU.mult).then_inc(sem["t2"], 1)

                def columns(g, h):
                    dve.wait_ge(sem["f"], g * 2)
                    apart(dve)
                    dve.tensor_copy(fcol[:, 0:1], LB[:, bass.ds(h, 1)]).then_inc(sem["fcol"], 1)
                    dve.tensor_copy(fcol[:, 1:2], OML[:, bass.ds(h, 1)]).then_inc(sem["fcol"], 1)
                    dve.wait_ge(sem["fcol"], g * 2 + 2)

                def head(g, h, following):
                    dve.wait_ge(sem["T"], g + 1)
                    dve.wait_ge(sem["inter"], g * NPAIR)
                    dve.tensor_copy(ksT, bank(5)).then_inc(sem["ksT"], 1)
                    dve.wait_ge(sem["M1"], g + 1)
                    dve.wait_ge(sem["inter"], g * NPAIR)
                    tt(sc, bank(4), C[:, C_MA:C_MA + HALF], ALU.mult).then_inc(sem["sA"], 1)
                    dve.wait_ge(sem["y1"], g)
                    apart(dve)
                    dve.tensor_copy(fcol[:, 2:3], PV[:, bass.ds(h + 16, 1)]).then_inc(sem["gcol"], 1)
                    dve.tensor_copy(Spp[0], S_all[:, bass.ds(h, 1), :]).then_inc(sem["S0"], 1)
                    dve.wait_ge(sem["M2"], g + 1)
                    dve.wait_ge(sem["sA"], g + 1)
                    apart(dve)
                    dve.copy_predicated(sc, MB[:], bank(5)).then_inc(sem["sc"], 1)
                    dve.wait_ge(sem["D"], g + 1)
                    dve.wait_ge(sem["S0"], g + 1)
                    ex = experts(h + ROUNDS * (hf - 1), h * STEPS) if hf else iter(())
                    following_gates = iter(())
                    for p in range(NPAIR):
                        dve.wait_ge(sem["St"], g * NPAIR + (p + 1))
                        dve.wait_ge(sem["inter"], g * NPAIR + p)
                        if p:
                            dve.wait_ge(sem["st"], g * NPAIR + p)
                        stt(Spp[(p + 1) % 2], Spp[p % 2], Dp[:, p:p + 1], bank(7 if p % 2 == 0 else 5)[:, 0:P],
                            ALU.mult, ALU.add).then_inc(sem["st"], 1)
                        next(ex, None)
                        if p % 2:
                            next(ex, None)
                        if p == 5 and following:
                            columns(g + 1, h + 1)
                            following_gates = chain(g + 1)
                        if p >= 5:
                            next(following_gates, None)
                    dve.wait_ge(sem["st"], g * NPAIR + NPAIR)
                    apart(dve)
                    dve.tensor_copy(S_all[:, bass.ds(h, 1), :], Spp[0]).then_inc(sem["Sb"], 1)
                    all_of(following_gates)
                    if following:
                        queries(g + 1)
                    dve.wait_ge(sem["std"], g + 1)
                    dve.wait_ge(sem["y"], g)
                    dve.reciprocal(rs, std).then_inc(sem["rs"], 1)
                    dve.wait_ge(sem["rs"], g + 1)
                    stt(y1, bank(6), fcol[:, 2:3], rs, ALU.mult, ALU.mult).then_inc(sem["y1"], 1)
                    dve.wait_ge(sem["y1"], g + 1)
                    tt(YH[:, bass.ds(h, 1), :], y1.unsqueeze(1), t2.unsqueeze(1), ALU.mult).then_inc(sem["y"], 1)
                    if following:
                        gate(g + 1)
                    all_of(ex)
                    dve.wait_ge(sem["Sb"], g + 1)
                    apart(dve)

                columns(HG * hf, 0)
                all_of(chain(HG * hf))
                gate(HG * hf)
                queries(HG * hf)
                with dve.Fori(0, HG - 1) as h:
                    head(h + HG * hf, h, True)
                head(HG * hf + HG - 1, HG - 1, False)
                end_stage(dve, 6 * hf)

                t0 = META + HALF * hf
                ex = iter(())
                if hf:
                    all_of(experts(ROUNDS * (hf - 1) + R_LATENT, R_LATENT * STEPS))
                    ex = experts(ROUNDS * (hf - 1) + R_LATENT + 1, (R_LATENT + 1) * STEPS)
                dve.wait_ge(sem["stdq"], hf + 1)
                dve.reciprocal(crs, cstd).then_inc(sem["rsq"], 1)
                dve.wait_ge(sem["rsq"], hf + 1)
                for i in range(QT):
                    stt(cqn[:, i, :], bank(i), PV[:, 24 + i:25 + i], crs, ALU.mult, ALU.mult).then_inc(sem["cn"], 1)
                next(ex, None)
                next(ex, None)
                dve.wait_ge(sem["stdkv"], hf + 1)
                dve.wait_ge(sem["cn"], QT * hf + QT)
                dve.reciprocal(crs, cstd).then_inc(sem["rskv"], 1)
                dve.wait_ge(sem["rskv"], hf + 1)
                for i in range(KVT):
                    stt(ckvn[:, i, t0:t0 + HALF], bank(QT + i), PV[:, 27 + i:28 + i], crs, ALU.mult, ALU.mult
                        ).then_inc(sem["ckn"], 1)
                dve.wait_ge(sem["cj"], 7 * hf + 7)
                tt(kta, bank(5), C[:, C_COS + t0:C_COS + t0 + HALF], ALU.mult).then_inc(sem["krA"], 1)
                tt(ktb, bank(6), C[:, C_SIN + t0:C_SIN + t0 + HALF], ALU.mult).then_inc(sem["krB"], 1)
                dve.wait_ge(sem["krA"], hf + 1)
                dve.wait_ge(sem["krB"], hf + 1)
                tt(krT[:, t0:t0 + HALF], kta, ktb, ALU.add).then_inc(sem["kr"], 1)
                if hf == 0:
                    dve.wait_ge(sem["m_act"], 5)
                    dve.reciprocal(mrs, mstd).then_inc(sem["m_dve"], 1)
                    dve.wait_ge(sem["m_dve"], 6)
                    for i in range(KVT):
                        stt(ckvn[:, i, 0:META], bank(7)[:, META * i:META * i + META], PV[:, 27 + i:28 + i], mrs,
                            ALU.mult, ALU.mult).then_inc(sem["m_dve"], 1)
                    tt(mka, bank(7)[:, 2 * META:3 * META], C[:, C_COS:C_COS + META], ALU.mult
                       ).then_inc(sem["m_dve"], 1)
                    tt(mkb, bank(7)[:, 3 * META:4 * META], C[:, C_SIN:C_SIN + META], ALU.mult
                       ).then_inc(sem["m_dve"], 1)
                    dve.wait_ge(sem["m_dve"], 10)
                    tt(krT[:, 0:META], mka, mkb, ALU.add).then_inc(sem["m_dve"], 1)
                all_of(ex)
                end_stage(dve, 6 * hf + 1)

                groups = groups_of(hf)
                with dve.Fori(0, 8) as u:
                    G = u + 8 * hf
                    for what, arg, b, n in jobs_of(hf):
                        if b == 6:
                            continue
                        if n == 0 and hf:
                            ex = experts(u * 2 + (ROUNDS * (hf - 1) + R_ATTEND), u * (2 * STEPS) + R_ATTEND * STEPS)
                        dve.wait_ge(sem["j7"], before(lambda x: bank_jobs(x, 7), hf, u) + (n + 1))
                        if what == "qrA":
                            dve.wait_ge(sem["e7"], before(lambda x: bank_jobs(x, 7), hf, u))
                            tt(qra, bank(7), C[:, C_COS + t0:C_COS + t0 + HALF], ALU.mult).then_inc(sem["e7"], 1)
                        elif what == "qrB":
                            tt(qrb, bank(7), C[:, C_SIN + t0:C_SIN + t0 + HALF], ALU.mult).then_inc(sem["qrb"], 1)
                            dve.wait_ge(sem["qrb"], G + 1)
                            tt(qr, qra, qrb, ALU.add).then_inc(sem["e7"], 1)
                        elif what == "kn":
                            e, c, n_ = arg
                            dve.tensor_copy(kn[e][:, c:c + n_], wide(7)[:, 0:n_]).then_inc(sem["e7"], 1)
                        else:
                            j, many = arg
                            r = P if many == 2 else META
                            dve.tensor_copy(V[0:r, j:j + many, :], wide(7)[0:r, 0:256 * many]).then_inc(sem["e7"], 1)
                        if hf and n < STEPS:
                            for _ in range(3):
                                next(ex)
                    if hf:
                        all_of(ex)
                        ex = experts(u * 2 + (ROUNDS * (hf - 1) + R_ATTEND + 1), u * (2 * STEPS) + (R_ATTEND + 1) * STEPS)

                    def copy_turned(i):
                        for tiles, bk, n in groups[i]:
                            if bk == 4:
                                dve.wait_ge(sem["pt4"], before(lambda x: bank_groups(x, 4), hf, u) + (n + 1))
                                dve.wait_ge(sem["pv4"], before(lambda x: bank_groups(x, 4), hf, u) + n)
                                full = [t for t in tiles if rows_of(hf, i % NB, t) == P]
                                if full:
                                    one = dve.tensor_copy(PTs[1][:, 0:P * len(full)], wide(4)[:, 0:P * len(full)])
                                if len(full) < len(tiles):
                                    s = len(full)
                                    one = dve.tensor_copy(PTs[1][0:META, cols(s)], wide(4)[0:META, cols(s)])
                                one.then_inc(sem["pe4"], 1)

                    for i in range(2 * NB):
                        nk = keys_of(hf, i % NB)
                        dve.wait_ge(sem["Sm"], G * 2 * NB + (i + 1))
                        tt(PS[:, nk - P:nk], PS[:, nk - P:nk], C[:, C_CAUS:C_CAUS + P], ALU.add
                           ).then_inc(sem["cau"], 1)
                        dve.wait_ge(sem["cau"], G * 2 * NB + (i + 1))
                        dve.wait_ge(sem["ngm"], G * 2 * NB + i)
                        dve.reduce_max(smx[:, i % 2:i % 2 + 1], PS[:, 0:nk], AX).then_inc(sem["mx"], 1)
                        dve.wait_ge(sem["mx"], G * 2 * NB + (i + 1))
                        ts(smx[:, 2 + i % 2:3 + i % 2], smx[:, i % 2:i % 2 + 1], -SCALE, None, ALU.mult
                           ).then_inc(sem["ngm"], 1)
                        if i:
                            copy_turned(i - 1)
                        if hf:
                            next(ex)
                        dve.wait_ge(sem["exp"], G * 2 * NB + (i + 1))
                        dve.wait_ge(sem["pn"], G * 2 * NB + max(i - 1, 0))
                        dve.reciprocal(smx[:, 6 + i % 2:7 + i % 2], smx[:, 4 + i % 2:5 + i % 2]
                                       ).then_inc(sem["rcp"], 1)
                        if hf:
                            for _ in range(2):
                                next(ex)
                    copy_turned(2 * NB - 1)
                    if hf:
                        all_of(ex)
                end_stage(dve, 6 * hf + 2)

                with dve.Fori(0, 2) as m:
                    def rounds():
                        for j in range(MIX_ROUNDS // 2):
                            yield from experts(m * (MIX_ROUNDS // 2) + (ROUNDS * (hf - 1) + R_MIX + j),
                                               m * (MIX_ROUNDS // 2 * STEPS) + (R_MIX + j) * STEPS)

                    ex = rounds() if hf else iter(())
                    for n in range(KD // 2):
                        N = m * (KD // 2) + (n + KD * hf)
                        for _ in range(3):
                            next(ex, None)
                        dve.wait_ge(sem["pya"], N + 1)
                        dve.wait_ge(sem["sga"], N + 1)
                        dve.wait_ge(sem["mix"], N)
                        tt(mm1, bank(0), sga, ALU.mult).then_inc(sem["m1"], 1)
                        dve.wait_ge(sem["pyb"], N + 1)
                        dve.wait_ge(sem["sgb"], N + 1)
                        tt(mm2, bank(1), sgb, ALU.mult).then_inc(sem["m2"], 1)
                        dve.wait_ge(sem["m2"], N + 1)
                        tt(MIX[:, bass.ds(m * (KD // 2) + n, 1), :], mm1.unsqueeze(1), mm2.unsqueeze(1), ALU.add
                           ).then_inc(sem["mix"], 1)
                        for _ in range(3):
                            next(ex, None)
                    all_of(ex)
                end_stage(dve, 6 * hf + 3)

                if hf:
                    for j in range(R_NORM, ROUNDS):
                        all_of(experts(ROUNDS * (hf - 1) + j, j * STEPS))
                dve.wait_ge(sem["xk_in"], 16 * hf + 16)
                dve.wait_ge(sem["ln_in"], 16 * hf + 16)
                for b in range(NB):
                    n = NB * hf + b
                    c0 = 8 * b
                    dve.wait_ge(sem["wo"], 2 * NB * hf + NB + b + 1)
                    if n >= 2:
                        dve.wait_ge(sem["n8"], n - 1)
                    for j in range(2):
                        stt(R1[b % 2][:, 512 * j:512 * j + 512], XK[:, b, 512 * j:512 * j + 512], ALPHA,
                            wide(2 * b + j), ALU.mult, ALU.add, accum_out=st1[:, c0 + j:c0 + j + 1]
                            ).then_inc(sem["r"], 1)
                    dve.wait_ge(sem["r"], 2 * n + 2)
                    tt(st1[:, c0 + 2:c0 + 3], st1[:, c0:c0 + 1], st1[:, c0 + 1:c0 + 2], ALU.add
                       ).then_inc(sem["nd"], 1)
                    dve.wait_ge(sem["nd"], 4 * n + 1)
                    ts(st1[:, c0 + 2:c0 + 3], st1[:, c0 + 2:c0 + 3], -1.0 / D, None, ALU.mult
                       ).then_inc(sem["n2"], 1)
                    dve.wait_ge(sem["n4"], n + 1)
                    dve.reciprocal(st1[:, c0 + 5:c0 + 6], st1[:, c0 + 4:c0 + 5]).then_inc(sem["nd"], 1)
                    dve.wait_ge(sem["nd"], 4 * n + 2)
                    ts(R1[b % 2], R1[b % 2], st1[:, c0 + 2:c0 + 3], st1[:, c0 + 5:c0 + 6], ALU.add, ALU.mult
                       ).then_inc(sem["nd"], 1)
                    dve.wait_ge(sem["nd"], 4 * n + 3)
                    tt(R1[b % 2], R1[b % 2], LN1[:, 0, :], ALU.mult).then_inc(sem["nd"], 1)
                    dve.wait_ge(sem["nd"], 4 * n + 4)
                    tt(HB[:, b, :], R1[b % 2], LN1[:, 1, :], ALU.add).then_inc(sem["n8"], 1)
                if hf:
                    norm2(hf - 1)
                end_stage(dve, 6 * hf + 4)

                big = -3e38

                def wave(op, n, k, name, base):
                    for s in range(n):
                        op(s).then_inc(sem[name], 1)
                    dve.wait_ge(sem[name], base + n * k)
                    apart(dve)

                def sides(H):
                    B1 = H * 10 * NB
                    dve.wait_ge(sem["pse"], H * 2 + 2)
                    dve.wait_ge(sem["t2nd"], H * 2)
                    apart(dve)
                    S = lambda s: SS[:, s // NB, s % NB, :]
                    S2 = lambda s: SS2[:, s // NB, s % NB, :]
                    tV = lambda s: tv[:, s // NB, s % NB, :]
                    tI = lambda s: ti[:, s // NB, s % NB, :]
                    wave(lambda s: dve.max(tV(s)[:, 0:8], S(s)), 2 * NB, 1, "dv", B1)
                    wave(lambda s: dve.max_index(tI(s)[:, 0:8], tV(s)[:, 0:8], S(s)), 2 * NB, 2, "dv", B1)
                    wave(lambda s: dve.match_replace(S2(s), tV(s)[:, 0:8], S(s), big), 2 * NB, 3, "dv", B1)
                    wave(lambda s: dve.max(tV(s)[:, 8:16], S2(s)), 2 * NB, 4, "dv", B1)
                    wave(lambda s: dve.max_index(tI(s)[:, 8:16], tV(s)[:, 8:16], S2(s)), 2 * NB, 5, "dv", B1)

                def best(H):
                    dve.tensor_copy(tif[:, :, 0, :], ti[:, 0, :, :]).then_inc(sem["t2nd"], 1)
                    dve.tensor_copy(tif[:, :, 1, :], ti[:, 1, :, :]).then_inc(sem["t2nd"], 1)
                    B2 = H * 6 * NB
                    wave(lambda b: tt(CA[:, b, :].rearrange("p (x y) -> p x y", x=TOP),
                                      tv[:, 0, b, :].unsqueeze(2).to_broadcast([P, TOP, TOP]),
                                      tv[:, 1, b, :].unsqueeze(1).to_broadcast([P, TOP, TOP]), ALU.add),
                         NB, 1, "dvb", B2)
                    dve.wait_ge(sem["gmx"], H)
                    apart(dve)
                    wave(lambda b: dve.max(bv[:, b, 0:8], CA[:, b, :]), NB, 2, "dvb", B2)
                    wave(lambda b: dve.max_index(bs[:, b, 0:8], bv[:, b, 0:8], CA[:, b, :]), NB, 3, "dvb", B2)
                    wave(lambda b: dve.match_replace(CA2[:, b, :], bv[:, b, 0:8], CA[:, b, :], big),
                         NB, 4, "dvb", B2)
                    wave(lambda b: dve.max(bv[:, b, 8:16], CA2[:, b, :]), NB, 5, "dvb", B2)
                    wave(lambda b: dve.max_index(bs[:, b, 8:16], bv[:, b, 8:16], CA2[:, b, :]), NB, 6, "dvb", B2)
                    dve.wait_ge(sem["gex"], H)
                    tt(gd, bv, bv[:, :, 0:1].to_broadcast([P, NB, TOP]), ALU.subtract).then_inc(sem["gmx"], 1)
                    ts(bs2[:, :, :, 0], bs, 4, None, ALU.logical_shift_right).then_inc(sem["dvc"], 1)
                    ts(bs2[:, :, :, 1], bs, 15, None, ALU.bitwise_and).then_inc(sem["dvc"], 1)
                    dve.wait_ge(sem["dvc"], H * DVC + 2)
                    dve.tensor_copy(bsf, bs2).then_inc(sem["dvc"], 1)
                    dve.wait_ge(sem["dvc"], H * DVC + 3)
                    tt(OH.rearrange("p (n r) -> p n r", r=TOP),
                       bsf.rearrange("p b j z -> p (b j z)").unsqueeze(2).to_broadcast([P, NB * TOP * 2, TOP]),
                       C[:, C_IOTA:C_IOTA + TOP].unsqueeze(1).to_broadcast([P, NB * TOP * 2, TOP]), ALU.is_equal
                       ).then_inc(sem["dvc"], 1)

                def numbers(H, h):
                    dve.wait_ge(sem["onehot"], H * NB + NB)
                    dve.wait_ge(sem["dvc"], H * DVC + 4)
                    dve.tensor_reduce(osum.rearrange("p b j z -> p (b j z)"),
                                      OH2.rearrange("p (n r) -> p n r", r=TOP), AX, ALU.add).then_inc(sem["dvc"], 1)
                    dve.wait_ge(sem["dvc"], H * DVC + 5)
                    stt(eif, osum[:, :, :, 0], 128.0, osum[:, :, :, 1], ALU.mult, ALU.add).then_inc(sem["dvc"], 1)
                    dve.wait_ge(sem["dvc"], H * DVC + 6)
                    apart(dve)
                    dve.tensor_copy(EIDX[:, :, bass.ds(h * TOP, TOP)], eif).then_inc(sem["dvc"], 1)
                    dve.wait_ge(sem["gex"], H + 1)
                    dve.tensor_reduce(gs, ge, AX, ALU.add).then_inc(sem["dvc"], 1)
                    dve.wait_ge(sem["dvc"], H * DVC + 8)
                    dve.reciprocal(gr, gs).then_inc(sem["dvc"], 1)
                    dve.wait_ge(sem["dvc"], H * DVC + 9)
                    tt(GATE[:, :, bass.ds(h * TOP, TOP)], ge, gr.unsqueeze(2).to_broadcast([P, NB, TOP]), ALU.mult
                       ).then_inc(sem["dvc"], 1)

                sides(PH * hf)
                best(PH * hf)
                with dve.Fori(0, PH - 1) as h:
                    sides(h + (PH * hf + 1))
                    numbers(h + PH * hf, h)
                    best(h + (PH * hf + 1))
                numbers(PH * hf + PH - 1, PH - 1)
                end_stage(dve, 6 * hf + 5)

            with dve.Fori(0, ROUNDS) as q:
                all_of(experts(q + ROUNDS * (NH - 1), q * STEPS))
            end_stage(dve, 6 * NH)
            norm2(NH - 1)

        @block.gpsimd
        def _(pool):
            tt, ts = pool.tensor_tensor, pool.tensor_scalar
            def gather(R, first, p):
                K = R * STEPS + p
                if not (isinstance(R, int) and R == 0):
                    pool.wait_ge(sem["accv"], (R - 1) * STEPS + (p + 1))
                    pool.wait_ge(sem["accp"], (R - 1) * STEPS + (p + 1))
                    apart(pool)
                pool.tensor_copy(IDX[p].unsqueeze(2), EIDX[:, :, bass.ds(first + p, 1)]).then_inc(sem["gidx"], 1)
                pool.wait_ge(sem["gidx"], K + 1)
                apart(pool)
                for b in range(NB):
                    pool.indirect_dma_start(ROW[NB * p + b], None, a["uv"], bass.IndirectOffsetOnAxis(
                        ap=IDX[p][:, b:b + 1], axis=0)).then_inc(got[NB * p + b], 16)

            def first_round(c):
                pool.wait_ge(stage_done, 4 * (6 * c + 5) + 4)
                for p in range(STEPS):
                    gather(ROUNDS * c, 0, p)

            def experts(R, first, p, more=True):
                K = R * STEPS + p
                pool.wait_ge(sem["g_v"], K + 1)
                pool.wait_ge(sem["accp"], K)
                tt(ACC[:, 1, :], ACC[:, 1, :], ROW[NB * p + 1][:, D:2 * D], ALU.add).then_inc(sem["accp"], 1)
                if more:
                    gather(R + 1, first + STEPS, p)

            halves = lambda x: x.rearrange("p (n z t) -> p n z t", z=2, t=CHUNK)
            pool.wait_ge(sem["m_dve"], 2)
            ts(mk, mf, -1.0, 1.0, ALU.mult, ALU.add).then_inc(sem["m_pool"], 1)
            pool.wait_ge(sem["m_pool"], 1)
            pool.wait_ge(sem["m_dve"], 4)
            tt(mks, mk, mest, ALU.mult).then_inc(sem["m_pool"], 1)
            for hf in range(NH):
                if hf:
                    first_round(hf - 1)
                def keys(g):
                    pool.wait_ge(sem["f"], g * 2 + 2)
                    pool.wait_ge(sem["ks16"], g)
                    pool.wait_ge(sem["ki"], g)
                    apart(pool)
                    ts(k, f, -1.0, 1.0, ALU.mult, ALU.add).then_inc(sem["k"], 1)
                    pool.wait_ge(sem["k"], g + 1)
                    pool.wait_ge(sem["est"], g + 1)
                    pool.wait_ge(sem["M2"], g)
                    tt(ks16, k, est, ALU.mult).then_inc(sem["ks16"], 1)
                    pool.wait_ge(sem["eb"], g + 1)
                    pool.wait_ge(sem["ks16"], g + 1)
                    pool.wait_ge(sem["T"], g)
                    tt(halves(ks32)[:, :, 0, :], halves(ks16)[:, :, 0, :],
                       ends[:, :, 1, :].to_broadcast([P, NPAIR, CHUNK]), ALU.mult).then_inc(sem["ks32a"], 1)
                    pool.tensor_copy(halves(ks32)[:, :, 1, :], halves(ks16)[:, :, 1, :]).then_inc(sem["ks32"], 1)
                    pool.wait_ge(sem["ebi"], g + 1)
                    pool.wait_ge(sem["M1"], g)
                    tt(ki, k, ebi, ALU.mult).then_inc(sem["ki"], 1)

                def queries(g):
                    pool.wait_ge(sem["eb"], g + 1)
                    pool.wait_ge(sem["st"], g * NPAIR)
                    tt(Dp.unsqueeze(2), ends[:, :, 0, :], ends[:, :, 1, :], ALU.mult).then_inc(sem["D"], 1)
                    pool.wait_ge(sem["qd16"], g + 1)
                    pool.wait_ge(sem["inter"], g * NPAIR)
                    tt(halves(qd32)[:, :, 1, :], halves(qd16)[:, :, 1, :],
                       ends[:, :, 0, :].to_broadcast([P, NPAIR, CHUNK]), ALU.mult).then_inc(sem["qd32a"], 1)
                    pool.tensor_copy(halves(qd32)[:, :, 0, :], halves(qd16)[:, :, 0, :]).then_inc(sem["qd32"], 1)

                def round_and_next(h, following):
                    for p in range(STEPS):
                        if hf:
                            experts(h + ROUNDS * (hf - 1), h * STEPS, p)
                        if following and p == 1:
                            keys(h + (HG * hf + 1))
                        if following and p == 2:
                            queries(h + (HG * hf + 1))

                ends = halves(eb)[:, :, :, CHUNK - 1:CHUNK]
                keys(HG * hf)
                queries(HG * hf)
                with pool.Fori(0, HG - 1) as h:
                    round_and_next(h, True)
                round_and_next(HG - 1, False)
                if hf:
                    for j in range(2 * STEPS):
                        experts(ROUNDS * (hf - 1) + R_LATENT + j // STEPS, (R_LATENT + j // STEPS) * STEPS, j % STEPS)
                with pool.Fori(0, 8) as u:
                    def step(j):
                        if hf:
                            experts(u * 2 + (ROUNDS * (hf - 1) + R_ATTEND + j // STEPS),
                                    u * (2 * STEPS) + (R_ATTEND + j // STEPS) * STEPS, j % STEPS)

                    for j in range(STEPS - 1):
                        step(j)
                    for i in range(2 * NB):
                        nk = keys_of(hf, i % NB)
                        pool.wait_ge(sem["rcp"], (u + 8 * hf) * 2 * NB + (i + 1))
                        apart(pool)
                        ts(PR[i % 2][:, 0:nk], PR[i % 2][:, 0:nk], smx[:, 6 + i % 2:7 + i % 2], 1.0, ALU.mult,
                           ALU.mult).then_inc(sem["pn"], 1)
                        step(STEPS - 1 + i)
                    step(2 * STEPS - 1)
                if hf:
                    with pool.Fori(0, MIX_ROUNDS) as n:
                        for p in range(STEPS):
                            experts(n + (ROUNDS * (hf - 1) + R_MIX), n * STEPS + R_MIX * STEPS, p)
                if hf:
                    for j in range(R_NORM, ROUNDS):
                        for p in range(STEPS):
                            experts(ROUNDS * (hf - 1) + j, j * STEPS, p, more=j < ROUNDS - 1)
                with pool.Fori(0, PH) as h:
                    H = h + PH * hf
                    oh = OH.rearrange("p (b j z r) -> p b j z r", b=NB, j=TOP, z=2)
                    oh2 = OH2.rearrange("p (b j z r) -> p b j z r", b=NB, j=TOP, z=2)
                    pool.wait_ge(sem["dvc"], H * DVC + 4)
                    pool.wait_ge(sem["t2nd"], H * 2 + 2)
                    for b in range(NB):
                        tt(oh2[:, b], oh[:, b], tif[:, b].unsqueeze(1).to_broadcast([P, TOP, 2, TOP]), ALU.mult
                           ).then_inc(sem["onehot"], 1)
            first_round(NH - 1)
            with pool.Fori(0, ROUNDS - 1) as q:
                for p in range(STEPS):
                    experts(q + ROUNDS * (NH - 1), q * STEPS, p)
            for p in range(STEPS):
                experts(ROUNDS * NH - 1, NSEL - STEPS, p, more=False)


def program(nc, a, out):
    build_program(nc, {**a, "out": out})


def kernel(**inputs):
    import concourse.bacc as bacc
    from concourse.bass_utils import run_bass_kernel_spmd

    x, w_in = inputs["x"][0], inputs["w_in"][0]
    w = {k: inputs[k][0] for k in ("w_uq", "w_ukv", "w_proj_hgrn", "w_proj_mla", "w_out", "peer_query",
                                   "peer_sub_keys", "peer_u", "peer_v")}

    def tiles(m):
        return m.reshape(-1, P, m.shape[1]).transpose(1, 0, 2)

    consts, cross = constants()
    q, f, i, g = (w_in[:, D * n:D * n + D] for n in range(4))
    whg = np.stack([tiles(m).reshape(P, KD, HG, P) for m in (f, g, q, i)])
    o = 4 * D
    cq, ckv, kr = w_in[:, o:o + 384], w_in[:, o + 384:o + 640], w_in[:, o + 640:o + 704]
    ga, gb = w_in[:, o + 704:o + 704 + D], w_in[:, o + 704 + D:]
    swap = np.concatenate([kr[:, 32:], kr[:, :32]], 1)
    wc = np.concatenate([cq, ckv, kr, kr, swap, swap], 1)
    uq = w["w_uq"].reshape(384, 8, 2, 192)
    ra, rb = uq[..., 128:], np.concatenate([uq[..., 160:], uq[..., 128:160]], -1)
    wuq = np.stack([uq[:, :, 0, :128], uq[:, :, 1, :128], ra.reshape(384, 8, 128), rb.reshape(384, 8, 128)], 2)
    ukv = w["w_ukv"].reshape(256, 8, 2, 2, 128).transpose(0, 1, 3, 2, 4).reshape(256, 8, 4, 128)
    mix = np.concatenate([tiles(m) for m in (w["w_proj_hgrn"], w["w_proj_mla"], ga, gb)], 1)
    feat = lambda v: v.reshape(-1, P).T
    pvec = np.concatenate([feat(inputs["hgrn_lb_logits"][0]), feat(inputs["hgrn_lb_logits"][1]),
                           feat(inputs["hgrn_norm_gain"][0]), feat(inputs["q_norm_gain"][0]),
                           feat(inputs["kv_norm_gain"][0])], 1)
    rows = lambda *v: np.stack([np.broadcast_to(z[0], (P, D)) for z in v], 1)
    arrays = {
        "consts": consts, "cross": cross, "pvec": pvec,
        "xm": tiles(inputs["meta_tokens"].T),
        "xt": x.T.reshape(KD, P, NH, HALF).transpose(2, 1, 0, 3),
        "xk": x.reshape(NH, NB, P, D).transpose(0, 2, 1, 3),
        "whg": whg.transpose(3, 0, 1, 2, 4),
        "wc": tiles(wc).reshape(P, KD, 7, P),
        "wuq": wuq.reshape(QT, P, 8, 4, 128).transpose(2, 1, 0, 3, 4),
        "wukv": ukv.reshape(KVT, P, 8, 4, 128).transpose(2, 1, 0, 3, 4),
        "wmix": mix.reshape(P, 40, KD, P).transpose(2, 0, 1, 3),
        "wout": tiles(w["w_out"]).reshape(P, KD, 2, D // 2).transpose(2, 0, 1, 3),
        "ln1": rows(inputs["ln1_gain"], inputs["ln1_bias"]),
        "ln2": rows(inputs["ln2_gain"], inputs["ln2_bias"]),
        "wpq": tiles(w["peer_query"]).reshape(P, KD, PH, 2, P).transpose(2, 3, 0, 1, 4),
        "wsk": w["peer_sub_keys"].transpose(0, 3, 1, 2),
        "uv": np.concatenate([w["peer_u"], w["peer_v"]], 1),
    }
    nc = bacc.Bacc("TRN2", target_bir_lowering=False, num_devices=1)
    arrays = {"in_" + k: np.ascontiguousarray(v) for k, v in arrays.items()}
    a = {k[3:]: nc.dram_tensor(k, v.shape, mybir.dt.from_np(v.dtype), kind="ExternalInput").ap()
         for k, v in arrays.items()}
    out = nc.dram_tensor("out_0", (NH, P, NB, D), F32, kind="ExternalOutput").ap()
    program(nc, a, out)
    r = run_bass_kernel_spmd(nc, [arrays], core_ids=[0])
    return r.results[0]["out_0"].transpose(0, 2, 1, 3).reshape(1, SEQ, D)
```

```python
from contextlib import ExitStack

import numpy as np

import concourse.bass as bass
from concourse import mybir

F32 = mybir.dt.float32
U32 = mybir.dt.uint32
U8 = mybir.dt.uint8
ALU = mybir.AluOpType
ACT = mybir.ActivationFunctionType
AX = mybir.AxisListType.X

P = 128
D = 1024
KD = D // P
SEQ = 1024
META = 16
TOK = 256
PARTS = SEQ // TOK
NB = TOK // P
NBLK = SEQ // P
KEYS = META + SEQ
CHUNK = 16
PAIR = 2 * CHUNK
NPAIR = TOK // PAIR
HG = 8
MH = 16
QT, KVT = 3, 2
ROPE = 64
SCALE = float((128 + ROPE) ** -0.5)
PH = 8
TOP = 16
NSEL = PH * TOP
ALPHA = float(2 ** 0.25)
EPS = 1e-5
NEG = -1e30
DVC = 10
STEPS = 4
ROUNDS = NSEL // STEPS
GSLOT = STEPS * NB
R_LATENT = HG
R_ATTEND = R_LATENT + 2
R_MIX = R_ATTEND + 16
MIX_ROUNDS = 4
R_NORM = R_MIX + MIX_ROUNDS
GELU_A, GELU_B = 0.044715, 0.7978845608028654

C_ID, C_ONE, C_MA, C_NS, C_END = 0, P, 2 * P, 2 * P + TOK, 2 * P + 2 * TOK
C_CAUS = C_END + TOK
C_IOTA = C_CAUS + P
C_COS = C_IOTA + 32
C_SIN = C_COS + KEYS
C_W = C_SIN + KEYS
ARENA_W = 42400


def constants():
    c = np.zeros((P, C_W), np.float32)
    t = np.arange(TOK)
    s = np.arange(P)
    c[:, C_ID:C_ID + P] = np.eye(P)
    c[:, C_ONE:C_ONE + P] = 1.0
    tl = t % P
    c[:, C_MA:C_MA + TOK] = (s[:, None] <= tl) & (s[:, None] // CHUNK == tl // CHUNK)
    c[:, C_NS:C_NS + TOK] = t % CHUNK != 0
    c[:, C_END:C_END + TOK] = t % CHUNK == CHUNK - 1
    c[:, C_CAUS:C_CAUS + P] = np.where(s[None, :] <= s[:, None], 0.0, NEG)
    c[:, C_IOTA:C_IOTA + 32] = np.arange(32) % 16
    inv = (np.float32(10000.0) ** (-np.arange(32, dtype=np.float32) / np.float32(32))).astype(np.float32)
    ang = np.arange(KEYS, dtype=np.float32)[None, :] * inv[:, None]
    c[:, C_COS:C_COS + KEYS] = np.tile(np.cos(ang), (4, 1))
    c[:, C_SIN:C_SIN + KEYS] = np.concatenate([-np.sin(ang), np.sin(ang)] * 2)
    cross = (s[:, None] // PAIR == tl // PAIR) & (s[:, None] // CHUNK % 2 == 0) & (tl // CHUNK % 2 == 1)
    return c, cross.astype(np.float32)


def build_program(nc, a):
    with ExitStack() as ctx:
        def sb(name, shape, dt=F32):
            return ctx.enter_context(nc.sbuf_tensor(name, shape, dt))

        names = []
        names += "c_in start apart lb_ready m_F m_I m_pe m_act m_dve m_pool".split()
        names += """xt_in wF_in wG_in wQ_in wI_in F G Q I fcol gcol sig sigG f fm fs eb est ebi
            k ki ks16 ks32a ks32 qd16 qd32a qd32 D T ksT M1 M2 sA sc isb St st S0 Sb
            inter sq ms std rs y1 y t2""".split()
        names += "wc_in cj csq mq mkv stdq stdkv rsq rskv cn ckn krA krB kr".split()
        names += """wuq_in wukv_in j6 j7 e6 e7 qrb Sm mx ngm exp rcp pn pt3 pt4 pe3 pe4 pv3 pv4
            OE""".split()
        names += "wga_in wgb_in wa_in wb_in pga pgb pya pyb sga sgb m1 m2 mix".split()
        names += "wo0_in wo1_in xk_in ln_in wo r n2 n3 n4 nd n8 hT hTe".split()
        names += "wpq0_in wpq1_in wsk_in pq0 pq1 pqe ps pse dv dvb t2nd gmx gex dvc onehot".split()
        names += "gidx g_dot g_z g_th g_w g_v accv accp acc0 q_in q1 q2 qd out_done".split()
        sem = {n: ctx.enter_context(nc.semaphore("s_" + n)) for n in names}
        got = [ctx.enter_context(nc.semaphore(f"s_got{i}")) for i in range(GSLOT)]
        stage_done = ctx.enter_context(nc.semaphore("s_stage_done"))

        def end_stage(eng, n):
            eng.drain().then_inc(stage_done, 1)
            eng.wait_ge(stage_done, 4 * n + 4)

        def apart(eng):
            eng.sem_inc(sem["apart"], 1)

        PS = ctx.enter_context(nc.psum_tensor("PS", [P, 8 * 512], F32))

        def bank(i):
            return PS[:, 512 * i:512 * i + TOK]

        def wide(i):
            return PS[:, 512 * i:512 * i + 512]

        C = sb("C", [P, C_W])
        MB = sb("MB", [P, TOK], U8)
        PV = sb("PV", [P, 29])
        small = sb("small", [P, 64])
        fcol = small[:, 56:59]
        LB, OML = small[:, 0:8], small[:, 8:16]
        EPSC = small[:, 16:17]
        S_all = sb("S_all", [P, HG, P])
        ckvn = sb("ckvn", [P, KVT, KEYS])
        krT = sb("krT", [P, KEYS])
        EIDX = sb("EIDX", [P, NB, NSEL], U32)
        GATE = sb("GATE", [P, NB, NSEL])
        XM = sb("XM", [P, KD, META])
        ident, ones = C[:, C_ID:C_ID + P], C[:, C_ONE:C_ONE + P]

        ARENA = sb("ARENA", [P, ARENA_W])
        top = [0]

        def at(off):
            top[0] = off

        def new(n):
            v = ARENA[:, top[0]:top[0] + n]
            top[0] += n
            assert top[0] <= ARENA_W
            return v

        def new3(x, y):
            return new(x * y).rearrange("p (x y) -> p x y", x=x)

        def new4(x, y, z):
            return new(x * y * z).rearrange("p (x y z) -> p x y z", x=x, y=y)

        at(0)
        ROW = [new(2 * D) for _ in range(GSLOT)]
        HB, ACC = new3(NB, D), new3(NB, D)
        IDX = [new(NB).bitcast(U32) for _ in range(STEPS)]
        ga_, gx_, gz_, gt_, gu_, gw_ = (new(GSLOT) for _ in range(6))
        st2 = new(16)
        BASE = top[0]
        XT = new3(KD, TOK)
        YH = new3(HG, TOK)
        YM = new3(MH, TOK)
        scratch = top[0]
        at(scratch - MH * TOK)
        wF, wG, wQ, wI = (new3(KD, P) for _ in range(4))
        (sg, sg2, f, fs, k, eb, est, ebi, qd16, ki, ks16, qd32, ks32, isb, ksT, sc, t2, y1, sqh, std,
         rs) = (new(TOK) for _ in range(21))
        fm = new(TOK + 1)
        Dp = new(NPAIR)
        Spp = [new(P) for _ in range(2)]
        msg, mf, mk, mest, mks = (new(P) for _ in range(5))
        mfm = new(P + 1)
        miT, mksT = new(HG * P), new(HG * P)
        at(scratch)
        cqn = new3(QT, TOK)
        wuq = new4(QT, 4, P)
        wukv = new4(KVT, 4, P)
        attend = top[0]
        csq = new3(QT + KVT, TOK)
        cstd, crs, kta, ktb = (new(TOK) for _ in range(4))
        mcsq = new3(KVT, META)
        mstd, mrs, mka, mkb = (new(META) for _ in range(4))
        assert top[0] <= ARENA_W - 7 * KD * P
        at(ARENA_W - 7 * KD * P)
        wc = new4(KD, 7, P)
        at(attend)
        qn = [new(TOK) for _ in range(2)]
        qr, qra, qrb = (new(TOK) for _ in range(3))
        kn = [new(KEYS) for _ in range(2)]
        V = new3(NBLK + 1, 2 * P)
        PR = [new(KEYS) for _ in range(2)]
        PTs = [new(512) for _ in range(2)]
        smx = new(64)
        at(scratch)
        MIX = new3(KD, TOK)
        wa, wga, wgb = (new3(KD, P) for _ in range(3))
        wb = new3(MH, P)
        sga, sgb, mm1, mm2 = (new(TOK) for _ in range(4))
        at(BASE)
        XK = new3(NB, D)
        HT = new3(KD, TOK)
        WO = [new3(KD, D // 2)]
        assert top[0] == scratch
        at(scratch + KD * TOK)
        WO.append(new3(KD, D // 2))
        R1 = [new(D) for _ in range(2)]
        junk = new(D)
        st1 = new(64)
        assert top[0] <= ARENA_W - 4 * D
        at(ARENA_W - 4 * D)
        LN1, LN2 = new3(2, D), new3(2, D)
        at(scratch)
        wpq = [new3(KD, P) for _ in range(2)]
        wsk = new3(2, P)
        qT = [new(TOK) for _ in range(2)]
        SS, SS2 = new4(2, NB, P), new4(2, NB, P)
        tv = new4(2, NB, TOP)
        ti = new(2 * NB * TOP).bitcast(U32).rearrange("p (x y z) -> p x y z", x=2, y=NB)
        tif = new4(NB, 2, TOP)
        CA, CA2 = new3(NB, TOP * TOP), new3(NB, TOP * TOP)
        bv = new3(NB, TOP)
        bs = new(NB * TOP).bitcast(U32).rearrange("p (x y) -> p x y", x=NB)
        bs2 = new(2 * NB * TOP).bitcast(U32).rearrange("p (x y z) -> p x y z", x=NB, y=TOP)
        bsf = new4(NB, TOP, 2)
        OH, OH2 = new(NB * TOP * 2 * TOP), new(NB * TOP * 2 * TOP)
        osum = new4(NB, TOP, 2)
        eif, ge, gd = (new3(NB, TOP) for _ in range(3))
        gs, gr = new(NB), new(NB)
        block = ctx.enter_context(nc.Block())

        def jobs_of(part):
            nfull = NB * (part + 1)
            out = [("qrA", None), ("qn", 0), ("qrB", None), ("qn", 1)]
            out += [("kn", (e, c, min(512, META + TOK * (part + 1) - c)))
                    for c in range(0, META + TOK * (part + 1), 512) for e in range(2)]
            out += [("v", (j, 2)) for j in range(0, nfull, 2)] + [("v", (nfull, 1))]
            return [(what, arg, 7 - i % 2, i // 2) for i, (what, arg) in enumerate(out)]

        def bank_jobs(part, b):
            return sum(j[2] == b for j in jobs_of(part))

        def before(count, part, u):
            return count(part) * u + 8 * sum(count(x) for x in range(part))

        def groups_of(part):
            out, n = [], 0
            for i in range(2 * NB):
                tiles = list(range(NB * part + i % NB + 2))
                here = []
                for c in range(0, len(tiles), 4):
                    here.append((tiles[c:c + 4], 3 + n % 2, n // 2))
                    n += 1
                out.append(here)
            return out

        def bank_groups(part, b):
            return sum(g[1] == b for here in groups_of(part) for g in here)

        def keys_of(part, b):
            return META + TOK * part + P * (b + 1)

        def rows_of(part, b, tile):
            return P if tile < NB * part + b + 1 else META

        def cols(b):
            return slice(P * b, P * b + P)

        @block.sync
        def _(sp):
            sp.dma_start(C[:], a["consts"]).then_inc(sem["c_in"], 16)
            sp.dma_start(y1, a["cross"]).then_inc(sem["c_in"], 16)
            sp.dma_start(PV[:], a["pvec"]).then_inc(sem["c_in"], 16)
            sp.dma_start(XM[:], a["xm"]).then_inc(sem["c_in"], 16)
            with sp.Fori(0, HG) as h:
                sp.wait_ge(sem["m_F"], h)
                sp.dma_start(wF, a["whg"][h, 0]).then_inc(sem["wF_in"], 16)
                sp.wait_ge(sem["m_I"], h)
                sp.dma_start(wI, a["whg"][h, 3]).then_inc(sem["wI_in"], 16)
            sp.wait_ge(sem["m_F"], HG)
            sp.wait_ge(sem["m_I"], HG)

            def first_head(part):
                sp.dma_start(XT, a["xt"][part]).then_inc(sem["xt_in"], 16)
                for n, (name, w) in enumerate((("F", wF), ("G", wG), ("Q", wQ), ("I", wI))):
                    sp.dma_start(w, a["whg"][0, n]).then_inc(sem[f"w{name}_in"], 16)

            for part in range(PARTS):
                if part == 0:
                    first_head(0)
                with sp.Fori(1, HG) as h:
                    for n, (name, w) in enumerate((("F", wF), ("G", wG), ("Q", wQ), ("I", wI))):
                        sp.wait_ge(sem[name], h + HG * part)
                        sp.dma_start(w, a["whg"][h, (0, 1, 2, 3)[n]]).then_inc(sem[f"w{name}_in"], 16)
                if part == 0:
                    sp.wait_ge(sem["m_dve"], 5)
                sp.dma_start(wc, a["wc"]).then_inc(sem["wc_in"], 16)
                end_stage(sp, 6 * part)
                sp.dma_start(wuq, a["wuq"][0]).then_inc(sem["wuq_in"], 16)
                sp.dma_start(wukv, a["wukv"][0]).then_inc(sem["wukv_in"], 16)
                end_stage(sp, 6 * part + 1)
                n7, n6 = bank_jobs(part, 7), bank_jobs(part, 6)
                with sp.Fori(1, 8) as u:
                    sp.wait_ge(sem["j7"], before(lambda x: bank_jobs(x, 7), part, u))
                    apart(sp)
                    sp.wait_ge(sem["j6"], before(lambda x: bank_jobs(x, 6), part, u))
                    sp.dma_start(wuq, a["wuq"][u]).then_inc(sem["wuq_in"], 16)
                    sp.dma_start(wukv, a["wukv"][u]).then_inc(sem["wukv_in"], 16)
                end_stage(sp, 6 * part + 2)
                with sp.Fori(0, KD) as n:
                    for name, w, k0, k1 in (("ga", wga, 24, 32), ("gb", wgb, 32, 40), ("ya", wa, 0, 8),
                                            ("yb", wb, 8, 24)):
                        sp.wait_ge(sem["p" + name], n + KD * part)
                        apart(sp)
                        sp.dma_start(w, a["wmix"][n, :, k0:k1, :]).then_inc(
                            sem[{"ga": "wga_in", "gb": "wgb_in", "ya": "wa_in", "yb": "wb_in"}[name]], 16)
                sp.dma_start(LN1, a["ln1"]).then_inc(sem["ln_in"], 16)
                if part:
                    sp.dma_start(LN2, a["ln2"]).then_inc(sem["q_in"], 16)
                end_stage(sp, 6 * part + 3)
                for j in range(2):
                    sp.dma_start(WO[j], a["wout"][j]).then_inc(sem[f"wo{j}_in"], 16)
                sp.dma_start(XK, a["xk"][part]).then_inc(sem["xk_in"], 16)
                if part:
                    sp.wait_ge(sem["qd"], 4 * NB * part)
                    sp.dma_start(a["out"][part - 1], ACC).then_inc(sem["out_done"], 16)
                end_stage(sp, 6 * part + 4)
                for j in range(2):
                    sp.dma_start(wpq[j], a["wpq"][0, j]).then_inc(sem[f"wpq{j}_in"], 16)
                sp.dma_start(wsk, a["wsk"][0]).then_inc(sem["wsk_in"], 16)
                if part < PARTS - 1:
                    first_head(part + 1)
                with sp.Fori(1, PH) as h:
                    for j in range(2):
                        sp.wait_ge(sem[f"pq{j}"], h + PH * part)
                        sp.dma_start(wpq[j], a["wpq"][h, j]).then_inc(sem[f"wpq{j}_in"], 16)
                    sp.wait_ge(sem["ps"], 2 * h + 2 * PH * part)
                    sp.dma_start(wsk, a["wsk"][h]).then_inc(sem["wsk_in"], 16)
                end_stage(sp, 6 * part + 5)
            sp.dma_start(LN2, a["ln2"]).then_inc(sem["q_in"], 16)
            end_stage(sp, 6 * PARTS)
            sp.wait_ge(sem["qd"], 4 * NB * PARTS)
            sp.dma_start(a["out"][PARTS - 1], ACC).then_inc(sem["out_done"], 16)
            sp.wait_ge(sem["out_done"], 16 * PARTS)

        @block.tensor
        def _(pe):
            def mm(out, lhsT, rhs, start, stop):
                return pe.matmul(out, lhsT, rhs, start=start, stop=stop, skip_group_check=True)

            def product(out, w, x, n=KD):
                for kt in range(n):
                    last = mm(out, w(kt), x(kt), kt == 0, kt == n - 1)
                return last

            pe.wait_ge(sem["c_in"], 64)
            with pe.Fori(0, HG) as h:
                pe.wait_ge(sem["wF_in"], 16 * h + 16)
                product(PS[:, bass.ds(h * META, META)], lambda kt: wF[:, kt, :], lambda kt: XM[:, kt, :]
                        ).then_inc(sem["m_F"], 1)
                pe.wait_ge(sem["wI_in"], 16 * h + 16)
                product(PS[0:META, bass.ds(h * P + 512, P)], lambda kt: XM[:, kt, :], lambda kt: wI[:, kt, :]
                        ).then_inc(sem["m_I"], 1)
            pe.wait_ge(sem["m_pool"], 2)
            for h in range(HG):
                last = pe.transpose(PS[0:META, 1536 + P * h:1536 + P * h + P], mks[:, META * h:META * h + META],
                                    ident)
            last.then_inc(sem["m_pe"], 1)
            pe.wait_ge(sem["m_act"], 3)
            pe.wait_ge(sem["m_act"], 2)
            for h in range(HG):
                last = mm(PS[:, 2560 + P * h:2560 + P * h + P], mksT[0:META, cols(h)], miT[0:META, cols(h)],
                          True, True)
            last.then_inc(sem["m_pe"], 1)
            pe.wait_ge(sem["m_dve"], 5)

            for part in range(PARTS):
                def project(g, name):
                    w = {"F": wF, "G": wG, "Q": wQ, "I": wI}[name]
                    b = {"F": 0, "G": 1, "Q": 2, "I": 3}[name]
                    used = {"F": "sig", "G": "t2", "Q": "qd16", "I": "isb"}[name]
                    extra = 16 * HG if name in "FI" else 0
                    pe.wait_ge(sem[f"w{name}_in"], g * 16 + (16 + extra))
                    pe.wait_ge(sem[used], g)
                    for i in range(NB if name == "I" else 1):
                        for kt in range(KD):
                            if name == "I":
                                last = mm(bank(b)[:, cols(i)], XT[:, kt, cols(i)], w[:, kt, :], kt == 0, kt == KD - 1)
                            else:
                                last = mm(bank(b), w[:, kt, :], XT[:, kt, :], kt == 0, kt == KD - 1)
                            if kt == KD - 1 and i == (NB if name == "I" else 1) - 1:
                                last.then_inc(sem[name], 1)
                            yield

                def all_of(steps):
                    for _ in steps:
                        pass

                def head(g, following):
                    pe.wait_ge(sem["ks32"], g + 1)
                    pe.wait_ge(sem["st"], g * NPAIR)
                    for b in range(NB):
                        last = pe.transpose(bank(5)[:, cols(b)], ks32[:, cols(b)], ident)
                    last.then_inc(sem["T"], 1)
                    pe.wait_ge(sem["ki"], g + 1)
                    pe.wait_ge(sem["qd16"], g + 1)
                    pe.wait_ge(sem["std"], g)
                    for b in range(NB):
                        last = mm(bank(4)[:, cols(b)], ki[:, cols(b)], qd16[:, cols(b)], True, True)
                    last.then_inc(sem["M1"], 1)
                    pe.wait_ge(sem["ksT"], g + 1)
                    for b in range(NB):
                        last = mm(bank(5)[:, cols(b)], ks16[:, cols(b)], qd16[:, cols(b)], True, True)
                    last.then_inc(sem["M2"], 1)
                    pe.wait_ge(sem["sc"], g + 1)
                    pe.wait_ge(sem["isb"], g + 1)
                    pe.wait_ge(sem["y1"], g)
                    for b in range(NB):
                        mm(bank(6)[:, cols(b)], isb[:, cols(b)], sc[:, cols(b)], b == 0, True)
                    more = iter(())
                    if following:
                        def both():
                            yield from project(g + 1, "F")
                            yield from project(g + 1, "G")
                        more = both()
                    pe.wait_ge(sem["qd32"], g + 1)
                    for p in range(NPAIR):
                        if p >= 2:
                            pe.wait_ge(sem["st"], g * NPAIR + (p - 1))
                        r = 32 * (p % 4)
                        c = P * (p // 4)
                        u = bank(7 if p % 2 == 0 else 5)[:, 0:P]
                        mm(u, ksT[r:r + 32, c:c + P], isb[r:r + 32, c:c + P], True, True).then_inc(sem["St"], 1)
                        next(more, None)
                        next(more, None)
                        if p == 0:
                            pe.wait_ge(sem["S0"], g + 1)
                        else:
                            pe.wait_ge(sem["st"], g * NPAIR + p)
                        mm(bank(6)[:, 32 * p:32 * p + 32], Spp[p % 2], qd32[:, 32 * p:32 * p + 32], False,
                           True).then_inc(sem["inter"], 1)
                    all_of(more)
                    if following:
                        all_of(project(g + 1, "Q"))
                    pe.wait_ge(sem["sq"], g + 1)
                    mm(bank(4), ones, sqh, True, True).then_inc(sem["ms"], 1)
                    if following:
                        all_of(project(g + 1, "I"))

                pe.wait_ge(sem["xt_in"], 16 * part + 16)
                for name in "FGQI":
                    all_of(project(HG * part, name))
                with pe.Fori(0, HG - 1) as h:
                    head(h + HG * part, True)
                head(HG * part + HG - 1, False)
                end_stage(pe, 6 * part)

                pe.wait_ge(sem["wc_in"], 16 * part + 16)
                for j in range(7):
                    product(bank(j), lambda kt: wc[:, kt, j, :], lambda kt: XT[:, kt, :]).then_inc(sem["cj"], 1)
                pe.wait_ge(sem["csq"], 5 * part + 3)
                product(bank(7), lambda i: ones, lambda i: csq[:, i, :], QT).then_inc(sem["mq"], 1)
                pe.wait_ge(sem["csq"], 5 * part + 5)
                pe.wait_ge(sem["stdq"], part + 1)
                product(bank(7), lambda i: ones, lambda i: csq[:, QT + i, :], KVT).then_inc(sem["mkv"], 1)
                if part == 0:
                    pe.wait_ge(sem["stdkv"], 1)
                    for j in range(4):
                        last = product(bank(7)[:, META * j:META * j + META], lambda kt: wc[:, kt, QT + j, :],
                                       lambda kt: XM[:, kt, :])
                    last.then_inc(sem["m_pe"], 1)
                    pe.wait_ge(sem["m_act"], 4)
                    pe.wait_ge(sem["cn"], QT)
                    product(bank(0)[:, 0:META], lambda i: ones, lambda i: mcsq[:, i, :], KVT
                            ).then_inc(sem["m_pe"], 1)
                end_stage(pe, 6 * part + 1)

                groups = groups_of(part)

                def pair(u):
                    G = u + 8 * part
                    pe.wait_ge(sem["wuq_in"], G * 16 + 16)
                    pe.wait_ge(sem["wukv_in"], G * 16 + 16)
                    for what, arg, b, n in jobs_of(part):
                        pe.wait_ge(sem[f"e{b}"], before(lambda x: bank_jobs(x, b), part, u) + n)
                        if what in ("qrA", "qrB", "qn"):
                            j = {"qrA": 2, "qrB": 3}.get(what, arg)
                            last = product(bank(b), lambda i: wuq[:, i, j, :], lambda i: cqn[:, i, :], QT)
                        elif what == "kn":
                            e, c, n_ = arg
                            last = product(wide(b)[:, 0:n_], lambda i: wukv[:, i, e, :],
                                           lambda i: ckvn[:, i, c:c + n_], KVT)
                        else:
                            j, many = arg
                            for t in range(many):
                                r = P if many == 2 else META
                                c = P * (j + t)
                                for i in range(KVT):
                                    last = mm(wide(b)[0:r, 256 * t:256 * t + 256], ckvn[:, i, c:c + r],
                                              wukv[:, i, 2:4, :], i == 0, i == KVT - 1)
                        last.then_inc(sem[f"j{b}"], 1)
                    for b in (6, 7):
                        pe.wait_ge(sem[f"e{b}"], before(lambda x: bank_jobs(x, b), part, u) + bank_jobs(part, b))

                    def scores(i):
                        e, b = divmod(i, NB)
                        nk = keys_of(part, b)
                        pe.wait_ge(sem["exp"], G * 2 * NB + i)
                        for c in range(0, nk, 512):
                            n = min(512, nk - c)
                            mm(PS[:, c:c + n], qn[e][:, cols(b)], kn[e][:, c:c + n], True, False)
                            lo = max(c, nk - P)
                            last = mm(PS[:, c:c + n], qr[ROPE * e:ROPE * e + ROPE, cols(b)],
                                      krT[ROPE * e:ROPE * e + ROPE, c:c + n], False, lo >= c + n)
                            if lo < c + n:
                                last = mm(PS[:, lo:c + n], ident, C[:, C_CAUS + lo - (nk - P):C_CAUS + c + n - (nk - P)],
                                          False, True)
                        last.then_inc(sem["Sm"], 1)

                    def turn(i, group):
                        tiles, bk, n = group
                        pe.wait_ge(sem[f"pe{bk}"], before(lambda x: bank_groups(x, bk), part, u) + n)
                        for s, t in enumerate(tiles):
                            r = rows_of(part, i % NB, t)
                            last = pe.transpose(wide(bk)[0:r, cols(s)], PR[i % 2][:, P * t:P * t + r], ident)
                        last.then_inc(sem[f"pt{bk}"], 1)

                    def values(i, group):
                        e, b = divmod(i, NB)
                        tiles, bk, n = group
                        pe.wait_ge(sem[f"pe{bk}"], before(lambda x: bank_groups(x, bk), part, u) + (n + 1))
                        for s, t in enumerate(tiles):
                            r = rows_of(part, b, t)
                            last = mm(bank(5)[:, cols(b)], V[0:r, t, cols(e)], PTs[bk - 3][0:r, cols(s)],
                                      t == 0, r < P)
                        last.then_inc(sem[f"pv{bk}"], 1)

                    def output(i):
                        pe.wait_ge(sem["pn"], G * 2 * NB + (i + 1))
                        if i % NB == 0:
                            pe.wait_ge(sem["OE"], G * 2 + i // NB)
                        for n, group in enumerate(groups[i]):
                            turn(i, group)
                            if n:
                                values(i, groups[i][n - 1])
                        values(i, groups[i][-1])

                    scores(0)
                    for i in range(1, 2 * NB):
                        scores(i)
                        output(i - 1)
                    output(2 * NB - 1)

                with pe.Fori(0, 8) as u:
                    pair(u)
                end_stage(pe, 6 * part + 2)

                with pe.Fori(0, KD) as n:
                    N = n + KD * part
                    for name, wname, w, x, kn_, b, used in (
                            ("pga", "wga_in", wga, XT, KD, 2, "sga"), ("pgb", "wgb_in", wgb, XT, KD, 3, "sgb"),
                            ("pya", "wa_in", wa, YH, HG, 0, "m1"), ("pyb", "wb_in", wb, YM, MH, 1, "m2")):
                        pe.wait_ge(sem[wname], N * 16 + 16)
                        pe.wait_ge(sem[used], N)
                        product(bank(b), lambda kt: w[:, kt, :], lambda kt: x[:, kt, :], kn_).then_inc(sem[name], 1)
                end_stage(pe, 6 * part + 3)

                for j in range(2):
                    pe.wait_ge(sem[f"wo{j}_in"], 16 * part + 16)
                    for b in range(NB):
                        product(wide(2 * b + j), lambda kt: MIX[:, kt, cols(b)],
                                lambda kt: WO[j][:, kt, :]).then_inc(sem["wo"], 1)
                for b in range(NB):
                    pe.wait_ge(sem["n8"], NB * part + b + 1)
                    for kt in range(KD):
                        last = pe.transpose(PS[:, 1024 * b + P * kt:1024 * b + P * kt + P],
                                            HB[:, b, P * kt:P * kt + P], ident)
                    last.then_inc(sem["hT"], 1)
                end_stage(pe, 6 * part + 4)

                with pe.Fori(0, PH) as h:
                    H = h + PH * part
                    for j in range(2):
                        pe.wait_ge(sem[f"wpq{j}_in"], H * 16 + 16)
                        pe.wait_ge(sem["pqe"], H * 2 + j)
                        product(bank(j), lambda kt: wpq[j][:, kt, :], lambda kt: HT[:, kt, :]
                                ).then_inc(sem[f"pq{j}"], 1)
                    pe.wait_ge(sem["wsk_in"], H * 16 + 16)
                    for j in range(2):
                        pe.wait_ge(sem["pqe"], H * 2 + (j + 1))
                        pe.wait_ge(sem["pse"], H * 2 + j)
                        for b in range(NB):
                            last = mm(bank(2 + j)[:, cols(b)], qT[j][:, cols(b)], wsk[:, j, :], True, True)
                        last.then_inc(sem["ps"], 1)
                end_stage(pe, 6 * part + 5)
            end_stage(pe, 6 * PARTS)

        @block.scalar
        def _(act):
            def run(out, in_, func, done, **kw):
                return act.activation(out, in_, func, **kw).then_inc(sem[done], 1)

            def tanh(R, p):
                act.wait_ge(sem["g_z"], R * 2 * STEPS + (2 * p + 2))
                run(gt_[:, NB * p:NB * p + NB], gz_[:, NB * p:NB * p + NB], ACT.Tanh, "g_th", scale=GELU_B)

            def weigh(R, p):
                act.wait_ge(sem["g_w"], R * 2 * STEPS + (2 * p + 2))
                v = ROW[NB * p + 1][:, D:2 * D]
                run(v, v, ACT.Copy, "g_v", scale=gw_[:, NB * p + 1:NB * p + 2])

            def norm2(c):
                for b in range(NB):
                    n = NB * c + b
                    act.wait_ge(sem["q1"], 3 * n)
                    act.wait_ge(sem["accv"], (c + 1) * NSEL)
                    act.wait_ge(sem["accp"], (c + 1) * NSEL)
                    run(junk, ACC[:, b, :], ACT.Copy, "q1", accum_out=st2[:, 8 * b:8 * b + 1])
                    act.wait_ge(sem["q2"], n + 1)
                    act.wait_ge(sem["q1"], 3 * n + 1)
                    run(junk, ACC[:, b, :], ACT.Square, "q1", bias=st2[:, 8 * b + 1:8 * b + 2],
                        accum_out=st2[:, 8 * b + 2:8 * b + 3])
                    act.wait_ge(sem["q1"], 3 * n + 2)
                    run(st2[:, 8 * b + 3:8 * b + 4], st2[:, 8 * b + 2:8 * b + 3], ACT.Sqrt, "q1", scale=1.0 / D,
                        bias=EPSC)

            act.wait_ge(sem["lb_ready"], 3)
            run(small[:, 24:40], small[:, 24:40], ACT.Exp, "lb_ready")
            act.wait_ge(sem["m_F"], HG)
            run(msg, PS[:, 0:P], ACT.Sigmoid, "m_act")
            act.wait_ge(sem["m_I"], HG)
            run(miT[0:META, :], PS[0:META, 512:512 + HG * P], ACT.Copy, "m_act")
            act.wait_ge(sem["m_pe"], 1)
            run(mksT[0:META, :], PS[0:META, 1536:1536 + HG * P], ACT.Copy, "m_act")

            for part in range(PARTS):
                def forget(g):
                    act.wait_ge(sem["F"], g + 1)
                    act.wait_ge(sem["f"], g * 2)
                    run(sg, bank(0), ACT.Sigmoid, "sig")

                def gate(g):
                    act.wait_ge(sem["G"], g + 1)
                    act.wait_ge(sem["t2"], g)
                    run(sg2, bank(1), ACT.Sigmoid, "sigG")

                def inputs(g):
                    act.wait_ge(sem["I"], g + 1)
                    act.wait_ge(sem["inter"], g * NPAIR)
                    run(isb, bank(3), ACT.Copy, "isb")

                def head(g, h, following):
                    R = h + ROUNDS * (part - 1)
                    if part:
                        tanh(R, 0)
                    if following:
                        forget(g + 1)
                    if part:
                        tanh(R, 1)
                        weigh(R, 0)
                        tanh(R, 2)
                        weigh(R, 1)
                    if following:
                        gate(g + 1)
                    act.wait_ge(sem["inter"], g * NPAIR + NPAIR)
                    act.wait_ge(sem["ms"], g)
                    run(sqh, bank(6), ACT.Square, "sq")
                    act.wait_ge(sem["ms"], g + 1)
                    act.wait_ge(sem["rs"], g)
                    run(std, bank(4), ACT.Sqrt, "std", scale=1.0 / P, bias=EPSC)
                    if part:
                        tanh(R, 3)
                        weigh(R, 2)
                    if following:
                        inputs(g + 1)
                    if part:
                        weigh(R, 3)

                forget(HG * part)
                gate(HG * part)
                inputs(HG * part)
                with act.Fori(0, HG - 1) as h:
                    head(h + HG * part, h, True)
                head(HG * part + HG - 1, HG - 1, False)
                end_stage(act, 6 * part)

                for i in range(QT + KVT):
                    act.wait_ge(sem["cj"], 7 * part + i + 1)
                    run(csq[:, i, :], bank(i), ACT.Square, "csq")
                    if part:
                        if i < STEPS:
                            tanh(ROUNDS * (part - 1) + R_LATENT, i)
                        if i:
                            weigh(ROUNDS * (part - 1) + R_LATENT, i - 1)
                act.wait_ge(sem["mq"], part + 1)
                run(cstd, bank(7), ACT.Sqrt, "stdq", scale=1.0 / (QT * P), bias=EPSC)
                act.wait_ge(sem["mkv"], part + 1)
                act.wait_ge(sem["rsq"], part + 1)
                run(cstd, bank(7), ACT.Sqrt, "stdkv", scale=1.0 / (KVT * P), bias=EPSC)
                if part == 0:
                    act.wait_ge(sem["m_pe"], 3)
                    run(mcsq.rearrange("p a b -> p (a b)"), bank(7)[:, 0:KVT * META], ACT.Square, "m_act")
                    act.wait_ge(sem["m_pe"], 4)
                    run(mstd, bank(0)[:, 0:META], ACT.Sqrt, "m_act", scale=1.0 / (KVT * P), bias=EPSC)
                else:
                    for p in range(STEPS):
                        tanh(ROUNDS * (part - 1) + R_LATENT + 1, p)
                        if p:
                            weigh(ROUNDS * (part - 1) + R_LATENT + 1, p - 1)
                    weigh(ROUNDS * (part - 1) + R_LATENT + 1, STEPS - 1)
                end_stage(act, 6 * part + 1)

                groups = groups_of(part)
                with act.Fori(0, 8) as u:
                    G = u + 8 * part
                    for what, arg, b, n in jobs_of(part):
                        if b == 7:
                            continue
                        act.wait_ge(sem["j6"], before(lambda x: bank_jobs(x, 6), part, u) + (n + 1))
                        if what == "qn":
                            run(qn[arg], bank(6), ACT.Copy, "e6")
                        elif what == "kn":
                            e, c, n_ = arg
                            run(kn[e][:, c:c + n_], wide(6)[:, 0:n_], ACT.Copy, "e6")
                        else:
                            j, many = arg
                            r = P if many == 2 else META
                            run(V[0:r, j:j + many, :], wide(6)[0:r, 0:256 * many], ACT.Copy, "e6")
                        if part and n in (1, 2, 4):
                            p = (1, 2, 4).index(n)
                            if p:
                                weigh(u * 2 + (ROUNDS * (part - 1) + R_ATTEND), p - 1)
                            tanh(u * 2 + (ROUNDS * (part - 1) + R_ATTEND), p)
                    if part:
                        tanh(u * 2 + (ROUNDS * (part - 1) + R_ATTEND), STEPS - 1)
                        for p in range(STEPS - 2, STEPS):
                            weigh(u * 2 + (ROUNDS * (part - 1) + R_ATTEND), p)

                    def copy_turned(i, some):
                        for tiles, bk, n in groups[i][some]:
                            if bk == 3:
                                act.wait_ge(sem["pt3"], before(lambda x: bank_groups(x, 3), part, u) + (n + 1))
                                act.wait_ge(sem["pv3"], before(lambda x: bank_groups(x, 3), part, u) + n)
                                full = [t for t in tiles if rows_of(part, i % NB, t) == P]
                                if full:
                                    one = act.activation(PTs[0][:, 0:P * len(full)], wide(3)[:, 0:P * len(full)],
                                                         ACT.Copy)
                                if len(full) < len(tiles):
                                    s = len(full)
                                    one = act.activation(PTs[0][0:META, cols(s)], wide(3)[0:META, cols(s)], ACT.Copy)
                                one.then_inc(sem["pe3"], 1)
                        if i % NB == NB - 1 and some.stop is None:
                            bk, n = groups[i][-1][1:]
                            act.wait_ge(sem[f"pv{bk}"], before(lambda x: bank_groups(x, bk), part, u) + (n + 1))
                            run(YM[:, bass.ds(u * 2 + i // NB, 1), :], bank(5), ACT.Copy, "OE")

                    for i in range(2 * NB):
                        nk = keys_of(part, i % NB)
                        if i:
                            copy_turned(i - 1, slice(0, 1))
                        act.wait_ge(sem["ngm"], G * 2 * NB + (i + 1))
                        run(PR[i % 2][:, 0:nk], PS[:, 0:nk], ACT.Exp, "exp", scale=SCALE,
                            bias=smx[:, 2 + i % 2:3 + i % 2], accum_out=smx[:, 4 + i % 2:5 + i % 2])
                        if i:
                            copy_turned(i - 1, slice(1, None))
                        if part:
                            if i:
                                weigh(u * 2 + (ROUNDS * (part - 1) + R_ATTEND + 1), i - 1)
                            tanh(u * 2 + (ROUNDS * (part - 1) + R_ATTEND + 1), i)
                    copy_turned(2 * NB - 1, slice(0, None))
                    if part:
                        weigh(u * 2 + (ROUNDS * (part - 1) + R_ATTEND + 1), STEPS - 1)
                end_stage(act, 6 * part + 2)

                with act.Fori(0, 2) as m:
                    for n in range(KD // 2):
                        N = m * (KD // 2) + (n + KD * part)
                        act.wait_ge(sem["pga"], N + 1)
                        act.wait_ge(sem["m1"], N)
                        run(sga, bank(2), ACT.Sigmoid, "sga")
                        act.wait_ge(sem["pgb"], N + 1)
                        act.wait_ge(sem["m2"], N)
                        run(sgb, bank(3), ACT.Sigmoid, "sgb")
                        for j in range(2 * n, 2 * n + 2) if part else ():
                            R, p = m * (MIX_ROUNDS // 2) + (ROUNDS * (part - 1) + R_MIX + j // STEPS), j % STEPS
                            tanh(R, p)
                            if p:
                                weigh(R, p - 1)
                            if p == STEPS - 1:
                                weigh(R, p)
                end_stage(act, 6 * part + 3)

                def whole_round(j):
                    for p in range(STEPS):
                        tanh(j, p)
                        if p:
                            weigh(j, p - 1)
                    weigh(j, STEPS - 1)

                if part:
                    whole_round(ROUNDS * (part - 1) + R_NORM)
                for b in range(NB):
                    n = NB * part + b
                    act.wait_ge(sem["n2"], n + 1)
                    act.wait_ge(sem["n3"], n)
                    run(junk, R1[b % 2], ACT.Square, "n3", bias=st1[:, 8 * b + 2:8 * b + 3],
                        accum_out=st1[:, 8 * b + 3:8 * b + 4])
                    act.wait_ge(sem["n3"], n + 1)
                    run(st1[:, 8 * b + 4:8 * b + 5], st1[:, 8 * b + 3:8 * b + 4], ACT.Sqrt, "n4", scale=1.0 / D,
                        bias=EPSC)
                if part:
                    whole_round(ROUNDS * part - 1)
                for b in range(NB):
                    act.wait_ge(sem["hT"], NB * part + b + 1)
                    for j in range(2):
                        run(HT[:, 4 * j:4 * j + 4, cols(b)],
                            wide(2 * b + j).rearrange("p (x y) -> p x y", x=4), ACT.Copy, "hTe")
                if part:
                    norm2(part - 1)
                end_stage(act, 6 * part + 4)

                def queries_and_scores(H):
                    for j in range(2):
                        act.wait_ge(sem[f"pq{j}"], H + 1)
                        act.wait_ge(sem["ps"], H * 2 + j)
                        run(qT[j], bank(j), ACT.Copy, "pqe")
                    for j in range(2):
                        act.wait_ge(sem["ps"], H * 2 + (j + 1))
                        act.wait_ge(sem["t2nd"], H * 2)
                        run(SS[:, j, :, :], bank(2 + j), ACT.Copy, "pse")

                def softmax(H):
                    act.wait_ge(sem["gmx"], H + 1)
                    act.wait_ge(sem["dvc"], H * DVC)
                    run(ge, gd, ACT.Exp, "gex")

                queries_and_scores(PH * part)
                with act.Fori(0, PH - 1) as h:
                    queries_and_scores(h + (PH * part + 1))
                    softmax(h + PH * part)
                if part:
                    act.wait_ge(sem["out_done"], 16 * part)
                for b in range(NB):
                    run(ACC[:, b, :], HB[:, b, :], ACT.Copy, "acc0", scale=ALPHA)
                softmax(PH * part + PH - 1)
                end_stage(act, 6 * part + 5)

            with act.Fori(0, ROUNDS) as q:
                for p in range(STEPS):
                    tanh(q + ROUNDS * (PARTS - 1), p)
                    if p:
                        weigh(q + ROUNDS * (PARTS - 1), p - 1)
                weigh(q + ROUNDS * (PARTS - 1), STEPS - 1)
            end_stage(act, 6 * PARTS)
            norm2(PARTS - 1)

        @block.vector
        def _(dve):
            tt, ts, stt = dve.tensor_tensor, dve.tensor_scalar, dve.scalar_tensor_tensor

            def experts(R, first):
                def weight(p):
                    K = R * STEPS + p
                    mine = slice(NB * p, NB * p + NB)
                    dve.wait_ge(sem["g_th"], K + 1)
                    stt(gu_[:, mine], gt_[:, mine], 1.0, ga_[:, mine], ALU.add, ALU.mult).then_inc(sem["g_w"], 1)
                    yield
                    dve.wait_ge(sem["g_w"], K * 2 + 1)
                    k = first + p
                    stt(gw_[:, mine].unsqueeze(2), gu_[:, mine].unsqueeze(2), 0.5, GATE[:, :, bass.ds(k, 1)],
                        ALU.mult, ALU.mult).then_inc(sem["g_w"], 1)
                    yield
                    dve.wait_ge(sem["g_w"], K * 2 + 2)
                    dve.wait_ge(sem["accv"], K)
                    stt(ACC[:, 0, :], ROW[NB * p][:, D:2 * D], gw_[:, NB * p:NB * p + 1], ACC[:, 0, :],
                        ALU.mult, ALU.add).then_inc(sem["accv"], 1)
                for p in range(STEPS):
                    K = R * STEPS + p
                    mine = slice(NB * p, NB * p + NB)
                    before_ = weight(p - 1) if p else iter(())
                    for b in range(NB):
                        s = NB * p + b
                        dve.wait_ge(got[s], R * 16 + 16)
                        dve.tensor_tensor_reduce(ROW[s][:, 0:D], ROW[s][:, 0:D], HB[:, b, :], 1.0, 0.0, ALU.mult,
                                                 ALU.add, ga_[:, s:s + 1]).then_inc(sem["g_dot"], 1)
                        next(before_, None)
                        yield
                    dve.wait_ge(sem["g_dot"], K * NB + NB)
                    stt(gx_[:, mine], ga_[:, mine], GELU_A, ga_[:, mine], ALU.mult, ALU.mult
                        ).then_inc(sem["g_z"], 1)
                    next(before_, None)
                    dve.wait_ge(sem["g_z"], K * 2 + 1)
                    stt(gz_[:, mine], gx_[:, mine], 1.0, ga_[:, mine], ALU.add, ALU.mult).then_inc(sem["g_z"], 1)
                    yield
                for _ in weight(STEPS - 1):
                    pass

            def norm2(c):
                dve.wait_ge(sem["q_in"], 16 * (c + 1))
                for b in range(NB):
                    n = NB * c + b
                    dve.wait_ge(sem["q1"], 3 * n + 1)
                    ts(st2[:, 8 * b + 1:8 * b + 2], st2[:, 8 * b:8 * b + 1], -1.0 / D, None, ALU.mult
                       ).then_inc(sem["q2"], 1)
                    dve.wait_ge(sem["q1"], 3 * n + 3)
                    dve.reciprocal(st2[:, 8 * b + 4:8 * b + 5], st2[:, 8 * b + 3:8 * b + 4]).then_inc(sem["qd"], 1)
                    dve.wait_ge(sem["qd"], 4 * n + 1)
                    ts(ACC[:, b, :], ACC[:, b, :], st2[:, 8 * b + 1:8 * b + 2], st2[:, 8 * b + 4:8 * b + 5], ALU.add,
                       ALU.mult).then_inc(sem["qd"], 1)
                    dve.wait_ge(sem["qd"], 4 * n + 2)
                    tt(ACC[:, b, :], ACC[:, b, :], LN2[:, 0, :], ALU.mult).then_inc(sem["qd"], 1)
                    dve.wait_ge(sem["qd"], 4 * n + 3)
                    tt(ACC[:, b, :], ACC[:, b, :], LN2[:, 1, :], ALU.add).then_inc(sem["qd"], 1)

            def all_of(steps):
                for _ in steps:
                    pass

            NOTSTART, END = C[:, C_NS:C_NS + TOK], C[:, C_END:C_END + TOK]
            dve.memset(EPSC, EPS).then_inc(sem["start"], 1)
            dve.memset(mfm[:, P:P + 1], 0.0).then_inc(sem["start"], 1)
            dve.memset(fm[:, TOK:TOK + 1], 0.0).then_inc(sem["start"], 1)
            dve.wait_ge(sem["start"], 3)
            dve.wait_ge(sem["c_in"], 64)
            dve.tensor_copy(MB[:], y1).then_inc(sem["start"], 1)
            dve.wait_ge(sem["start"], 4)
            tt(small[:, 40:48], PV[:, 0:8], PV[:, 8:16], ALU.max).then_inc(sem["lb_ready"], 1)
            dve.wait_ge(sem["lb_ready"], 1)
            for j in range(2):
                tt(small[:, 24 + 8 * j:32 + 8 * j], PV[:, 8 * j:8 * j + 8], small[:, 40:48], ALU.subtract
                   ).then_inc(sem["lb_ready"], 1)
            dve.wait_ge(sem["lb_ready"], 4)
            tt(small[:, 48:56], small[:, 24:32], small[:, 32:40], ALU.add).then_inc(sem["lb_ready"], 1)
            dve.wait_ge(sem["lb_ready"], 5)
            dve.reciprocal(small[:, 48:56], small[:, 48:56]).then_inc(sem["lb_ready"], 1)
            dve.wait_ge(sem["lb_ready"], 6)
            tt(LB, small[:, 24:32], small[:, 48:56], ALU.mult).then_inc(sem["lb_ready"], 1)
            dve.wait_ge(sem["lb_ready"], 7)
            ts(OML, LB, -1.0, 1.0, ALU.mult, ALU.add).then_inc(sem["lb_ready"], 1)
            dve.wait_ge(sem["lb_ready"], 8)
            dve.wait_ge(sem["m_act"], 1)
            by_head = lambda x: x.rearrange("p (h t) -> p h t", h=HG)
            tt(by_head(mf), by_head(msg), OML.unsqueeze(2).to_broadcast([P, HG, META]), ALU.mult
               ).then_inc(sem["m_dve"], 1)
            dve.wait_ge(sem["m_dve"], 1)
            tt(by_head(mf), by_head(mf), LB.unsqueeze(2).to_broadcast([P, HG, META]), ALU.add
               ).then_inc(sem["m_dve"], 1)
            dve.wait_ge(sem["m_dve"], 2)
            tt(mfm[:, 0:P], mf, NOTSTART[:, 0:P], ALU.mult).then_inc(sem["m_dve"], 1)
            dve.wait_ge(sem["m_dve"], 3)
            dve.tensor_tensor_scan(mest[:, ::-1], mfm[:, P:0:-1], END[:, P - 1::-1], 0.0, ALU.mult, ALU.add
                                   ).then_inc(sem["m_dve"], 1)
            dve.wait_ge(sem["m_pe"], 2)
            dve.tensor_copy(S_all[:], PS[:, 2560:2560 + HG * P]).then_inc(sem["m_dve"], 1)

            for part in range(PARTS):
                def chain(g):
                    dve.wait_ge(sem["sig"], g + 1)
                    dve.wait_ge(sem["k"], g)
                    dve.wait_ge(sem["ebi"], g)
                    dve.wait_ge(sem["est"], g)
                    dve.wait_ge(sem["qd16"], g)
                    ts(f, sg, fcol[:, 1:2], fcol[:, 0:1], ALU.mult, ALU.add).then_inc(sem["f"], 2)
                    yield
                    dve.wait_ge(sem["f"], g * 2 + 2)
                    tt(fm[:, 0:TOK], f, NOTSTART, ALU.mult).then_inc(sem["fm"], 1)
                    yield
                    dve.wait_ge(sem["fm"], g + 1)
                    dve.wait_ge(sem["ks16"], g)
                    dve.tensor_tensor_scan(est[:, ::-1], fm[:, TOK:0:-1], END[:, ::-1], 0.0, ALU.mult, ALU.add
                                           ).then_inc(sem["est"], 1)
                    tt(fs, f, fm[:, 0:TOK], ALU.subtract).then_inc(sem["fs"], 1)
                    yield
                    dve.wait_ge(sem["fs"], g + 1)
                    dve.wait_ge(sem["D"], g)
                    dve.wait_ge(sem["qd32"], g)
                    dve.tensor_tensor_scan(eb, fm[:, 0:TOK], fs, 0.0, ALU.mult, ALU.add).then_inc(sem["eb"], 1)
                    yield
                    dve.wait_ge(sem["eb"], g + 1)
                    dve.wait_ge(sem["ki"], g)
                    dve.reciprocal(ebi, eb).then_inc(sem["ebi"], 1)

                def queries(g):
                    dve.wait_ge(sem["Q"], g + 1)
                    dve.wait_ge(sem["M2"], g)
                    dve.wait_ge(sem["qd32"], g)
                    tt(qd16, bank(2), eb, ALU.mult).then_inc(sem["qd16"], 1)

                def gate(g):
                    dve.wait_ge(sem["sigG"], g + 1)
                    dve.wait_ge(sem["y"], g)
                    tt(t2, bank(1), sg2, ALU.mult).then_inc(sem["t2"], 1)

                def columns(g, h):
                    dve.wait_ge(sem["f"], g * 2)
                    apart(dve)
                    dve.tensor_copy(fcol[:, 0:1], LB[:, bass.ds(h, 1)]).then_inc(sem["fcol"], 1)
                    dve.tensor_copy(fcol[:, 1:2], OML[:, bass.ds(h, 1)]).then_inc(sem["fcol"], 1)
                    dve.wait_ge(sem["fcol"], g * 2 + 2)

                def head(g, h, following):
                    dve.wait_ge(sem["T"], g + 1)
                    dve.wait_ge(sem["inter"], g * NPAIR)
                    dve.tensor_copy(ksT, bank(5)).then_inc(sem["ksT"], 1)
                    dve.wait_ge(sem["M1"], g + 1)
                    dve.wait_ge(sem["inter"], g * NPAIR)
                    tt(sc, bank(4), C[:, C_MA:C_MA + TOK], ALU.mult).then_inc(sem["sA"], 1)
                    dve.wait_ge(sem["y1"], g)
                    apart(dve)
                    dve.tensor_copy(fcol[:, 2:3], PV[:, bass.ds(h + 16, 1)]).then_inc(sem["gcol"], 1)
                    dve.tensor_copy(Spp[0], S_all[:, bass.ds(h, 1), :]).then_inc(sem["S0"], 1)
                    dve.wait_ge(sem["M2"], g + 1)
                    dve.wait_ge(sem["sA"], g + 1)
                    apart(dve)
                    dve.copy_predicated(sc, MB[:], bank(5)).then_inc(sem["sc"], 1)
                    dve.wait_ge(sem["D"], g + 1)
                    dve.wait_ge(sem["S0"], g + 1)
                    ex = experts(h + ROUNDS * (part - 1), h * STEPS) if part else iter(())
                    following_gates = iter(())
                    for p in range(NPAIR):
                        dve.wait_ge(sem["St"], g * NPAIR + (p + 1))
                        dve.wait_ge(sem["inter"], g * NPAIR + p)
                        if p:
                            dve.wait_ge(sem["st"], g * NPAIR + p)
                        stt(Spp[(p + 1) % 2], Spp[p % 2], Dp[:, p:p + 1], bank(7 if p % 2 == 0 else 5)[:, 0:P],
                            ALU.mult, ALU.add).then_inc(sem["st"], 1)
                        next(ex, None)
                        if p % 2:
                            next(ex, None)
                        if p == 5 and following:
                            columns(g + 1, h + 1)
                            following_gates = chain(g + 1)
                        if p >= 5:
                            next(following_gates, None)
                    dve.wait_ge(sem["st"], g * NPAIR + NPAIR)
                    apart(dve)
                    dve.tensor_copy(S_all[:, bass.ds(h, 1), :], Spp[0]).then_inc(sem["Sb"], 1)
                    all_of(following_gates)
                    if following:
                        queries(g + 1)
                    dve.wait_ge(sem["std"], g + 1)
                    dve.wait_ge(sem["y"], g)
                    dve.reciprocal(rs, std).then_inc(sem["rs"], 1)
                    dve.wait_ge(sem["rs"], g + 1)
                    stt(y1, bank(6), fcol[:, 2:3], rs, ALU.mult, ALU.mult).then_inc(sem["y1"], 1)
                    dve.wait_ge(sem["y1"], g + 1)
                    tt(YH[:, bass.ds(h, 1), :], y1.unsqueeze(1), t2.unsqueeze(1), ALU.mult).then_inc(sem["y"], 1)
                    if following:
                        gate(g + 1)
                    all_of(ex)
                    dve.wait_ge(sem["Sb"], g + 1)
                    apart(dve)

                columns(HG * part, 0)
                all_of(chain(HG * part))
                gate(HG * part)
                queries(HG * part)
                with dve.Fori(0, HG - 1) as h:
                    head(h + HG * part, h, True)
                head(HG * part + HG - 1, HG - 1, False)
                end_stage(dve, 6 * part)

                t0 = META + TOK * part
                ex = iter(())
                if part:
                    all_of(experts(ROUNDS * (part - 1) + R_LATENT, R_LATENT * STEPS))
                    ex = experts(ROUNDS * (part - 1) + R_LATENT + 1, (R_LATENT + 1) * STEPS)
                dve.wait_ge(sem["stdq"], part + 1)
                dve.reciprocal(crs, cstd).then_inc(sem["rsq"], 1)
                dve.wait_ge(sem["rsq"], part + 1)
                for i in range(QT):
                    stt(cqn[:, i, :], bank(i), PV[:, 24 + i:25 + i], crs, ALU.mult, ALU.mult).then_inc(sem["cn"], 1)
                next(ex, None)
                next(ex, None)
                dve.wait_ge(sem["stdkv"], part + 1)
                dve.wait_ge(sem["cn"], QT * part + QT)
                dve.reciprocal(crs, cstd).then_inc(sem["rskv"], 1)
                dve.wait_ge(sem["rskv"], part + 1)
                for i in range(KVT):
                    stt(ckvn[:, i, t0:t0 + TOK], bank(QT + i), PV[:, 27 + i:28 + i], crs, ALU.mult, ALU.mult
                        ).then_inc(sem["ckn"], 1)
                dve.wait_ge(sem["cj"], 7 * part + 7)
                tt(kta, bank(5), C[:, C_COS + t0:C_COS + t0 + TOK], ALU.mult).then_inc(sem["krA"], 1)
                tt(ktb, bank(6), C[:, C_SIN + t0:C_SIN + t0 + TOK], ALU.mult).then_inc(sem["krB"], 1)
                dve.wait_ge(sem["krA"], part + 1)
                dve.wait_ge(sem["krB"], part + 1)
                tt(krT[:, t0:t0 + TOK], kta, ktb, ALU.add).then_inc(sem["kr"], 1)
                if part == 0:
                    dve.wait_ge(sem["m_act"], 5)
                    dve.reciprocal(mrs, mstd).then_inc(sem["m_dve"], 1)
                    dve.wait_ge(sem["m_dve"], 6)
                    for i in range(KVT):
                        stt(ckvn[:, i, 0:META], bank(7)[:, META * i:META * i + META], PV[:, 27 + i:28 + i], mrs,
                            ALU.mult, ALU.mult).then_inc(sem["m_dve"], 1)
                    tt(mka, bank(7)[:, 2 * META:3 * META], C[:, C_COS:C_COS + META], ALU.mult
                       ).then_inc(sem["m_dve"], 1)
                    tt(mkb, bank(7)[:, 3 * META:4 * META], C[:, C_SIN:C_SIN + META], ALU.mult
                       ).then_inc(sem["m_dve"], 1)
                    dve.wait_ge(sem["m_dve"], 10)
                    tt(krT[:, 0:META], mka, mkb, ALU.add).then_inc(sem["m_dve"], 1)
                all_of(ex)
                end_stage(dve, 6 * part + 1)

                groups = groups_of(part)
                with dve.Fori(0, 8) as u:
                    G = u + 8 * part
                    for what, arg, b, n in jobs_of(part):
                        if b == 6:
                            continue
                        if n == 0 and part:
                            ex = experts(u * 2 + (ROUNDS * (part - 1) + R_ATTEND), u * (2 * STEPS) + R_ATTEND * STEPS)
                        dve.wait_ge(sem["j7"], before(lambda x: bank_jobs(x, 7), part, u) + (n + 1))
                        if what == "qrA":
                            dve.wait_ge(sem["e7"], before(lambda x: bank_jobs(x, 7), part, u))
                            tt(qra, bank(7), C[:, C_COS + t0:C_COS + t0 + TOK], ALU.mult).then_inc(sem["e7"], 1)
                        elif what == "qrB":
                            tt(qrb, bank(7), C[:, C_SIN + t0:C_SIN + t0 + TOK], ALU.mult).then_inc(sem["qrb"], 1)
                            dve.wait_ge(sem["qrb"], G + 1)
                            tt(qr, qra, qrb, ALU.add).then_inc(sem["e7"], 1)
                        elif what == "kn":
                            e, c, n_ = arg
                            dve.tensor_copy(kn[e][:, c:c + n_], wide(7)[:, 0:n_]).then_inc(sem["e7"], 1)
                        else:
                            j, many = arg
                            r = P if many == 2 else META
                            dve.tensor_copy(V[0:r, j:j + many, :], wide(7)[0:r, 0:256 * many]).then_inc(sem["e7"], 1)
                        if part and n < 6:
                            next(ex)
                            next(ex)
                    if part:
                        all_of(ex)
                        ex = experts(u * 2 + (ROUNDS * (part - 1) + R_ATTEND + 1), u * (2 * STEPS) + (R_ATTEND + 1) * STEPS)

                    def copy_turned(i):
                        for tiles, bk, n in groups[i]:
                            if bk == 4:
                                dve.wait_ge(sem["pt4"], before(lambda x: bank_groups(x, 4), part, u) + (n + 1))
                                dve.wait_ge(sem["pv4"], before(lambda x: bank_groups(x, 4), part, u) + n)
                                full = [t for t in tiles if rows_of(part, i % NB, t) == P]
                                if full:
                                    one = dve.tensor_copy(PTs[1][:, 0:P * len(full)], wide(4)[:, 0:P * len(full)])
                                if len(full) < len(tiles):
                                    s = len(full)
                                    one = dve.tensor_copy(PTs[1][0:META, cols(s)], wide(4)[0:META, cols(s)])
                                one.then_inc(sem["pe4"], 1)

                    for i in range(2 * NB):
                        nk = keys_of(part, i % NB)
                        dve.wait_ge(sem["Sm"], G * 2 * NB + (i + 1))
                        dve.wait_ge(sem["ngm"], G * 2 * NB + i)
                        dve.reduce_max(smx[:, i % 2:i % 2 + 1], PS[:, 0:nk], AX).then_inc(sem["mx"], 1)
                        dve.wait_ge(sem["mx"], G * 2 * NB + (i + 1))
                        ts(smx[:, 2 + i % 2:3 + i % 2], smx[:, i % 2:i % 2 + 1], -SCALE, None, ALU.mult
                           ).then_inc(sem["ngm"], 1)
                        if i:
                            copy_turned(i - 1)
                        if part:
                            next(ex)
                        dve.wait_ge(sem["exp"], G * 2 * NB + (i + 1))
                        dve.wait_ge(sem["pn"], G * 2 * NB + max(i - 1, 0))
                        dve.reciprocal(smx[:, 6 + i % 2:7 + i % 2], smx[:, 4 + i % 2:5 + i % 2]
                                       ).then_inc(sem["rcp"], 1)
                        if part:
                            for _ in range(2):
                                next(ex)
                    copy_turned(2 * NB - 1)
                    if part:
                        all_of(ex)
                end_stage(dve, 6 * part + 2)

                with dve.Fori(0, 2) as m:
                    def rounds():
                        for j in range(MIX_ROUNDS // 2):
                            yield from experts(m * (MIX_ROUNDS // 2) + (ROUNDS * (part - 1) + R_MIX + j),
                                               m * (MIX_ROUNDS // 2 * STEPS) + (R_MIX + j) * STEPS)

                    ex = rounds() if part else iter(())
                    for n in range(KD // 2):
                        N = m * (KD // 2) + (n + KD * part)
                        for _ in range(3):
                            next(ex, None)
                        dve.wait_ge(sem["pya"], N + 1)
                        dve.wait_ge(sem["sga"], N + 1)
                        dve.wait_ge(sem["mix"], N)
                        tt(mm1, bank(0), sga, ALU.mult).then_inc(sem["m1"], 1)
                        dve.wait_ge(sem["pyb"], N + 1)
                        dve.wait_ge(sem["sgb"], N + 1)
                        tt(mm2, bank(1), sgb, ALU.mult).then_inc(sem["m2"], 1)
                        dve.wait_ge(sem["m2"], N + 1)
                        tt(MIX[:, bass.ds(m * (KD // 2) + n, 1), :], mm1.unsqueeze(1), mm2.unsqueeze(1), ALU.add
                           ).then_inc(sem["mix"], 1)
                        for _ in range(3):
                            next(ex, None)
                    all_of(ex)
                end_stage(dve, 6 * part + 3)

                if part:
                    all_of(experts(ROUNDS * (part - 1) + R_NORM, R_NORM * STEPS))
                dve.wait_ge(sem["xk_in"], 16 * part + 16)
                dve.wait_ge(sem["ln_in"], 16 * part + 16)
                for b in range(NB):
                    n = NB * part + b
                    c0 = 8 * b
                    dve.wait_ge(sem["wo"], 2 * NB * part + NB + b + 1)
                    if n >= 2:
                        dve.wait_ge(sem["n8"], n - 1)
                    for j in range(2):
                        stt(R1[b % 2][:, 512 * j:512 * j + 512], XK[:, b, 512 * j:512 * j + 512], ALPHA,
                            wide(2 * b + j), ALU.mult, ALU.add, accum_out=st1[:, c0 + j:c0 + j + 1]
                            ).then_inc(sem["r"], 1)
                    dve.wait_ge(sem["r"], 2 * n + 2)
                    tt(st1[:, c0 + 2:c0 + 3], st1[:, c0:c0 + 1], st1[:, c0 + 1:c0 + 2], ALU.add
                       ).then_inc(sem["nd"], 1)
                    dve.wait_ge(sem["nd"], 4 * n + 1)
                    ts(st1[:, c0 + 2:c0 + 3], st1[:, c0 + 2:c0 + 3], -1.0 / D, None, ALU.mult
                       ).then_inc(sem["n2"], 1)
                    dve.wait_ge(sem["n4"], n + 1)
                    dve.reciprocal(st1[:, c0 + 5:c0 + 6], st1[:, c0 + 4:c0 + 5]).then_inc(sem["nd"], 1)
                    dve.wait_ge(sem["nd"], 4 * n + 2)
                    ts(R1[b % 2], R1[b % 2], st1[:, c0 + 2:c0 + 3], st1[:, c0 + 5:c0 + 6], ALU.add, ALU.mult
                       ).then_inc(sem["nd"], 1)
                    dve.wait_ge(sem["nd"], 4 * n + 3)
                    tt(R1[b % 2], R1[b % 2], LN1[:, 0, :], ALU.mult).then_inc(sem["nd"], 1)
                if part:
                    all_of(experts(ROUNDS * part - 1, NSEL - STEPS))
                for b in range(NB):
                    dve.wait_ge(sem["nd"], 4 * (NB * part + b) + 4)
                    tt(HB[:, b, :], R1[b % 2], LN1[:, 1, :], ALU.add).then_inc(sem["n8"], 1)
                if part:
                    norm2(part - 1)
                end_stage(dve, 6 * part + 4)

                big = -3e38

                def wave(op, n, k, name, base):
                    for s in range(n):
                        op(s).then_inc(sem[name], 1)
                    dve.wait_ge(sem[name], base + n * k)
                    apart(dve)

                def sides(H):
                    B1 = H * 10 * NB
                    dve.wait_ge(sem["pse"], H * 2 + 2)
                    dve.wait_ge(sem["t2nd"], H * 2)
                    apart(dve)
                    S = lambda s: SS[:, s // NB, s % NB, :]
                    S2 = lambda s: SS2[:, s // NB, s % NB, :]
                    tV = lambda s: tv[:, s // NB, s % NB, :]
                    tI = lambda s: ti[:, s // NB, s % NB, :]
                    wave(lambda s: dve.max(tV(s)[:, 0:8], S(s)), 2 * NB, 1, "dv", B1)
                    wave(lambda s: dve.max_index(tI(s)[:, 0:8], tV(s)[:, 0:8], S(s)), 2 * NB, 2, "dv", B1)
                    wave(lambda s: dve.match_replace(S2(s), tV(s)[:, 0:8], S(s), big), 2 * NB, 3, "dv", B1)
                    wave(lambda s: dve.max(tV(s)[:, 8:16], S2(s)), 2 * NB, 4, "dv", B1)
                    wave(lambda s: dve.max_index(tI(s)[:, 8:16], tV(s)[:, 8:16], S2(s)), 2 * NB, 5, "dv", B1)

                def best(H):
                    dve.tensor_copy(tif[:, :, 0, :], ti[:, 0, :, :]).then_inc(sem["t2nd"], 1)
                    dve.tensor_copy(tif[:, :, 1, :], ti[:, 1, :, :]).then_inc(sem["t2nd"], 1)
                    B2 = H * 6 * NB
                    wave(lambda b: tt(CA[:, b, :].rearrange("p (x y) -> p x y", x=TOP),
                                      tv[:, 0, b, :].unsqueeze(2).to_broadcast([P, TOP, TOP]),
                                      tv[:, 1, b, :].unsqueeze(1).to_broadcast([P, TOP, TOP]), ALU.add),
                         NB, 1, "dvb", B2)
                    dve.wait_ge(sem["gmx"], H)
                    apart(dve)
                    wave(lambda b: dve.max(bv[:, b, 0:8], CA[:, b, :]), NB, 2, "dvb", B2)
                    wave(lambda b: dve.max_index(bs[:, b, 0:8], bv[:, b, 0:8], CA[:, b, :]), NB, 3, "dvb", B2)
                    wave(lambda b: dve.match_replace(CA2[:, b, :], bv[:, b, 0:8], CA[:, b, :], big),
                         NB, 4, "dvb", B2)
                    wave(lambda b: dve.max(bv[:, b, 8:16], CA2[:, b, :]), NB, 5, "dvb", B2)
                    wave(lambda b: dve.max_index(bs[:, b, 8:16], bv[:, b, 8:16], CA2[:, b, :]), NB, 6, "dvb", B2)
                    dve.wait_ge(sem["gex"], H)
                    tt(gd, bv, bv[:, :, 0:1].to_broadcast([P, NB, TOP]), ALU.subtract).then_inc(sem["gmx"], 1)
                    ts(bs2[:, :, :, 0], bs, 4, None, ALU.logical_shift_right).then_inc(sem["dvc"], 1)
                    ts(bs2[:, :, :, 1], bs, 15, None, ALU.bitwise_and).then_inc(sem["dvc"], 1)
                    dve.wait_ge(sem["dvc"], H * DVC + 2)
                    dve.tensor_copy(bsf, bs2).then_inc(sem["dvc"], 1)
                    dve.wait_ge(sem["dvc"], H * DVC + 3)
                    tt(OH.rearrange("p (n r) -> p n r", r=TOP),
                       bsf.rearrange("p b j z -> p (b j z)").unsqueeze(2).to_broadcast([P, NB * TOP * 2, TOP]),
                       C[:, C_IOTA:C_IOTA + TOP].unsqueeze(1).to_broadcast([P, NB * TOP * 2, TOP]), ALU.is_equal
                       ).then_inc(sem["dvc"], 1)

                def numbers(H, h):
                    dve.wait_ge(sem["onehot"], H * NB + NB)
                    dve.wait_ge(sem["dvc"], H * DVC + 4)
                    dve.tensor_reduce(osum.rearrange("p b j z -> p (b j z)"),
                                      OH2.rearrange("p (n r) -> p n r", r=TOP), AX, ALU.add).then_inc(sem["dvc"], 1)
                    dve.wait_ge(sem["dvc"], H * DVC + 5)
                    stt(eif, osum[:, :, :, 0], 128.0, osum[:, :, :, 1], ALU.mult, ALU.add).then_inc(sem["dvc"], 1)
                    dve.wait_ge(sem["dvc"], H * DVC + 6)
                    apart(dve)
                    dve.tensor_copy(EIDX[:, :, bass.ds(h * TOP, TOP)], eif).then_inc(sem["dvc"], 1)
                    dve.wait_ge(sem["gex"], H + 1)
                    dve.tensor_reduce(gs, ge, AX, ALU.add).then_inc(sem["dvc"], 1)
                    dve.wait_ge(sem["dvc"], H * DVC + 8)
                    dve.reciprocal(gr, gs).then_inc(sem["dvc"], 1)
                    dve.wait_ge(sem["dvc"], H * DVC + 9)
                    tt(GATE[:, :, bass.ds(h * TOP, TOP)], ge, gr.unsqueeze(2).to_broadcast([P, NB, TOP]), ALU.mult
                       ).then_inc(sem["dvc"], 1)

                sides(PH * part)
                best(PH * part)
                with dve.Fori(0, PH - 1) as h:
                    sides(h + (PH * part + 1))
                    numbers(h + PH * part, h)
                    best(h + (PH * part + 1))
                numbers(PH * part + PH - 1, PH - 1)
                end_stage(dve, 6 * part + 5)

            with dve.Fori(0, ROUNDS) as q:
                all_of(experts(q + ROUNDS * (PARTS - 1), q * STEPS))
            end_stage(dve, 6 * PARTS)
            norm2(PARTS - 1)

        @block.gpsimd
        def _(pool):
            tt, ts = pool.tensor_tensor, pool.tensor_scalar
            def gather(R, first, p):
                K = R * STEPS + p
                if not (isinstance(R, int) and R == 0):
                    pool.wait_ge(sem["accv"], (R - 1) * STEPS + (p + 1))
                    pool.wait_ge(sem["accp"], (R - 1) * STEPS + (p + 1))
                    apart(pool)
                pool.tensor_copy(IDX[p].unsqueeze(2), EIDX[:, :, bass.ds(first + p, 1)]).then_inc(sem["gidx"], 1)
                pool.wait_ge(sem["gidx"], K + 1)
                apart(pool)
                for b in range(NB):
                    pool.indirect_dma_start(ROW[NB * p + b], None, a["uv"], bass.IndirectOffsetOnAxis(
                        ap=IDX[p][:, b:b + 1], axis=0)).then_inc(got[NB * p + b], 16)

            def first_round(c):
                pool.wait_ge(stage_done, 4 * (6 * c + 5) + 4)
                for p in range(STEPS):
                    gather(ROUNDS * c, 0, p)

            def experts(R, first, p, more=True):
                K = R * STEPS + p
                pool.wait_ge(sem["g_v"], K + 1)
                pool.wait_ge(sem["accp"], K)
                tt(ACC[:, 1, :], ACC[:, 1, :], ROW[NB * p + 1][:, D:2 * D], ALU.add).then_inc(sem["accp"], 1)
                if more:
                    gather(R + 1, first + STEPS, p)

            halves = lambda x: x.rearrange("p (n z t) -> p n z t", z=2, t=CHUNK)
            pool.wait_ge(sem["m_dve"], 2)
            ts(mk, mf, -1.0, 1.0, ALU.mult, ALU.add).then_inc(sem["m_pool"], 1)
            pool.wait_ge(sem["m_pool"], 1)
            pool.wait_ge(sem["m_dve"], 4)
            tt(mks, mk, mest, ALU.mult).then_inc(sem["m_pool"], 1)
            for part in range(PARTS):
                if part:
                    first_round(part - 1)
                def keys(g):
                    pool.wait_ge(sem["f"], g * 2 + 2)
                    pool.wait_ge(sem["ks16"], g)
                    pool.wait_ge(sem["ki"], g)
                    apart(pool)
                    ts(k, f, -1.0, 1.0, ALU.mult, ALU.add).then_inc(sem["k"], 1)
                    pool.wait_ge(sem["k"], g + 1)
                    pool.wait_ge(sem["est"], g + 1)
                    pool.wait_ge(sem["M2"], g)
                    tt(ks16, k, est, ALU.mult).then_inc(sem["ks16"], 1)
                    pool.wait_ge(sem["eb"], g + 1)
                    pool.wait_ge(sem["ks16"], g + 1)
                    pool.wait_ge(sem["T"], g)
                    tt(halves(ks32)[:, :, 0, :], halves(ks16)[:, :, 0, :],
                       ends[:, :, 1, :].to_broadcast([P, NPAIR, CHUNK]), ALU.mult).then_inc(sem["ks32a"], 1)
                    pool.tensor_copy(halves(ks32)[:, :, 1, :], halves(ks16)[:, :, 1, :]).then_inc(sem["ks32"], 1)
                    pool.wait_ge(sem["ebi"], g + 1)
                    pool.wait_ge(sem["M1"], g)
                    tt(ki, k, ebi, ALU.mult).then_inc(sem["ki"], 1)

                def queries(g):
                    pool.wait_ge(sem["eb"], g + 1)
                    pool.wait_ge(sem["st"], g * NPAIR)
                    tt(Dp.unsqueeze(2), ends[:, :, 0, :], ends[:, :, 1, :], ALU.mult).then_inc(sem["D"], 1)
                    pool.wait_ge(sem["qd16"], g + 1)
                    pool.wait_ge(sem["inter"], g * NPAIR)
                    tt(halves(qd32)[:, :, 1, :], halves(qd16)[:, :, 1, :],
                       ends[:, :, 0, :].to_broadcast([P, NPAIR, CHUNK]), ALU.mult).then_inc(sem["qd32a"], 1)
                    pool.tensor_copy(halves(qd32)[:, :, 0, :], halves(qd16)[:, :, 0, :]).then_inc(sem["qd32"], 1)

                def round_and_next(h, following):
                    for p in range(STEPS):
                        if part:
                            experts(h + ROUNDS * (part - 1), h * STEPS, p)
                        if following and p == 1:
                            keys(h + (HG * part + 1))
                        if following and p == 2:
                            queries(h + (HG * part + 1))

                ends = halves(eb)[:, :, :, CHUNK - 1:CHUNK]
                keys(HG * part)
                queries(HG * part)
                with pool.Fori(0, HG - 1) as h:
                    round_and_next(h, True)
                round_and_next(HG - 1, False)
                if part:
                    for j in range(2 * STEPS):
                        experts(ROUNDS * (part - 1) + R_LATENT + j // STEPS, (R_LATENT + j // STEPS) * STEPS, j % STEPS)
                with pool.Fori(0, 8) as u:
                    def step(j):
                        if part:
                            experts(u * 2 + (ROUNDS * (part - 1) + R_ATTEND + j // STEPS),
                                    u * (2 * STEPS) + (R_ATTEND + j // STEPS) * STEPS, j % STEPS)

                    for j in range(STEPS - 1):
                        step(j)
                    for i in range(2 * NB):
                        nk = keys_of(part, i % NB)
                        pool.wait_ge(sem["rcp"], (u + 8 * part) * 2 * NB + (i + 1))
                        apart(pool)
                        ts(PR[i % 2][:, 0:nk], PR[i % 2][:, 0:nk], smx[:, 6 + i % 2:7 + i % 2], 1.0, ALU.mult,
                           ALU.mult).then_inc(sem["pn"], 1)
                        step(STEPS - 1 + i)
                    step(2 * STEPS - 1)
                if part:
                    with pool.Fori(0, MIX_ROUNDS) as n:
                        for p in range(STEPS):
                            experts(n + (ROUNDS * (part - 1) + R_MIX), n * STEPS + R_MIX * STEPS, p)
                if part:
                    for j in range(R_NORM, ROUNDS):
                        for p in range(STEPS):
                            experts(ROUNDS * (part - 1) + j, j * STEPS, p, more=j < ROUNDS - 1)
                with pool.Fori(0, PH) as h:
                    H = h + PH * part
                    oh = OH.rearrange("p (b j z r) -> p b j z r", b=NB, j=TOP, z=2)
                    oh2 = OH2.rearrange("p (b j z r) -> p b j z r", b=NB, j=TOP, z=2)
                    pool.wait_ge(sem["dvc"], H * DVC + 4)
                    pool.wait_ge(sem["t2nd"], H * 2 + 2)
                    for b in range(NB):
                        tt(oh2[:, b], oh[:, b], tif[:, b].unsqueeze(1).to_broadcast([P, TOP, 2, TOP]), ALU.mult
                           ).then_inc(sem["onehot"], 1)
            first_round(PARTS - 1)
            with pool.Fori(0, ROUNDS - 1) as q:
                for p in range(STEPS):
                    experts(q + ROUNDS * (PARTS - 1), q * STEPS, p)
            for p in range(STEPS):
                experts(ROUNDS * PARTS - 1, NSEL - STEPS, p, more=False)


def program(nc, a, out):
    build_program(nc, {**a, "out": out})


def kernel(**inputs):
    import concourse.bacc as bacc
    from concourse.bass_utils import run_bass_kernel_spmd

    x, w_in = inputs["x"][0], inputs["w_in"][0]
    w = {k: inputs[k][0] for k in ("w_uq", "w_ukv", "w_proj_hgrn", "w_proj_mla", "w_out", "peer_query",
                                   "peer_sub_keys", "peer_u", "peer_v")}

    def tiles(m):
        return m.reshape(-1, P, m.shape[1]).transpose(1, 0, 2)

    consts, cross = constants()
    q, f, i, g = (w_in[:, D * n:D * n + D] for n in range(4))
    whg = np.stack([tiles(m).reshape(P, KD, HG, P) for m in (f, g, q, i)])
    o = 4 * D
    cq, ckv, kr = w_in[:, o:o + 384], w_in[:, o + 384:o + 640], w_in[:, o + 640:o + 704]
    ga, gb = w_in[:, o + 704:o + 704 + D], w_in[:, o + 704 + D:]
    swap = np.concatenate([kr[:, 32:], kr[:, :32]], 1)
    wc = np.concatenate([cq, ckv, kr, kr, swap, swap], 1)
    uq = w["w_uq"].reshape(384, 8, 2, 192)
    ra, rb = uq[..., 128:], np.concatenate([uq[..., 160:], uq[..., 128:160]], -1)
    wuq = np.stack([uq[:, :, 0, :128], uq[:, :, 1, :128], ra.reshape(384, 8, 128), rb.reshape(384, 8, 128)], 2)
    ukv = w["w_ukv"].reshape(256, 8, 2, 2, 128).transpose(0, 1, 3, 2, 4).reshape(256, 8, 4, 128)
    mix = np.concatenate([tiles(m) for m in (w["w_proj_hgrn"], w["w_proj_mla"], ga, gb)], 1)
    feat = lambda v: v.reshape(-1, P).T
    pvec = np.concatenate([feat(inputs["hgrn_lb_logits"][0]), feat(inputs["hgrn_lb_logits"][1]),
                           feat(inputs["hgrn_norm_gain"][0]), feat(inputs["q_norm_gain"][0]),
                           feat(inputs["kv_norm_gain"][0])], 1)
    rows = lambda *v: np.stack([np.broadcast_to(z[0], (P, D)) for z in v], 1)
    arrays = {
        "consts": consts, "cross": cross, "pvec": pvec,
        "xm": tiles(inputs["meta_tokens"].T),
        "xt": x.T.reshape(KD, P, PARTS, TOK).transpose(2, 1, 0, 3),
        "xk": x.reshape(PARTS, NB, P, D).transpose(0, 2, 1, 3),
        "whg": whg.transpose(3, 0, 1, 2, 4),
        "wc": tiles(wc).reshape(P, KD, 7, P),
        "wuq": wuq.reshape(QT, P, 8, 4, 128).transpose(2, 1, 0, 3, 4),
        "wukv": ukv.reshape(KVT, P, 8, 4, 128).transpose(2, 1, 0, 3, 4),
        "wmix": mix.reshape(P, 40, KD, P).transpose(2, 0, 1, 3),
        "wout": tiles(w["w_out"]).reshape(P, KD, 2, D // 2).transpose(2, 0, 1, 3),
        "ln1": rows(inputs["ln1_gain"], inputs["ln1_bias"]),
        "ln2": rows(inputs["ln2_gain"], inputs["ln2_bias"]),
        "wpq": tiles(w["peer_query"]).reshape(P, KD, PH, 2, P).transpose(2, 3, 0, 1, 4),
        "wsk": w["peer_sub_keys"].transpose(0, 3, 1, 2),
        "uv": np.concatenate([w["peer_u"], w["peer_v"]], 1),
    }
    nc = bacc.Bacc("TRN2", target_bir_lowering=False, num_devices=1)
    arrays = {"in_" + k: np.ascontiguousarray(v) for k, v in arrays.items()}
    a = {k[3:]: nc.dram_tensor(k, v.shape, mybir.dt.from_np(v.dtype), kind="ExternalInput").ap()
         for k, v in arrays.items()}
    out = nc.dram_tensor("out_0", (PARTS, P, NB, D), F32, kind="ExternalOutput").ap()
    program(nc, a, out)
    r = run_bass_kernel_spmd(nc, [arrays], core_ids=[0])
    return r.results[0]["out_0"].transpose(0, 2, 1, 3).reshape(1, SEQ, D)
```
